# Optimizing a Trainium2 kernel written in Bass

```python
import math
import jax, jax.numpy as jnp
from jax import lax
import numpy as np

D_MODEL = 1024
BATCH = 1
SEQ = 512
DEPTH = 2

HEAD_DIM = 64
MLA_HEADS = 8
MLA_NOPE = 64
MLA_ROPE = 32
MLA_V = 64
MLA_Q_LORA = 384
MLA_KV_LORA = 256
ROPE_THETA = 10000.0
SWA_HEADS = 8
SWA_KV_HEADS = 2
SWA_WINDOW = 128
REL_BUCKETS = 32
REL_MAX_DIST = 128
FOX_HEADS = 16
D_FF = 4 * D_MODEL
D_PLE = 256
BLOCK_Q = 128
DN_ALPHA = (2 * DEPTH) ** 0.25
DN_BETA = (8 * DEPTH) ** -0.25
NORM_EPS = 1e-5
NEG_INF = -1e30
N_EVEN = (DEPTH + 1) // 2
N_ODD = DEPTH // 2
EVEN_SPLIT = (MLA_Q_LORA, MLA_KV_LORA, MLA_ROPE, SWA_HEADS * HEAD_DIM,
              SWA_KV_HEADS * HEAD_DIM, SWA_KV_HEADS * HEAD_DIM)
EVEN_IN = MLA_Q_LORA + MLA_KV_LORA + MLA_ROPE + (SWA_HEADS + 2 * SWA_KV_HEADS) * HEAD_DIM
EVEN_MIX = MLA_HEADS * MLA_V + SWA_HEADS * HEAD_DIM
ODD_SPLIT = (FOX_HEADS * HEAD_DIM, FOX_HEADS * HEAD_DIM, FOX_HEADS * HEAD_DIM, FOX_HEADS)
ODD_IN = 3 * FOX_HEADS * HEAD_DIM + FOX_HEADS
ODD_MIX = FOX_HEADS * HEAD_DIM


def _split(h, sizes):
    out, o = [], 0
    for n in sizes:
        out.append(h[..., o:o + n])
        o += n
    return out

def _layer_norm(x, g, b):
    xf = x.astype(jnp.float32)
    mu = jnp.mean(xf, -1, keepdims=True)
    var = jnp.mean(jnp.square(xf - mu), -1, keepdims=True)
    y = (xf - mu) * lax.rsqrt(var + NORM_EPS)
    return (y * g.astype(jnp.float32) + b.astype(jnp.float32)).astype(x.dtype)

def _rms_norm(x, g):
    xf = x.astype(jnp.float32)
    y = xf * lax.rsqrt(jnp.mean(jnp.square(xf), -1, keepdims=True) + NORM_EPS)
    return (y * g.astype(jnp.float32)).astype(x.dtype)

def _rope_tables(seq_len, dim):
    inv = 1.0 / (ROPE_THETA ** (jnp.arange(0, dim, 2, dtype=jnp.float32) / dim))
    ang = jnp.arange(seq_len, dtype=jnp.float32)[:, None] * inv[None, :]
    return jnp.cos(ang), jnp.sin(ang)

def _apply_rope(x, cos, sin):
    x1, x2 = jnp.split(x.astype(jnp.float32), 2, axis=-1)
    c = cos[:, None, :]
    s = sin[:, None, :]
    return jnp.concatenate([x1 * c - x2 * s, x2 * c + x1 * s], -1).astype(x.dtype)

def _t5_bucket(dist):
    exact = REL_BUCKETS // 2
    d = jnp.maximum(dist, 1).astype(jnp.float32)
    large = exact + (jnp.log(d / exact) / math.log(REL_MAX_DIST / exact)
                     * (REL_BUCKETS - exact)).astype(jnp.int32)
    large = jnp.minimum(large, REL_BUCKETS - 1)
    return jnp.where(dist < exact, dist, large)

def _mla_attend(q_nope, q_rope, k_nope, k_rope, v):
    B, S, H, _ = q_nope.shape
    nb = S // BLOCK_Q
    scale = (MLA_NOPE + MLA_ROPE) ** -0.5
    qn = q_nope.reshape(B, nb, BLOCK_Q, H, MLA_NOPE).transpose(1, 0, 2, 3, 4)
    qr = q_rope.reshape(B, nb, BLOCK_Q, H, MLA_ROPE).transpose(1, 0, 2, 3, 4)
    kpos = jnp.arange(S)

    def block(args):
        i, qn_b, qr_b = args
        s = (jnp.einsum('bqhd,bkhd->bhqk', qn_b, k_nope, preferred_element_type=jnp.float32)
             + jnp.einsum('bqhd,bkd->bhqk', qr_b, k_rope, preferred_element_type=jnp.float32)) * scale
        qpos = i * BLOCK_Q + jnp.arange(BLOCK_Q)
        s = jnp.where(kpos[None, :] <= qpos[:, None], s, NEG_INF)
        w = jax.nn.softmax(s, axis=-1).astype(v.dtype)
        return jnp.einsum('bhqk,bkhd->bqhd', w, v)

    out = lax.map(block, (jnp.arange(nb), qn, qr))
    return out.transpose(1, 0, 2, 3, 4).reshape(B, S, H * MLA_V)

def _swa_attend(q, k, v, sinks, rel_bias):
    B, S, H, d = q.shape
    KVH = k.shape[2]
    G = H // KVH
    nb = S // BLOCK_Q
    qb = q.reshape(B, nb, BLOCK_Q, KVH, G, d)

    def band(t):
        tb = t.reshape(B, nb, BLOCK_Q, KVH, d)
        prev = jnp.pad(tb, ((0, 0), (1, 0), (0, 0), (0, 0), (0, 0)))[:, :-1]
        return jnp.concatenate([prev, tb], axis=2)

    kb, vb = band(k), band(v)
    s = jnp.einsum('bnqkgd,bnskd->bnkgqs', qb, kb, preferred_element_type=jnp.float32) * (d ** -0.5)
    a = jnp.arange(BLOCK_Q)[:, None]
    col = jnp.arange(2 * BLOCK_Q)[None, :]
    dist = a + BLOCK_Q - col
    in_win = (dist >= 0) & (dist < SWA_WINDOW)
    pad = (jnp.arange(nb)[:, None, None] == 0) & (col < BLOCK_Q)[None]
    valid = in_win[None] & ~pad
    bias = rel_bias[_t5_bucket(jnp.maximum(dist, 0))].astype(jnp.float32)
    bias = bias.transpose(2, 0, 1).reshape(KVH, G, BLOCK_Q, 2 * BLOCK_Q)
    s = jnp.where(valid[None, :, None, None], s + bias, NEG_INF)
    sink = jnp.broadcast_to(sinks.astype(jnp.float32).reshape(1, 1, KVH, G, 1, 1), s.shape[:-1] + (1,))
    w = jax.nn.softmax(jnp.concatenate([s, sink], axis=-1), axis=-1)[..., :-1].astype(v.dtype)
    out = jnp.einsum('bnkgqs,bnskd->bnqkgd', w, vb)
    return out.reshape(B, S, H * d)

def _fox_attend(q, k, v, log_f):
    B, S, H, d = q.shape
    nb = S // BLOCK_Q
    c = jnp.cumsum(log_f, axis=1)
    cq = c.reshape(B, nb, BLOCK_Q, H).transpose(1, 0, 3, 2)
    ck = c.transpose(0, 2, 1)
    qb = q.reshape(B, nb, BLOCK_Q, H, d).transpose(1, 0, 2, 3, 4)
    kpos = jnp.arange(S)

    def block(args):
        i, q_b, cq_b = args
        s = jnp.einsum('bqhd,bkhd->bhqk', q_b, k, preferred_element_type=jnp.float32) * (d ** -0.5)
        s = s + cq_b[..., :, None] - ck[:, :, None, :]
        qpos = i * BLOCK_Q + jnp.arange(BLOCK_Q)
        s = jnp.where(kpos[None, :] <= qpos[:, None], s, NEG_INF)
        w = jax.nn.softmax(s, axis=-1).astype(v.dtype)
        return jnp.einsum('bhqk,bkhd->bqhd', w, v)

    out = lax.map(block, (jnp.arange(nb), qb, cq))
    return out.transpose(1, 0, 2, 3, 4).reshape(B, S, H * d)

def _even_mixer(x, w_in, q_norm, w_uq, kv_norm, w_ukv, sinks, w_out, rel_bias, cos, sin):
    B, S, _ = x.shape
    h = x @ w_in
    c_q, c_kv, k_rope, q_s, k_s, v_s = _split(h, EVEN_SPLIT)
    q = (_rms_norm(c_q, q_norm) @ w_uq).reshape(B, S, MLA_HEADS, MLA_NOPE + MLA_ROPE)
    q_nope = q[..., :MLA_NOPE]
    q_rope = _apply_rope(q[..., MLA_NOPE:], cos, sin)
    kv = (_rms_norm(c_kv, kv_norm) @ w_ukv).reshape(B, S, MLA_HEADS, MLA_NOPE + MLA_V)
    k_nope, v = kv[..., :MLA_NOPE], kv[..., MLA_NOPE:]
    k_rope = _apply_rope(k_rope[:, :, None, :], cos, sin)[:, :, 0]
    o_mla = _mla_attend(q_nope, q_rope, k_nope, k_rope, v)
    o_swa = _swa_attend(q_s.reshape(B, S, SWA_HEADS, HEAD_DIM),
                        k_s.reshape(B, S, SWA_KV_HEADS, HEAD_DIM),
                        v_s.reshape(B, S, SWA_KV_HEADS, HEAD_DIM), sinks, rel_bias)
    return jnp.concatenate([o_mla, o_swa], axis=-1) @ w_out

def _odd_mixer(x, w_in, b_f, w_out):
    B, S, _ = x.shape
    q, k, v, f = _split(x @ w_in, ODD_SPLIT)
    log_f = jax.nn.log_sigmoid((f + b_f).astype(jnp.float32))
    o = _fox_attend(q.reshape(B, S, FOX_HEADS, HEAD_DIM), k.reshape(B, S, FOX_HEADS, HEAD_DIM),
                    v.reshape(B, S, FOX_HEADS, HEAD_DIM), log_f)
    return o @ w_out

def _sq_relu_mlp(x, w_up, w_down):
    return jnp.square(jax.nn.relu(x @ w_up)) @ w_down

def first_inputs(seed: int = 0) -> dict:
    key = jax.random.key(seed)
    ks = jax.random.split(key, 24)
    nrm = jax.random.normal
    f32 = jnp.float32
    return {
        "x": nrm(ks[0], (BATCH, SEQ, D_MODEL), f32),
        "p": nrm(ks[1], (DEPTH, BATCH, SEQ, D_PLE), f32),
        "rel_bias": 0.5 * nrm(ks[2], (REL_BUCKETS, SWA_HEADS), f32),
        "ev_w_in": nrm(ks[3], (N_EVEN, D_MODEL, EVEN_IN), f32) * D_MODEL ** -0.5,
        "ev_q_norm": 1.0 + 0.02 * nrm(ks[4], (N_EVEN, MLA_Q_LORA), f32),
        "ev_w_uq": nrm(ks[5], (N_EVEN, MLA_Q_LORA, MLA_HEADS * (MLA_NOPE + MLA_ROPE)), f32) * MLA_Q_LORA ** -0.5,
        "ev_kv_norm": 1.0 + 0.02 * nrm(ks[6], (N_EVEN, MLA_KV_LORA), f32),
        "ev_w_ukv": nrm(ks[7], (N_EVEN, MLA_KV_LORA, MLA_HEADS * (MLA_NOPE + MLA_V)), f32) * MLA_KV_LORA ** -0.5,
        "ev_sinks": 0.5 * nrm(ks[8], (N_EVEN, SWA_HEADS), f32),
        "ev_w_out": nrm(ks[9], (N_EVEN, EVEN_MIX, D_MODEL), f32) * (EVEN_MIX ** -0.5 * DN_BETA),
        "od_w_in": nrm(ks[10], (N_ODD, D_MODEL, ODD_IN), f32) * D_MODEL ** -0.5,
        "od_b_f": jax.random.uniform(ks[11], (N_ODD, FOX_HEADS), f32, 1.0, 4.0),
        "od_w_out": nrm(ks[12], (N_ODD, ODD_MIX, D_MODEL), f32) * (ODD_MIX ** -0.5 * DN_BETA),
        "ln1_g": 1.0 + 0.02 * nrm(ks[13], (DEPTH, D_MODEL), f32),
        "ln1_b": 0.02 * nrm(ks[14], (DEPTH, D_MODEL), f32),
        "w_up": nrm(ks[15], (DEPTH, D_MODEL, D_FF), f32) * D_MODEL ** -0.5,
        "w_down": nrm(ks[16], (DEPTH, D_FF, D_MODEL), f32) * (D_FF ** -0.5 * DN_BETA),
        "ln2_g": 1.0 + 0.02 * nrm(ks[17], (DEPTH, D_MODEL), f32),
        "ln2_b": 0.02 * nrm(ks[18], (DEPTH, D_MODEL), f32),
        "ple_w_proj": nrm(ks[19], (DEPTH, D_PLE, D_MODEL), f32) * D_PLE ** -0.5,
        "ple_w_gate": nrm(ks[20], (DEPTH, D_MODEL, D_MODEL), f32) * D_MODEL ** -0.5,
        "ple_b_gate": 0.02 * nrm(ks[21], (DEPTH, D_MODEL), f32),
    }

def first_block(x, p, rel_bias, ev_w_in, ev_q_norm, ev_w_uq, ev_kv_norm, ev_w_ukv, ev_sinks, ev_w_out,
              od_w_in, od_b_f, od_w_out, ln1_g, ln1_b, w_up, w_down, ln2_g, ln2_b,
              ple_w_proj, ple_w_gate, ple_b_gate):
    S = x.shape[1]
    cos, sin = _rope_tables(S, MLA_ROPE)
    for i in range(DEPTH):
        j = i // 2
        if i % 2 == 0:
            m = _even_mixer(x, ev_w_in[j], ev_q_norm[j], ev_w_uq[j], ev_kv_norm[j], ev_w_ukv[j],
                            ev_sinks[j], ev_w_out[j], rel_bias, cos, sin)
        else:
            m = _odd_mixer(x, od_w_in[j], od_b_f[j], od_w_out[j])
        x = _layer_norm(DN_ALPHA * x + m, ln1_g[i], ln1_b[i])
        x = _layer_norm(DN_ALPHA * x + _sq_relu_mlp(x, w_up[i], w_down[i]), ln2_g[i], ln2_b[i])
        gate = jax.nn.sigmoid(x @ ple_w_gate[i] + ple_b_gate[i])
        x = x + gate * (p[i] @ ple_w_proj[i])
    return x


DEPTH_2 = 1

CHUNK = 64
HEAD_SIZE = 64
D_RWKV = D_MODEL
N_RWKV_HEADS = D_RWKV // HEAD_SIZE
D_CONV = D_MODEL
CONV_WIDTH = 31
D_DECAY_LORA = 64
D_AAA_LORA = 64
D_GATE_LORA = 128
D_FF_2 = 4 * D_MODEL
N_BRANCHES = 2
RMS_EPS = 1e-6
LN_EPS = 1e-5
GN_EPS = 64e-5
DECAY_OFFSET = 0.5
COL_RKV = 3 * D_RWKV
COL_GLU = 2 * D_CONV
COL_GATE = N_BRANCHES * D_MODEL
IN_COLS = COL_RKV + COL_GLU + COL_GATE


def _rmsnorm(x, g):
    xf = x.astype(jnp.float32)
    y = xf * lax.rsqrt(jnp.mean(xf * xf, axis=-1, keepdims=True) + RMS_EPS)
    return (y * g.astype(jnp.float32)).astype(x.dtype)

def _layernorm(x, g, b):
    xf = x.astype(jnp.float32)
    mu = jnp.mean(xf, axis=-1, keepdims=True)
    var = jnp.mean(jnp.square(xf - mu), axis=-1, keepdims=True)
    y = (xf - mu) * lax.rsqrt(var + LN_EPS)
    return (y * g.astype(jnp.float32) + b.astype(jnp.float32)).astype(x.dtype)

def _token_shift(z):
    return jnp.pad(z, ((0, 0), (1, 0), (0, 0)))[:, :-1]

def _heads(z):
    b, t, _ = z.shape
    return z.reshape(b, t, N_RWKV_HEADS, HEAD_SIZE)

def _wkv7_scan(r, w, k, v, kk, a):
    b, t, h, n = r.shape
    n_chunks = t // CHUNK

    def to_chunks(z):
        return jnp.moveaxis(z.astype(jnp.float32).reshape(b, n_chunks, CHUNK, h, n), (1, 2), (0, 1))

    def frame_step(S, inp):
        r_t, w_t, k_t, v_t, kk_t, a_t = inp
        sa = jnp.einsum('bhvk,bhk->bhv', S, -kk_t)
        S = (S * w_t[:, :, None, :]
             + sa[..., None] * (kk_t * a_t)[:, :, None, :]
             + v_t[..., None] * k_t[:, :, None, :])
        o_t = jnp.einsum('bhvk,bhk->bhv', S, r_t)
        return S, o_t

    def chunk_step(S, chunk_inp):
        return lax.scan(frame_step, S, chunk_inp)

    S0 = jnp.zeros((b, h, n, n), jnp.float32)
    inputs = (to_chunks(r), to_chunks(w), to_chunks(k), to_chunks(v), to_chunks(kk), to_chunks(a))
    _, o = lax.scan(chunk_step, S0, inputs)
    return jnp.moveaxis(o, (0, 1), (1, 2)).reshape(b, t, h, n)

def _rwkv7_mixer(h, r, k, v, mu_lora, w0, w1, w2, a0, a1, a2, g1, g2, k_k, k_a, r_k, ln_g, ln_b):
    dh = _token_shift(h) - h
    xw = h + dh * mu_lora[0]
    xa = h + dh * mu_lora[1]
    xg = h + dh * mu_lora[2]
    w_log = -jax.nn.softplus(-(w0 + jnp.tanh(xw @ w1) @ w2)) - DECAY_OFFSET
    decay = jnp.exp(-jnp.exp(w_log.astype(jnp.float32)))
    a = jax.nn.sigmoid(a0 + (xa @ a1) @ a2)
    g = jax.nn.sigmoid(xg @ g1) @ g2
    kk = _heads(k * k_k).astype(jnp.float32)
    kk = kk / jnp.maximum(jnp.linalg.norm(kk, axis=-1, keepdims=True), 1e-12)
    k = k * (1.0 + (a - 1.0) * k_a)
    rh, kh, vh, ah = _heads(r), _heads(k), _heads(v), _heads(a)
    o = _wkv7_scan(rh, _heads(decay), kh, vh, kk, ah)
    mu = jnp.mean(o, axis=-1, keepdims=True)
    var = jnp.mean(jnp.square(o - mu), axis=-1, keepdims=True)
    o = ((o - mu) * lax.rsqrt(var + GN_EPS)).reshape(h.shape[0], h.shape[1], D_RWKV)
    o = (o * ln_g.astype(jnp.float32) + ln_b.astype(jnp.float32)).astype(h.dtype)
    bonus = jnp.sum(rh * kh * r_k, axis=-1, keepdims=True) * vh
    o = o + bonus.reshape(o.shape)
    return o * g

def _conformer_conv_mixer(glu_in, conv_w, conv_b, ln_g, ln_b):
    u = glu_in[..., :D_CONV] * jax.nn.sigmoid(glu_in[..., D_CONV:])
    u = lax.conv_general_dilated(
        u, conv_w[:, None, :], window_strides=(1,), padding=((CONV_WIDTH - 1, 0),),
        dimension_numbers=('NWC', 'WIO', 'NWC'), feature_group_count=D_CONV) + conv_b
    u = _layernorm(u, ln_g, ln_b)
    return jax.nn.silu(u)

def second_inputs(seed: int = 0) -> dict:
    key = jax.random.key(seed)
    ks = iter(jax.random.split(key, 40))
    L = DEPTH_2
    f32 = jnp.float32

    def nrm(shape, scale):
        return jax.random.normal(next(ks), shape, f32) * scale

    def unif(shape, lo, hi):
        return jax.random.uniform(next(ks), shape, f32, minval=lo, maxval=hi)

    return {
        "x": nrm((BATCH, SEQ, D_MODEL), 1.0),
        "norm_mix_g": 1.0 + nrm((L, D_MODEL), 0.05),
        "w_in": nrm((L, D_MODEL, IN_COLS), D_MODEL ** -0.5),
        "b_gate": nrm((L, COL_GATE), 0.1),
        "mu_rkv": unif((L, COL_RKV), 0.0, 1.0),
        "mu_lora": unif((L, 3, D_MODEL), 0.0, 1.0),
        "decay_w0": unif((L, D_RWKV), -3.0, 2.0),
        "decay_w1": nrm((L, D_MODEL, D_DECAY_LORA), D_MODEL ** -0.5),
        "decay_w2": nrm((L, D_DECAY_LORA, D_RWKV), 0.1),
        "aaa_a0": nrm((L, D_RWKV), 0.1),
        "aaa_a1": nrm((L, D_MODEL, D_AAA_LORA), D_MODEL ** -0.5),
        "aaa_a2": nrm((L, D_AAA_LORA, D_RWKV), 0.5 * D_AAA_LORA ** -0.5),
        "gate_g1": nrm((L, D_MODEL, D_GATE_LORA), D_MODEL ** -0.5),
        "gate_g2": nrm((L, D_GATE_LORA, D_RWKV), D_GATE_LORA ** -0.5),
        "k_k": 0.85 + nrm((L, D_RWKV), 0.05),
        "k_a": 1.0 + nrm((L, D_RWKV), 0.05),
        "r_k": nrm((L, N_RWKV_HEADS, HEAD_SIZE), 0.1),
        "ln_x_g": 1.0 + nrm((L, D_RWKV), 0.05),
        "ln_x_b": nrm((L, D_RWKV), 0.02),
        "w_rwkv_proj": nrm((L, D_RWKV, D_MODEL), D_RWKV ** -0.5),
        "conv_w": nrm((L, CONV_WIDTH, D_CONV), CONV_WIDTH ** -0.5),
        "conv_b": nrm((L, D_CONV), 0.02),
        "conv_ln_g": 1.0 + nrm((L, D_CONV), 0.05),
        "conv_ln_b": nrm((L, D_CONV), 0.02),
        "w_conv_proj": nrm((L, D_CONV, D_MODEL), D_CONV ** -0.5),
        "w_out": nrm((L, D_MODEL, D_MODEL), D_MODEL ** -0.5),
        "norm_ff_g": 1.0 + nrm((L, D_MODEL), 0.05),
        "w_ff1": nrm((L, D_MODEL, D_FF_2), D_MODEL ** -0.5),
        "w_ff2": nrm((L, D_FF_2, D_MODEL), 0.5 * D_FF_2 ** -0.5),
        "norm_final_g": 1.0 + nrm((D_MODEL,), 0.05),
    }

def second_block(x, norm_mix_g, w_in, b_gate, mu_rkv, mu_lora, decay_w0, decay_w1, decay_w2,
              aaa_a0, aaa_a1, aaa_a2, gate_g1, gate_g2, k_k, k_a, r_k, ln_x_g, ln_x_b,
              w_rwkv_proj, conv_w, conv_b, conv_ln_g, conv_ln_b, w_conv_proj, w_out,
              norm_ff_g, w_ff1, w_ff2, norm_final_g):
    b, t, _ = x.shape
    for l in range(DEPTH_2):
        h = _rmsnorm(x, norm_mix_g[l])
        proj = h @ w_in[l]
        rkv = proj[..., :COL_RKV]
        glu_in = proj[..., COL_RKV:COL_RKV + COL_GLU]
        gate_logits = proj[..., COL_RKV + COL_GLU:] + b_gate[l]
        rkv = rkv + (_token_shift(rkv) - rkv) * mu_rkv[l]
        r = rkv[..., :D_RWKV]
        k = rkv[..., D_RWKV:2 * D_RWKV]
        v = rkv[..., 2 * D_RWKV:]
        a_out = _rwkv7_mixer(h, r, k, v, mu_lora[l], decay_w0[l], decay_w1[l], decay_w2[l],
                             aaa_a0[l], aaa_a1[l], aaa_a2[l], gate_g1[l], gate_g2[l],
                             k_k[l], k_a[l], r_k[l], ln_x_g[l], ln_x_b[l])
        c_out = _conformer_conv_mixer(glu_in, conv_w[l], conv_b[l], conv_ln_g[l], conv_ln_b[l])
        gates = jax.nn.sigmoid(gate_logits).reshape(b, t, N_BRANCHES, D_MODEL)
        merged = gates[:, :, 0] * (a_out @ w_rwkv_proj[l]) + gates[:, :, 1] * (c_out @ w_conv_proj[l])
        x = x + merged @ w_out[l]
        h2 = _rmsnorm(x, norm_ff_g[l])
        x = x + jnp.square(jax.nn.relu(h2 @ w_ff1[l])) @ w_ff2[l]
    return _rmsnorm(x, norm_final_g)


def setup_inputs(seed=0):
    out = dict(first_inputs(seed))
    for name, value in second_inputs(seed + 1).items():
        if name != "x":
            out[name + "_2"] = value
    return out


def reference(
    x, p, rel_bias, ev_w_in, ev_q_norm, ev_w_uq, ev_kv_norm, ev_w_ukv, ev_sinks, ev_w_out,
    od_w_in, od_b_f, od_w_out, ln1_g, ln1_b, w_up, w_down, ln2_g, ln2_b, ple_w_proj, ple_w_gate,
    ple_b_gate, norm_mix_g_2, w_in_2, b_gate_2, mu_rkv_2, mu_lora_2, decay_w0_2, decay_w1_2,
    decay_w2_2, aaa_a0_2, aaa_a1_2, aaa_a2_2, gate_g1_2, gate_g2_2, k_k_2, k_a_2, r_k_2,
    ln_x_g_2, ln_x_b_2, w_rwkv_proj_2, conv_w_2, conv_b_2, conv_ln_g_2, conv_ln_b_2,
    w_conv_proj_2, w_out_2, norm_ff_g_2, w_ff1_2, w_ff2_2, norm_final_g_2,
):
    x = first_block(
        x, p, rel_bias, ev_w_in, ev_q_norm, ev_w_uq, ev_kv_norm, ev_w_ukv, ev_sinks, ev_w_out,
        od_w_in, od_b_f, od_w_out, ln1_g, ln1_b, w_up, w_down, ln2_g, ln2_b, ple_w_proj,
        ple_w_gate, ple_b_gate,
    )
    return second_block(
        x, norm_mix_g_2, w_in_2, b_gate_2, mu_rkv_2, mu_lora_2, decay_w0_2, decay_w1_2,
        decay_w2_2, aaa_a0_2, aaa_a1_2, aaa_a2_2, gate_g1_2, gate_g2_2, k_k_2, k_a_2, r_k_2,
        ln_x_g_2, ln_x_b_2, w_rwkv_proj_2, conv_w_2, conv_b_2, conv_ln_g_2, conv_ln_b_2,
        w_conv_proj_2, w_out_2, norm_ff_g_2, w_ff1_2, w_ff2_2, norm_final_g_2,
    )


_drawn_inputs = setup_inputs


def setup_inputs(seed=0):
    import zlib

    import numpy as np

    out = dict(_drawn_inputs(seed))
    spreads = {}
    factors = {'rel_bias': 2.815,
     'ev_q_norm': 8.0,
     'ev_kv_norm': 8.0,
     'ev_sinks': 60.774,
     'ple_b_gate': 8.0,
     'b_gate_2': 3.838,
     'aaa_a0_2': 4.518,
     'k_k_2': 41.613,
     'k_a_2': 4.059,
     'ln_x_g_2': 4.556,
     'ln_x_b_2': 8.0,
     'conv_b_2': 5.172,
     'conv_ln_g_2': 3.585,
     'conv_ln_b_2': 8.0,
     'norm_ff_g_2': 3.524}
    for name, (base, spread) in spreads.items():
        noise = np.random.default_rng([zlib.crc32(name.encode()), seed]).standard_normal(out[name].shape)
        drawn = base * np.exp(spread * noise) if base else spread * noise
        out[name] = __import__('jax').numpy.asarray(drawn.astype(out[name].dtype))
    for name, factor in factors.items():
        out[name] = (out[name] * factor).astype(out[name].dtype)
    return out
```

```python
from contextlib import ExitStack

import numpy as np
import concourse.bass as bass
from concourse import mybir

F32 = mybir.dt.float32
F32R = mybir.dt.float32r
ALU = mybir.AluOpType
ACT = mybir.ActivationFunctionType
AX = mybir.AxisListType.X

P = 128
T = 512
D = 1024
NC = D // P
NB = T // P
SLOTS = 4
ALPHA = 4 ** 0.25
LN_EPS, RMS1_EPS, RMS_EPS, GN_EPS = 1e-5, 1e-5, 1e-6, 64e-5
NEG = -1e30
MLA_SCALE = 96 ** -0.5
HEAD_SCALE = 64 ** -0.5


class Idx:

    def __init__(self, turn, k):
        self.turn, self.k = turn, k

    def __add__(self, n):
        return Idx(self.turn, self.k + n)

    @property
    def v(self):
        return self.turn * 4 + self.k

    def over4(self):
        return self.turn + self.k // 4

    def over2(self):
        return self.turn * 2 + self.k // 2


class Walk:

    def __init__(self):
        self.p = 0
        self.g = 0
        self.mid = 0
        self.od = 0
        self.op = 0
        self.h = 0
        self.norm = 0
        self.nsq = 0
        self.u = 0
        self.ple = 0
        self.nd = 0
        self.mg = 0
        self.mean = 0


def turns(eng, n, body, peel_last=False):
    full = n // 4
    if peel_last and n % 4 == 0:
        full -= 1
    if full >= 2:
        with eng.Fori(0, full) as t:
            for k in range(4):
                body(Idx(t, k))
    else:
        full = 0
    for j in range(4 * full, n):
        body(Idx(0, j))


PAR = {}


def _par(name, n):
    PAR[name] = (sum(x[1] for x in PAR.values()), n)


for _n, _c in (("q_norm", 3), ("kv_norm", 2), ("ln1_g", 16), ("ln1_b", 16), ("ln2_g", 16), ("ln2_b", 16),
               ("ple_b", 16), ("norm_mix", 8), ("b_gate", 16), ("mu_rkv", 24), ("mu_lora", 24), ("w0", 8),
               ("a0", 8), ("k_k", 8), ("k_a", 8), ("r_k", 8), ("lnx_g", 8), ("lnx_b", 8), ("conv_b", 8),
               ("cln_g", 8), ("cln_b", 8), ("norm_ff", 8), ("norm_fin", 8)):
    _par(_n, _c)
NPAR = sum(x[1] for x in PAR.values())
SWA_F = 384
PAIR_LINKS = 23
CHUNK_LINKS = 32


class Chain:

    def __init__(self, eng, sem):
        self.eng, self.sem, self.n, self.turn, self.per = eng, sem, 0, 0, 0

    def link(self, ins):
        self.n += 1
        ins.then_inc(self.sem, 1)
        self.eng.wait_ge(self.sem, self.turn * self.per + self.n)

    def turns(self, n, body, links):
        seen = []

        def counted(j):
            self.turn = j.turn
            self.per = 4 * links if not isinstance(j.turn, int) else 0
            at = self.n
            body(j)
            seen.append(self.n - at)
            assert seen[-1] == links, (seen[-1], links)

        full = n // 4
        turns(self.eng, n, counted)
        if full >= 2:
            self.n += 4 * links * (full - 1)
        self.turn = self.per = 0


def build(nc, A, n_panels, b2_start, upto=None):
    ctx = ExitStack()
    with ctx:
        def sb(name, shape, dt=F32, at=ctx):
            return at.enter_context(nc.sbuf_tensor("sb_" + name, shape, dt))

        def sem(name):
            return ctx.enter_context(nc.semaphore(name))

        raw = sb("raw", [P, SLOTS, D])
        wh = sb("wh", [P, SLOTS, D], F32R)
        wl = sb("wl", [P, SLOTS, D], F32R)
        x = sb("x", [P, NC, T])
        bh = [sb(f"bh{i}", [P, NC, T], F32R) for i in range(2)]
        bl = [sb(f"bl{i}", [P, NC, T], F32R) for i in range(2)]
        par = sb("par", [P, NPAR])
        ident = sb("ident", [P, P])
        ones = sb("ones", [P, P])
        mask = sb("mask", [P, P])
        t2 = sb("t2", [P, 2, T])
        sq = sb("sq", [P, 2, T])
        eps = sb("eps", [P, 4])
        w4 = sb("w4", [P, 4 * T])
        s1, s1c, sd, rs = (w4[:, i * T:(i + 1) * T] for i in range(4))
        psum = ctx.enter_context(nc.psum_tensor("banks", [P, 8, T], F32))

        def pcol(name, c=0):
            o = PAR[name][0]
            if isinstance(c, Idx):
                c = c.v
            return par[:, o + c:o + c + 1] if isinstance(c, int) else par[:, bass.ds(c + o, 1)]

        pcol_at = pcol

        with ExitStack() as part:
            bh.append(sb("bh2", [P, NC, T], F32R, part))
            bl.append(sb("bl2", [P, NC, T], F32R, part))
            pj = sb("pj", [P, NC, T], F32, part)
            praw = pj[:, 6:8, :]
            ph = sb("ph", [P, 2, T], F32R, part)
            pl = sb("pl", [P, 2, T], F32R, part)
        with ExitStack() as part:
            qa = sb("qa", [P, 4, T], F32, part)
            ka = sb("ka", [P, 4, T], F32, part)
            va = sb("va", [P, NB, T], F32, part)
            qs = sb("qs", [P, 2 * T], F32, part)
            ks = sb("ks", [P, 2 * T], F32, part)
            vs = sb("vs", [P, NB, P], F32, part)
            pa = sb("pa", [P, 2, 1280], F32, part)
            lat = pa[:, :, :].rearrange("p a b -> p (a b)").rearrange("p (c t) -> p c t", t=T)
            nm = sb("nm", [P, 2, 4], F32, part)
            sm = sb("sm", [P, 2, 4], F32, part)
            rc = sb("rc", [P, 2, 4], F32, part)
            with ExitStack() as mla:
                lath, latl = bh[0][:, 3:8, :], bl[0][:, 3:8, :]
                rope = sb("rope", [P, T], F32, mla)
                rt = sb("rt", [P, 2, T], F32, mla)
            with ExitStack() as swa:
                bias = sb("bias", [P, 8, 2 * P], F32, swa)
                sink = sb("sink", [P, 8], F32, swa)
                nsink = sb("nsink", [P, 8], F32, swa)
                snk = sb("snk", [P, 3, 4], F32, swa)
                relb = sb("relb", [32, 8], F32, swa)
                oneh = sb("oneh", [32, SWA_F], F32, swa)
                negm = sb("negm", [8, SWA_F], F32, swa)
                brow = sb("brow", [8, SWA_F], F32, swa)
            with ExitStack() as fox:
                fsel = sb("fsel", [P, 19], F32, fox)
                fsc = sb("fsc", [P, 2], F32, fox)
                fc = sb("fc", [P, T], F32, fox)
                ft = lat[:, 0:3, :]
                fone = t2[:, 0, :]
                fq = sb("fq", [P, T], F32, fox)
                fk = sb("fk", [P, T], F32, fox)
        with ExitStack() as part:
            z = [sb(f"z{n}", [P, T + 1], F32, part) for n in "rkv"]
            zr, zk, zv = (a[:, 1:T + 1] for a in z)
            gt = sb("gt", [P, T], F32, part)
            ep = sb("ep", [P, 8, 65], F32, part)
            m_a, m_b, m_k, m_r, m_v, m_bd, m_kd, m_at, m_bt, m_kt, m_vt, m_lt, m_rb, m_ak, m_rk, m_off = (
                sb("m_" + n, [P, 4, P], F32, part) for n in
                "a b k r v bd kd at bt kt vt lt rb ak rk off".split())
            m_t = sb("m_t", [P, 4, P], F32, part)
            m_w, m_ta, m_tw, m_p, m_x, m_z, m_mm, m_n = m_a, m_b, m_k, m_r, m_bd, m_kd, m_v, m_ak
            m_s = sb("m_s", [P, 5, P], F32, part)
            wm = sb("wm", [P, 9, P], F32, part)
            o64 = mask
            half_b = sb("half_b", [P, 16], F32, part)
            going = sb("going", [P, T], F32, part)
            lh = [sb(f"lh{n}", [P, T], F32R, part) for n in "ag"]
            ll = [sb(f"ll{n}", [P, T], F32R, part) for n in "ag"]
        cu, em, rn, kkn = s1, s1c, sd, rs
        la, lw = t2[:, 0, :], t2[:, 1, :]
        with ExitStack() as part:
            mg = sb("mg", [P, NC, T], F32, part)
            with ExitStack() as conv:
                y = sb("y", [P, NC, T], F32, conv)
                ub = sb("ub", [P, T + 30], F32, conv)
                cw = sb("cw", [P, NC, 31], F32, conv)
                sg = sb("sg", [P, NC, T], F32, conv)
            mh = sb("mh", [P, NC, T], F32R, part)
            ml = sb("ml", [P, NC, T], F32R, part)
        bh.append(mh)
        bl.append(ml)
        scratch = nc.dram_tensor("bias_rows", [8, P, SWA_F], F32, kind="Internal")

        panel_in = [sem(f"panel_in{i}") for i in range(SLOTS)]
        hi_ready, lo_ready = sem("hi_ready"), sem("lo_ready")
        panel_done, mid_done = sem("panel_done"), sem("mid_done")
        bank_free = [sem("bank0_free"), sem("bank1_free")]
        opnd_dve, opnd_pool = sem("opnd_dve"), sem("opnd_pool")
        dve_step, act_step, pool_step = sem("dve_step"), sem("act_step"), sem("pool_step")
        par_in, x_in = sem("par_in"), sem("x_in")
        xh0 = sem("x_hi_ready")
        u_free = sem("u_free")
        s1_ready, mu_done, d_ready, sq_ready, sq_used = (sem(n) for n in (
            "s1_ready", "mu_done", "d_ready", "sq_ready", "sq_used"))
        sd_ready, t_ready, nhi_ready = sem("sd_ready"), sem("t_ready"), sem("nhi_ready")
        pp_in, ph_ready, pl_ready, xn_ready, xnh_ready = (sem(n) for n in (
            "pp_in", "ph_ready", "pl_ready", "xn_ready", "xnh_ready"))
        s_ready, nm_ready, exp_done, rc_done, p_ready, pt_ready, pt_copied, o_ready, ohi_done = (sem(n) for n in (
            "s_ready", "nm_ready", "exp_done", "rc_done", "p_ready", "pt_ready", "pt_copied", "o_ready", "ohi_done"))
        qk_staged, v_staged, att_in, lat_sq, lat_ss, lat_sd, lat_t, lat_h, lat_l = (sem(n) for n in (
            "qk_staged", "v_staged", "att_in", "lat_sq", "lat_ss", "lat_sd", "lat_t", "lat_h", "lat_l"))
        snk_ready, snk_done, brow_ps, brow_out, bias_in, fox_f, fox_a, fox_b, fox_c, const_set = (sem(n) for n in (
            "snk_ready", "snk_done", "brow_ps", "brow_out", "bias_in", "fox_f", "fox_a", "fox_b", "fox_c", "const_set"))
        brow_mm, fsel_in = sem("brow_mm"), sem("fsel_in")
        scaled, wk_in, wk_set, lora_h, lora_l, m_done, mrg_h, cw_in, yz, ysg = (sem(n) for n in (
            "scaled", "wk_in", "wk_set", "lora_h", "lora_l", "m_done", "mrg_h", "cw_in", "yz", "ysg"))
        lora_z, lora_t = sem("lora_z"), sem("lora_t")
        pair_pe, pair_act, pair_dve = sem("pair_pe"), sem("pair_act"), sem("pair_dve")
        post_pe, post_act, post_dve = sem("post_pe"), sem("post_act"), sem("post_dve")
        half_pe, half_act, half_dve, half_pool = sem("half_pe"), sem("half_act"), sem("half_dve"), sem("half_pool")
        stored = sem("stored")

        block = ctx.enter_context(nc.Block())
        n_pan = n_panels
        MLP = ("U0", "U1", "D0", "U2", "D1", "U3", "D2", "D3")

        def span(kind, i):
            if kind == "swa":
                return (0, P, 0) if i == 0 else (P + 2 * P * (i - 1), 2 * P, i - 1)
            return P * (i * (i + 1) // 2), P * (i + 1), 0

        def pt_blocks(kind, j):
            return [i for i in range(j, NB) if kind != "swa" or i <= j + 1]

        @block.sync
        def _(sp):
            sp.dma_start(x[:, :, :], A["xT"]).then_inc(x_in, 16)
            for s in range(SLOTS):
                sp.dma_start(raw[:, s, :], A["w"][s]).then_inc(panel_in[s], 16)
                if s == 0:
                    sp.dma_start(par[:, :], A["par"]).then_inc(par_in, 16)
                    sp.dma_start(ident[:, :], A["ident"]).then_inc(par_in, 16)
                    sp.dma_start(mask[:, :], A["mask"]).then_inc(par_in, 16)

            def load(q):
                s = q.k % SLOTS
                sp.wait_ge(lo_ready, (q + -3).v)
                sp.dma_start(raw[:, s, :], A["w"][q.v]).then_inc(panel_in[s], 16)

            turns(sp, n_pan - SLOTS, lambda j: load(j + SLOTS))
            if upto:
                sp.wait_ge(xn_ready, 8 if upto == "l0" else 16)
                sp.dma_start(A["out"], x[:, :, :]).then_inc(stored, 16)
                sp.wait_ge(stored, 16)
            else:
                for c in range(0, NC, 2):
                    sp.wait_ge(t_ready, 7 * NC + c + 2)
                    sp.dma_start(A["out"][:, c:c + 2, :], x[:, c:c + 2, :]).then_inc(stored, 16)
                sp.wait_ge(stored, 16 * (NC // 2))

        def pts_at(kind, j):
            return 2 * P * j if kind == "swa" else (0, 4 * P, 7 * P, 9 * P)[j]

        LEVELS = (2, 4, 8, 16, 32)
        EARLY = ["l", "lt", "rb", "ak", "rk", "at", "bt", "kt", "vt", "z2", "w"]
        INVERSE = [f"{m}{b}" for b in LEVELS for m in "ztx" if m + str(b) not in ("z2", "t32")]
        LATE = ["ta", "tw", "mm", "p", "n"]

        def groups(names):
            return [f"{n}.{g}" for n in names for g in range(2)]
        PRODUCTS = groups(EARLY + INVERSE + LATE)
        EVENTS = {
            pair_pe: ["kk", "bonus"],
            pair_act: ["decay", "square", "root"],
            pair_dve: ["sums", "mixed", "kmax", "prod", "ready"],
            post_pe: ["mean", "var"],
            post_act: ["osquare", "oroot", "high"],
            post_dve: ["centred", "out"],
            half_act: ["v"] + groups(["at", "bt", "kt", "vt", "z2", "w"] + [f"z{b}" for b in LEVELS[1:]] + ["ta", "n"]) + ["o"],
            half_dve: ["a", "b", "k", "r"] + groups(["t1", "lt", "rb", "ak", "rk", "x1"]
                                                    + [f"{m}{b}" for b in LEVELS for m in "tx" if m + str(b) != "t32"]
                                                    + ["tw", "mm", "p"]) + ["s0", "s1", "s2", "s3", "s4"],
            half_pool: ["bd", "kd"] + groups([f"off{b}" for b in LEVELS]),
            half_pe: PRODUCTS + [f"{m}{i}" for i in range(4) for m in "co"],
        }
        BANK = {n: 2 + i % 6 for i, n in enumerate(PRODUCTS)}
        O_BANK = 2 + len(PRODUCTS) % 6
        BANK.update({f"c{i}": 2 + (len(PRODUCTS) + 1 + i) % 6 for i in range(4)})

        def bank(product):
            return psum[:, BANK[product], 0:2 * P].rearrange("p (a n) -> p a n", a=2)
        o_bank = psum[:, O_BANK, :].rearrange("p (a n) -> p a n", a=4)

        MOVED = {}
        for n in PRODUCTS:
            name, g = n.split(".")
            MOVED[n] = (half_act, n) if n in EVENTS[half_act] else (half_dve, "t1." + g if name == "l" else n)

        def each(m):
            return m.unsqueeze(1).broadcast_to([P, 2, P])

        def hcol(c, o):
            return half_b[:, bass.ds(c + o, 1)]

        def at(sema, n, what):
            names = EVENTS[sema]
            return n * len(names) + (names.index(what) + credit(sema))

        def credit(sema):
            return 2 if sema in (half_pe, half_act, half_dve, half_pool) else 1

        def before(sema, n):
            return n * len(EVENTS[sema]) + 1

        class Steps:

            def __init__(self, eng, *sems):
                self.eng, self.seen = eng, {s: [] for s in sems}

            def did(self, sema, what, ins):
                assert EVENTS[sema][len(self.seen[sema]) % len(EVENTS[sema])] == what, (what, self.seen[sema][-3:])
                self.seen[sema].append(what)
                ins.then_inc(sema, 1)

            def wait(self, sema, n, what):
                self.eng.wait_ge(sema, at(sema, n, what))

        B2 = b2_start
        GROUPS = 2
        LATS = ((0, 0), (1, 1), (3, 2), (4, 3), (5, 4))

        @block.scalar
        def _(act):
            w = Walk()

            def split(q, forced=False):
                if isinstance(q.turn, int) and (q.v >= n_pan or (q.v == B2 + 2 and not forced)):
                    return
                s = q.k % SLOTS
                act.wait_ge(panel_in[s], q.over4() * 16 + 16)
                if q.k >= SLOTS:
                    act.wait_ge(panel_done, (q + -3).v)
                nc.scalar.copy(wh[:, s, :], raw[:, s, :]).then_inc(hi_ready, 1)

            def panels(n, body):
                p0, g0 = w.p, w.g

                def step(j):
                    split(j + (p0 + 3))
                    body(j, j + p0, (g0 + j.k) % 2)
                turns(act, n, step, w.p + n in (n_pan, B2))
                w.p += n
                w.g += n

            def up():
                u0 = w.u

                def body(j, p, b):
                    act.wait_ge(panel_done, (p + 1).v)
                    act.wait_ge(u_free, (j + (u0 + 1)).v)
                    nc.scalar.activation(sq[:, j.k % 2, :], psum[:, b, :], ACT.Relu).then_inc(bank_free[b], 1)
                panels(NC, body)
                w.u += NC

            def only_split(n):
                panels(n, lambda j, p, b: None)

            def squares(src, mean, chunks):
                for c in chunks:
                    n = w.nsq
                    if mean:
                        act.wait_ge(d_ready, w.nd + 1)
                        w.nd += 1
                    if n >= 2:
                        act.wait_ge(sq_used, n - 1)
                    nc.scalar.activation(sq[:, c % 2, :], src[:, c, :], ACT.Square).then_inc(sq_ready, 1)
                    w.nsq += 1

            def root(mean):
                act.wait_ge(sq_used, w.nsq)
                nc.scalar.activation(sd, psum[:, 3, :], ACT.Sqrt, bias=eps_col[mean]).then_inc(sd_ready, 1)
                w.norm += 1

            def norm(src, mean, after=(), bcol=None, bo=0, final=False):
                for sema, n in after:
                    act.wait_ge(sema, n)
                squares(src, mean, range(NC))
                root(mean)
                if final:
                    return
                for c in range(NC):
                    act.wait_ge(t_ready, NC * (w.norm - 1) + c + 1)
                    if mean:
                        nc.scalar.activation(bh[bo][:, c, :], src[:, c, :], ACT.Identity, bias=pcol(*bcol(c)))
                        nc.scalar.activation(src[:, c, :], src[:, c, :], ACT.Identity, bias=pcol(*bcol(c))).then_inc(nhi_ready, 1)
                    else:
                        nc.scalar.copy(bh[bo][:, c, :], t2[:, c % 2, :]).then_inc(nhi_ready, 1)

            def silu(c):
                act.wait_ge(t_ready, NC * (w.norm - 1) + c + 1)
                nc.scalar.activation(sq[:, c % 2, :], y[:, c, :], ACT.Sigmoid, bias=pcol("cln_b", c))
                nc.scalar.activation(y[:, c, :], y[:, c, :], ACT.Identity, bias=pcol("cln_b", c)).then_inc(ysg, 1)
                act.wait_ge(yz, c + 1)
                nc.scalar.copy(bh[1][:, c, :], y[:, c, :]).then_inc(nhi_ready, 1)

            def ple(layer):
                act.wait_ge(pp_in, 16 * (layer + 1))
                nc.scalar.copy(ph[:, :, :], praw).then_inc(ph_ready, 1)

                p0, g0 = w.p, w.g
                for q in range(2):
                    split(Idx(0, p0 + q + 3))
                    for i in range(4):
                        if i < 3:
                            act.wait_ge(mid_done, w.mid + 3 * q + i + 1)
                        else:
                            act.wait_ge(panel_done, p0 + q + 1)
                        b = (g0 + i) % 2
                        nc.scalar.copy(pj[:, 4 * q + i, :], psum[:, b, :]).then_inc(bank_free[b], 1)
                w.mid += 6
                w.p += 2
                w.g += 8
                x0 = NC * w.ple

                def body(j, p, b):
                    act.wait_ge(panel_done, (p + 1).v)
                    nc.scalar.activation(sq[:, 0, :], psum[:, b, :], ACT.Sigmoid,
                                         bias=pcol("ple_b", j + NC * layer)).then_inc(bank_free[b], 1)
                    act.wait_ge(xn_ready, (j + (x0 + 1)).v)
                    nc.scalar.copy(bh[1][:, j.v, :], x[:, j.v, :]).then_inc(xnh_ready, 1)
                panels(NC, body)
                w.ple += 1

            def attention(kind, units, chunk0):
                h0, g0 = w.h, w.g

                def exps(u, e):
                    n = u * 2 + (h0 + e)
                    for i in range(NB):
                        col, width, _ = span(kind, i)
                        act.wait_ge(nm_ready, n * 4 + (i + 1))
                        if not isinstance(u, int) or n >= 2:
                            act.wait_ge(pt_ready, n * 4 - 4)
                        nc.scalar.activation(pa[:, e, col:col + width], psum[:, 4 + i, 0:width], ACT.Exp,
                                             bias=nm[:, e, i:i + 1], accum_out=sm[:, e, i:i + 1]).then_inc(exp_done, 1)
                    if kind == "swa":
                        k = u * 1 + 4 * e
                        sk = sink[:, bass.ds(k, 1)] if not isinstance(k, int) else sink[:, k:k + 1]
                        act.wait_ge(snk_done, u * 2 + e)
                        nc.scalar.activation(snk[:, 2, :], nm[:, e, :], ACT.Exp, bias=sk).then_inc(snk_ready, 1)

                def high(u, e):
                    b = (g0 + e) % 2
                    act.wait_ge(o_ready, u * 2 + (h0 + e + 1))
                    nc.scalar.copy(bh[0][64 * e:64 * e + 64, u + chunk0, :],
                                   psum[64 * e:64 * e + 64, b, :]).then_inc(ohi_done, 1)

                def body(u):
                    exps(u, 1)
                    exps(u + 1, 0)
                    high(u, 0)
                    high(u, 1)
                exps(0, 0)
                if units > 2:
                    with act.Fori(0, units - 1) as u:
                        body(u)
                else:
                    body(0)
                exps(units - 1, 1)
                high(units - 1, 0)
                high(units - 1, 1)
                w.h += 2 * units
                w.g += 2 * units

            def layer0_in():
                for q, c in ((0, 0), (1, 1), (2, None), (3, 2), (4, 3), (5, 4)):
                    split(Idx(0, w.p + 3))
                    if c is not None:
                        b = w.g % 2
                        act.wait_ge(panel_done, w.p + 1)
                        nc.scalar.copy(lat[:, c, :], psum[:, b, :]).then_inc(bank_free[b], 1)
                    w.p += 1
                    w.g += 1
                for c in range(5):
                    if c >= 2:
                        act.wait_ge(lat_ss, c - 1)
                    b = ((0, 1, 3, 4, 5)[c]) % 2
                    act.wait_ge(bank_free[b], (0, 1, 3, 4, 5)[c] // 2 + 1)
                    nc.scalar.activation(sq[:, c % 2, :], lat[:, c, :], ACT.Square).then_inc(lat_sq, 1)
                act.wait_ge(lat_ss, 5)
                nc.scalar.activation(sd, psum[:, 2, :], ACT.Sqrt, bias=eps_col["rms1"], scale=4.0).then_inc(lat_sd, 1)
                nc.scalar.activation(s1c, psum[:, 3, :], ACT.Sqrt, bias=eps_col["rms1"], scale=1024 / 384).then_inc(lat_sd, 1)
                for c in range(5):
                    act.wait_ge(lat_t, c + 1)
                    nc.scalar.copy(lath[:, c, :], lat[:, c, :]).then_inc(lat_h, 1)

            def mla_in(grp):
                split(Idx(0, w.p + 3))
                split(Idx(0, w.p + 4))
                w.mid += 1
                w.g += 2
                if grp:
                    act.wait_ge(v_staged, 2)
                for i in range(2):
                    b = w.g % 2
                    if i == 0:
                        act.wait_ge(mid_done, w.mid + 1)
                    else:
                        act.wait_ge(panel_done, w.p + 2)
                    nc.scalar.copy(va[:, 2 * i:2 * i + 2, 0:2 * P],
                                   psum[:, b, :].rearrange("p (a n) -> p a n", a=2)).then_inc(bank_free[b], 1)
                    w.g += 1
                split(Idx(0, w.p + 5))
                split(Idx(0, w.p + 6))
                w.mid += 3
                w.p += 4
                w.g += 4

            def token_major(dst, b, p):
                act.wait_ge(panel_done, p)
                nc.scalar.copy(dst, psum[:, b, :].rearrange("p (a n) -> p a n", a=NB)).then_inc(bank_free[b], 1)

            act.wait_ge(x_in, 16)
            for c in range(NC):
                nc.scalar.copy(bh[1][:, c, :], x[:, c, :]).then_inc(xh0, 1)
            for q in range(3):
                split(Idx(0, q))
            act.dma_start(rope[:, :], A["rope"]).then_inc(par_in, 16)
            act.wait_ge(par_in, 64)
            act.wait_ge(const_set, 1)
            eps_col = {True: eps[:, 0:1], False: eps[:, 1:2], "rms1": eps[:, 0:1]}
            layer0_in()
            for grp in range(GROUPS):
                mla_in(grp)
                attention("mla", 2, 2 * grp)
            act.wait_ge(o_ready, 8)
            act.wait_ge(qk_staged, 4)
            act.wait_ge(bank_free[0], w.g // 2)
            act.wait_ge(bank_free[1], w.g // 2)
            act.dma_start(relb[:, :], A["relb"]).then_inc(bias_in, 16)
            act.dma_start(oneh[:, :], A["oneh"]).then_inc(bias_in, 16)
            act.dma_start(negm[:, :], A["negm"]).then_inc(bias_in, 16)
            act.dma_start(sink[:, :], A["sink"].partition_broadcast(P)).then_inc(bias_in, 16)
            act.wait_ge(brow_ps, 1)
            act.dma_start(scratch.ap(), brow[:, :].unsqueeze(1).broadcast_to([8, P, SWA_F])).then_inc(brow_out, 16)
            act.wait_ge(brow_out, 16)
            act.dma_start(bias[:, :, :], bass.AP(scratch, P - 1, [[SWA_F - 1, P], [P * SWA_F, 8], [1, 2 * P]])).then_inc(bias_in, 16)
            for i in range(6):
                split(Idx(0, w.p + 3))
                b = w.g % 2
                if i == 0:
                    act.wait_ge(panel_done, w.p + 1)
                    nc.scalar.copy(ka[:, 0, :], psum[:, b, :]).then_inc(bank_free[b], 1)
                elif i == 1:
                    token_major(vs[:, :, :], b, w.p + 1)
                else:
                    act.wait_ge(panel_done, w.p + 1)
                    nc.scalar.activation(qa[:, i - 2, :], psum[:, b, :], ACT.Copy, scale=HEAD_SCALE).then_inc(bank_free[b], 1)
                w.p += 1
                w.g += 1
            attention("swa", 4, 4)
            only_split(NC)

            def feed_forward_and_gate(layer):
                norm(x, True, (), lambda c: ("ln1_b", NC * layer + c))
                for part_name in MLP:
                    if part_name[0] == "U":
                        up()
                    else:
                        only_split(NC)
                norm(x, True, (), lambda c: ("ln2_b", NC * layer + c))
                ple(layer)
            feed_forward_and_gate(0)
            if upto != "l0":
                split(Idx(0, w.p + 3))
                b = w.g % 2
                act.wait_ge(fsel_in, 32)
                act.wait_ge(panel_done, w.p + 1)
                nc.scalar.activation(ft[:, 0, :], psum[:, b, :], ACT.Identity, bias=fsel[:, 18:19]).then_inc(bank_free[b], 1)
                act.wait_ge(bank_free[b], w.g // 2 + 1)
                w.p += 1
                w.g += 1
                nc.scalar.activation(ft[:, 1, :], ft[:, 0, :], ACT.Abs).then_inc(act_step, 1)
                act.wait_ge(act_step, 1)
                nc.scalar.activation(ft[:, 2, :], ft[:, 1, :], ACT.Exp, scale=-1.0).then_inc(act_step, 1)
                act.wait_ge(act_step, 2)
                nc.scalar.activation(ft[:, 1, :], ft[:, 2, :], ACT.Ln, bias=1.0).then_inc(fox_a, 1)
                for grp in range(GROUPS):
                    p0, g0 = w.p, w.g

                    def queries(j, p, b):
                        act.wait_ge(panel_done, (p + 1).v)
                        nc.scalar.activation(qa[:, j.v, :], psum[:, b, :], ACT.Copy, scale=HEAD_SCALE).then_inc(bank_free[b], 1)

                    def values(j, p, b):
                        v = j.v * P
                        cols = slice(v, v + P) if isinstance(v, int) else bass.ds(v, P)
                        token_major(va[:, :, cols], b, (p + 1).v)
                    act.wait_ge(qk_staged, 8 + 4 * grp)
                    panels(4, queries)
                    only_split(4)
                    act.wait_ge(v_staged, 4 + 4 * grp)
                    panels(4, values)
                    attention("fox", 4, 4 * grp)
                only_split(NC)
                feed_forward_and_gate(1)

            if upto not in ("l0", "l1"):
                st = Steps(act, pair_act, post_act, half_act)
                act.wait_ge(xn_ready, 16)
                act.dma_start(wm[:, :, :], A["wm"]).then_inc(wk_in, 16)
                act.dma_start(o64[:, :], A["o64"]).then_inc(wk_in, 16)
                norm(x, False, ((xn_ready, 16),))
                act.wait_ge(scaled, 1)
                split(Idx(0, B2 + 2), forced=True)
                act.wait_ge(scaled, 2)
                for i, dst in enumerate((la, rn, zr, zv)):
                    split(Idx(0, w.p + 3))
                    b = w.g % 2
                    act.wait_ge(panel_done, w.p + 1)
                    if i >= 2:
                        act.wait_ge(wk_set, 1)
                    nc.scalar.copy(dst, psum[:, b, :]).then_inc(bank_free[b], 1)
                    w.p += 1
                    w.g += 1
                act.wait_ge(lora_z, 1)
                nc.scalar.activation(lw[0:64, :], la[0:64, :], ACT.Tanh)
                nc.scalar.copy(lw[64:128, :], la[64:128, :]).then_inc(lora_t, 1)
                act.wait_ge(lora_t, 1)
                nc.scalar.copy(lh[0][:, :], lw).then_inc(lora_h, 1)
                act.wait_ge(lora_z, 2)
                nc.scalar.activation(rn, kkn, ACT.Tanh, scale=0.5).then_inc(lora_t, 1)
                act.wait_ge(lora_z, 3)
                nc.scalar.copy(lh[1][:, :], kkn).then_inc(lora_h, 1)

                od0 = NC * 11

                def pair(c):
                    p0, g0, m0 = w.p, w.g, w.mid
                    split(Idx(c, p0 + 3))
                    act.wait_ge(mid_done, c * 2 + (m0 + 1))
                    nc.scalar.activation(lw, psum[:, g0 % 2, :], ACT.Tanh, bias=hcol(c, 0), scale=0.5).then_inc(bank_free[g0 % 2], 1)
                    act.wait_ge(mid_done, c * 2 + (m0 + 2))
                    b = (g0 + 1) % 2
                    nc.scalar.activation(la, psum[:, b, :], ACT.Tanh, bias=hcol(c, 8), scale=0.5).then_inc(bank_free[b], 1)
                    st.wait(pair_dve, c, "sums")
                    nc.scalar.activation(ep[:, :, 1:65], cu.rearrange("p (a t) -> p a t", a=8), ACT.Exp)
                    st.did(pair_act, "decay", nc.scalar.activation(em, cu, ACT.Exp, scale=-1.0))
                    if not isinstance(c, int) or c > 0:
                        roots(c + -1)

                    def copy_tile(i, dst, p):
                        b = (g0 + i) % 2
                        act.wait_ge(panel_done, Idx(c, p0 + p).v)
                        nc.scalar.copy(dst, psum[:, b, :]).then_inc(bank_free[b], 1)
                    split(Idx(c, p0 + 4))
                    copy_tile(3, zk, 2)
                    if not isinstance(c, int) or c > 0:
                        st.wait(post_dve, c + -1, "out")
                    copy_tile(2, gt[:, :], 1)
                    if not isinstance(c, int) or c > 0:
                        high(c + -1)
                    st.wait(pair_dve, c, "mixed")
                    st.did(pair_act, "square", nc.scalar.activation(sq[:, 0, :], zk, ACT.Square, scale=pcol("k_k", c)))
                    split(Idx(c, p0 + 5))
                    act.wait_ge(opnd_dve, c + od0)
                    copy_tile(4, zr, 3)
                    st.wait(pair_dve, c, "kmax")
                    st.did(pair_act, "root", nc.scalar.activation(kkn, rn, ACT.Sqrt))
                    split(Idx(c, p0 + 6))
                    copy_tile(5, zv, 4)
                    st.wait(pair_dve, c, "ready")
                    for f in range(2):
                        half(c * 2 + f, f)

                def roots(c):
                    st.wait(post_dve, c, "centred")
                    st.did(post_act, "osquare", nc.scalar.activation(sq[:, 0, :], zr, ACT.Square))
                    st.wait(post_pe, c, "var")
                    st.did(post_act, "oroot", nc.scalar.activation(rn, psum[:, 3, :], ACT.Sqrt, bias=eps[:, 2:3]))

                def high(c):
                    st.wait(post_dve, c, "out")
                    st.did(post_act, "high", nc.scalar.copy(bh[1][:, c, :], zr))

                def half(n, f):
                    cols = slice(f * 256, f * 256 + 256)
                    for sema in (half_pe, half_dve, half_pool):
                        act.wait_ge(sema, before(sema, n))
                    for e in range(2):
                        r = slice(64 * e, 64 * e + 64)
                        last = nc.scalar.copy(m_v[r, :, r], zv[r, cols].rearrange("p (a t) -> p a t", a=4))
                    st.did(half_act, "v", last)

                    def move(dst, product):
                        for g in range(2):
                            st.wait(half_pe, n, f"{product}.{g}")
                            st.did(half_act, f"{product}.{g}", nc.scalar.copy(dst[:, 2 * g:2 * g + 2, :], bank(f"{product}.{g}")))
                    move(m_at, "at")
                    move(m_bt, "bt")
                    move(m_kt, "kt")
                    move(m_vt, "vt")
                    move(m_z, "z2")
                    move(m_w, "w")
                    for b in LEVELS[1:]:
                        move(m_z, f"z{b}")
                    move(m_ta, "ta")
                    move(m_n, "n")
                    st.wait(half_pe, n, "o3")
                    for e in range(2):
                        r = slice(64 * e, 64 * e + 64)
                        last = nc.scalar.copy(zr[r, cols].rearrange("p (a t) -> p a t", a=4), o_bank[r, :, r])
                    st.did(half_act, "o", last)

                pair(0)
                with act.Fori(1, NC) as c:
                    pair(c)
                roots(NC - 1)
                high(NC - 1)
                w.p += 4 * NC
                w.g += 6 * NC
                w.mid += 2 * NC

                act.dma_start(cw[:, :, :], A["cw"]).then_inc(cw_in, 16)
                g0 = w.g

                def sigmoid(j, p, b):
                    if j.k % 2 == 0:
                        act.wait_ge(panel_done, (p + 1).v)
                        act.wait_ge(bank_free[1 - b], (j + (g0 - 3)).over2() + 1)
                        nc.scalar.activation(sq[:, j.k // 2, :], psum[:, b, :], ACT.Sigmoid,
                                             bias=pcol("b_gate", j.over4()) if j.k else 0.0).then_inc(bank_free[b], 1)
                panels(4 * NC, sigmoid)
                for j in range(NC):
                    split(Idx(0, w.p + 3))
                    b = w.g % 2
                    act.wait_ge(panel_done, w.p + 1)
                    nc.scalar.activation(sg[:, j, :], psum[:, b, :], ACT.Sigmoid, bias=pcol("b_gate", NC + j)).then_inc(bank_free[b], 1)
                    w.p += 1
                    w.g += 1
                    if j == 1:
                        squares(y, True, range(2))
                    if j == 3:
                        squares(y, True, range(2, NC))
                        root(True)
                    for c in {4: (0, 1, 2), 5: (3, 4, 5), 6: (6, 7)}.get(j, ()):
                        silu(c)

                def merged(j, p, b):
                    act.wait_ge(m_done, (j + 1).v)
                    nc.scalar.copy(mh[:, j.v, :], mg[:, j.v, :]).then_inc(mrg_h, 1)
                panels(NC, merged)
                only_split(NC)
                norm(x, False, ((bank_free[w.g % 2], w.g // 2), (bank_free[1 - w.g % 2], (w.g + 1) // 2)))
                for part_name in MLP:
                    if part_name[0] == "U":
                        up()
                    else:
                        only_split(NC)
                norm(x, False, ((bank_free[w.g % 2], w.g // 2), (bank_free[1 - w.g % 2], (w.g + 1) // 2)), final=True)

        @block.vector
        def _(dve):
            w = Walk()
            chain = Chain(dve, dve_step)
            link = chain.link

            def panels(n, body, links=0):
                p0, g0 = w.p, w.g
                chain.turns(n, lambda j: body(j, j + p0, (g0 + j.k) % 2, j + g0), links)
                w.p += n
                w.g += n

            def skip(n):
                w.p += n
                w.g += n

            def residual(scale, total):
                if total:
                    link(nc.vector.memset(s1, 0.0))

                def body(j, p, b, g):
                    dve.wait_ge(panel_done, (p + 1).v)
                    nc.vector.scalar_tensor_tensor(x[:, j.v, :], x[:, j.v, :], scale, psum[:, b, :],
                                                   ALU.mult, ALU.add).then_inc(bank_free[b], 1)
                    if total:
                        dve.wait_ge(bank_free[b], g.over2() + 1)
                        link(nc.vector.tensor_tensor(s1, s1, x[:, j.v, :], ALU.add))
                panels(NC, body, links=int(total))

            def up(hb):
                u0, d0 = w.u, w.od

                def body(j, p, b, g):
                    dve.wait_ge(bank_free[b], g.over2() + 1)
                    h = sq[:, j.k % 2, :]
                    nc.vector.tensor_tensor(bh[hb][:, j.v, :], h, h, ALU.mult)
                    nc.vector.tensor_tensor(t2[:, j.k % 2, :], h, h, ALU.mult).then_inc(u_free, 1)
                    dve.wait_ge(u_free, (j + (u0 + 3)).v)
                    nc.vector.tensor_tensor(bl[hb][:, j.v, :], t2[:, j.k % 2, :], bh[hb][:, j.v, :].bitcast(F32),
                                            ALU.subtract).then_inc(opnd_dve, 1)
                panels(NC, body)
                w.u += NC
                w.od += NC

            def norm(gcol, src=x):
                nc.vector.tensor_copy(s1c, s1).then_inc(s1_ready, 1)
                dve.wait_ge(mu_done, w.mean + 1)
                for c in range(NC):
                    nc.vector.tensor_tensor(src[:, c, :], src[:, c, :], psum[:, 2, :], ALU.subtract).then_inc(d_ready, 1)
                dve.wait_ge(sd_ready, w.norm + 1)
                link(nc.vector.reciprocal(rs, sd))
                for c in range(NC):
                    nc.vector.scalar_tensor_tensor(src[:, c, :], src[:, c, :], pcol(*gcol(c)), rs,
                                                   ALU.mult, ALU.mult).then_inc(t_ready, 1)
                w.norm += 1
                w.mean += 1
                w.op += NC

            def rms_norm(gain, final=False):
                dve.wait_ge(sd_ready, w.norm + 1)
                link(nc.vector.reciprocal(rs, sd))
                for c in range(NC):
                    dst = x[:, c, :] if final else t2[:, c % 2, :]
                    if c >= 2 and not final:
                        dve.wait_ge(opnd_pool, w.op + c - 1)
                    nc.vector.scalar_tensor_tensor(dst, x[:, c, :], pcol(gain, c), rs, ALU.mult, ALU.mult).then_inc(t_ready, 1)
                w.norm += 1
                w.op += NC

            def ple(layer):
                dve.wait_ge(ph_ready, layer + 1)
                nc.vector.tensor_tensor(pl[:, :, :], praw, ph[:, :, :].bitcast(F32), ALU.subtract).then_inc(pl_ready, 1)
                w.p += 2
                w.g += 8
                x0 = NC * w.ple

                def body(j, p, b, g):
                    dve.wait_ge(bank_free[b], g.over2() + 1)
                    link(nc.vector.tensor_tensor(t2[:, 0, :], sq[:, 0, :], pj[:, j.v, :], ALU.mult))
                    nc.vector.tensor_tensor(x[:, j.v, :], x[:, j.v, :], t2[:, 0, :], ALU.add).then_inc(xn_ready, 1)
                    dve.wait_ge(xnh_ready, (j + (x0 + 1)).v)
                    nc.vector.tensor_tensor(bl[1][:, j.v, :], x[:, j.v, :], bh[1][:, j.v, :].bitcast(F32),
                                            ALU.subtract).then_inc(opnd_dve, 1)
                panels(NC, body, links=1)
                w.ple += 1
                w.od += NC

            def attention(kind, units, chunk0):
                h0, g0 = w.h, w.g

                def soft(u, e):
                    n = u * 2 + (h0 + e)
                    for i in range(NB):
                        _, width, _ = span(kind, i)
                        dve.wait_ge(s_ready, n * 4 + (i + 1))
                        s_i = psum[:, 4 + i, 0:width]
                        if kind == "swa":
                            k = u * 1 + 4 * e
                            nk = nsink[:, k:k + 1] if isinstance(k, int) else nsink[:, bass.ds(k, 1)]
                            link(nc.vector.tensor_reduce(snk[:, 0, i:i + 1], s_i, AX, ALU.max, negate=True))
                            nc.vector.tensor_scalar(nm[:, e, i:i + 1], snk[:, 0, i:i + 1], nk, None,
                                                    ALU.min).then_inc(nm_ready, 1)
                        else:
                            nc.vector.tensor_reduce(nm[:, e, i:i + 1], s_i, AX, ALU.max, negate=True).then_inc(nm_ready, 1)
                    dve.wait_ge(exp_done, n * 4 + 4)
                    if kind == "swa":
                        dve.wait_ge(snk_ready, u * 2 + (e + 1))
                        nc.vector.tensor_tensor(sm[:, e, :], sm[:, e, :], snk[:, 2, :], ALU.add).then_inc(snk_done, 1)
                        dve.wait_ge(snk_done, u * 2 + (e + 1))
                    nc.vector.reciprocal(rc[:, e, :], sm[:, e, :]).then_inc(rc_done, 1)

                def turned(u, e):
                    n = u * 2 + (h0 + e)
                    if not isinstance(n, int) or n >= 1:
                        dve.wait_ge(o_ready, n)
                    for j in range(NB):
                        width = P * len(pt_blocks(kind, j))
                        dve.wait_ge(pt_ready, n * 4 + (j + 1))
                        nc.vector.tensor_copy(w4[:, pts_at(kind, j):pts_at(kind, j) + width],
                                              psum[:, 2 + j % 2, 0:width]).then_inc(pt_copied, 1)

                def low(u, e):
                    b = (g0 + e) % 2
                    dve.wait_ge(ohi_done, u * 2 + (h0 + e + 1))
                    r = slice(64 * e, 64 * e + 64)
                    nc.vector.tensor_tensor(bl[0][r, u + chunk0, :], psum[r, b, :], bh[0][r, u + chunk0, :].bitcast(F32),
                                            ALU.subtract).then_inc(bank_free[b], 1)

                def body(u):
                    soft(u, 1)
                    turned(u, 0)
                    soft(u + 1, 0)
                    low(u, 0)
                    turned(u, 1)
                    low(u, 1)
                soft(0, 0)
                if units > 2:
                    at = chain.n
                    with dve.Fori(0, units - 1) as u:
                        chain.turn, chain.per = u, 8 * (kind == "swa")
                        body(u)
                    assert chain.n - at == chain.per
                    chain.n += chain.per * (units - 2)
                    chain.turn = chain.per = 0
                else:
                    body(0)
                soft(units - 1, 1)
                turned(units - 1, 0)
                low(units - 1, 0)
                turned(units - 1, 1)
                low(units - 1, 1)
                w.h += 2 * units
                w.g += 2 * units

            def rotate(dst, b, scale):
                nc.vector.scalar_tensor_tensor(rt[64:96, 0, :], psum[96:128, b, :], scale, rope[96:128, :], ALU.mult, ALU.mult)
                link(nc.vector.scalar_tensor_tensor(rt[64:96, 1, :], psum[64:96, b, :], scale, rope[64:96, :],
                                                    ALU.mult, ALU.mult))
                for d in dst:
                    last = nc.vector.tensor_tensor(d, rt[64:96, 0, :], rt[64:96, 1, :], ALU.add)
                return last

            def mla_in(grp):
                if grp:
                    dve.wait_ge(qk_staged, 2)
                else:
                    dve.wait_ge(bank_free[0], 2)
                for t in range(2):
                    b = w.g % 2
                    if t == 0:
                        dve.wait_ge(mid_done, w.mid + 1)
                    else:
                        dve.wait_ge(panel_done, w.p + 1)
                    nc.vector.tensor_copy(ka[0:64, 2 * t, :], psum[0:64, b, :])
                    nc.vector.tensor_copy(ka[0:64, 2 * t + 1, :], psum[64:128, b, :]).then_inc(bank_free[b], 1)
                    w.g += 1
                w.g += 2
                w.mid += 2
                for t in range(4):
                    b = w.g % 2
                    if t % 2 == 0:
                        w.mid += 1
                        dve.wait_ge(mid_done, w.mid)
                    else:
                        dve.wait_ge(panel_done, w.p + 3 + t // 2)
                    if t:
                        dve.wait_ge(bank_free[1 - b], (w.g - 1) // 2 + 1)
                    nc.vector.tensor_scalar(qa[0:64, t, :], psum[0:64, b, :], MLA_SCALE, None, ALU.mult)
                    rotate([qa[64:96, t, :]], b, MLA_SCALE).then_inc(bank_free[b], 1)
                    w.g += 1
                w.p += 4

            nc.vector.memset(ones[:, :], 1.0 / D)
            nc.vector.memset(eps[:, 0:1], LN_EPS)
            nc.vector.memset(eps[:, 2:3], GN_EPS)
            nc.vector.memset(eps[:, 1:2], RMS_EPS).then_inc(const_set, 1)
            nc.vector.memset(sq[:, 0, 0:1], 0.0).then_inc(u_free, 2)
            for c in range(NC):
                dve.wait_ge(xh0, c + 1)
                nc.vector.tensor_tensor(bl[1][:, c, :], x[:, c, :], bh[1][:, c, :].bitcast(F32), ALU.subtract).then_inc(opnd_dve, 1)
            w.od += NC
            dve.wait_ge(par_in, 64)
            dve.wait_ge(panel_done, 3)
            rotate([ka[64:96, h, :] for h in range(4)], 0, 1.0).then_inc(bank_free[0], 1)
            w.p += 6
            w.g += 6
            dve.wait_ge(lat_sd, 1)
            link(nc.vector.reciprocal(rs, sd))
            dve.wait_ge(lat_sd, 2)
            link(nc.vector.reciprocal(s1, s1c))
            for c in range(5):
                col = pcol("kv_norm", c) if c < 2 else pcol("q_norm", c - 2)
                nc.vector.scalar_tensor_tensor(lat[:, c, :], lat[:, c, :], col, rs if c < 2 else s1,
                                               ALU.mult, ALU.mult).then_inc(lat_t, 1)
            for c in range(5):
                dve.wait_ge(lat_h, c + 1)
                nc.vector.tensor_tensor(latl[:, c, :], lat[:, c, :], lath[:, c, :].bitcast(F32), ALU.subtract).then_inc(lat_l, 1)
            for grp in range(GROUPS):
                mla_in(grp)
                attention("mla", 2, 2 * grp)
            dve.wait_ge(brow_mm, 1)
            dve.wait_ge(bias_in, 64)
            nc.vector.tensor_scalar(nsink[:, :], sink[:, :], -1.0, None, ALU.mult)
            nc.vector.tensor_tensor(brow[:, :], psum[0:8, 3, 0:SWA_F], negm[:, :], ALU.add).then_inc(brow_ps, 1)
            skip(6)
            attention("swa", 4, 4)
            residual(ALPHA, True)

            def feed_forward_and_gate(layer):
                norm(lambda c: ("ln1_g", NC * layer + c))
                for part_name in MLP:
                    q = int(part_name[1])
                    if part_name[0] == "U":
                        up(1 + q % 2)
                    else:
                        residual(ALPHA if q == 0 else 1.0, q == 3)
                norm(lambda c: ("ln2_g", NC * layer + c))
                ple(layer)
            feed_forward_and_gate(0)
            if upto != "l0":
                skip(1)
                dve.wait_ge(fsel_in, 32)
                link(nc.vector.memset(fone, 1.0))
                dve.wait_ge(fox_a, 1)
                link(nc.vector.scalar_tensor_tensor(ft[:, 2, :], ft[:, 0, :], 0.0, ft[:, 1, :], ALU.min, ALU.subtract))
                nc.vector.tensor_tensor_scan(fc[:, :], fone, ft[:, 2, :], 0.0, ALU.mult, ALU.add).then_inc(fox_b, 1)
                for grp in range(GROUPS):
                    skip(4)
                    dve.wait_ge(qk_staged, 8 + 4 * grp)

                    def keys(j, p, b, g):
                        dve.wait_ge(panel_done, (p + 1).v)
                        nc.vector.tensor_copy(ka[:, j.v, :], psum[:, b, :]).then_inc(bank_free[b], 1)
                    panels(4, keys)
                    skip(4)
                    attention("fox", 4, 4 * grp)
                residual(ALPHA, True)
                feed_forward_and_gate(1)

            if upto not in ("l0", "l1"):
                st = Steps(dve, pair_dve, post_dve, half_dve)
                wait_tile = lambda b, count: dve.wait_ge(bank_free[b], count)
                for q, gains in ((B2 + 2, (0, 1)), (B2 + 3, (2, 2))):
                    s = q % SLOTS
                    dve.wait_ge(panel_in[s], q // SLOTS * 16 + 16)
                    for k in range(NC):
                        if gains[0] == gains[1]:
                            c = slice(k * P, k * P + P)
                            last = nc.vector.tensor_scalar(raw[:, s, c], raw[:, s, c], pcol("mu_lora", gains[0] * NC + k),
                                                           None, ALU.mult)
                            continue
                        for e in range(2):
                            c = slice(k * P + 64 * e, k * P + 64 * e + 64)
                            last = nc.vector.tensor_scalar(raw[:, s, c], raw[:, s, c], pcol("mu_lora", gains[e] * NC + k),
                                                           None, ALU.mult)
                    last.then_inc(scaled, 1)
                nc.vector.memset(m_v[:, :, :], 0.0)
                for m, sema in ((m_a, half_pe), (m_b, half_act), (m_k, half_dve), (m_r, half_pool)):
                    nc.vector.memset(m[:, :, :], 0.0).then_inc(sema, 1)
                for a in z:
                    nc.vector.memset(a[:, 0:1], 0.0)
                nc.vector.memset(ep[:, :, 0:1], 1.0)
                link(nc.vector.memset(going[:, :], 1.0))
                nc.vector.memset(going[:, :].rearrange("p (a t) -> p a t", t=64)[:, :, 0:1], 0.0)
                nc.vector.tensor_scalar(half_b[:, 0:8], par[:, PAR["w0"][0]:PAR["w0"][0] + 8], 0.5, None, ALU.mult)
                nc.vector.tensor_scalar(half_b[:, 8:16], par[:, PAR["a0"][0]:PAR["a0"][0] + 8], 0.5, None,
                                        ALU.mult).then_inc(wk_set, 1)
                rms_norm("norm_mix")
                g = w.g
                wait_tile(g % 2, g // 2 + 2)
                link(nc.vector.tensor_tensor(la, la, z[0][:, 0:T], ALU.add))
                nc.vector.tensor_tensor(la, la, zr, ALU.subtract).then_inc(lora_z, 1)
                wait_tile(1 - g % 2, (g + 1) // 2 + 2)
                link(nc.vector.tensor_tensor(kkn, rn, z[2][:, 0:T], ALU.add))
                nc.vector.tensor_tensor(kkn, kkn, zv, ALU.subtract).then_inc(lora_z, 1)
                dve.wait_ge(lora_t, 2)
                nc.vector.tensor_scalar(kkn, rn, 0.5, 0.5, ALU.mult, ALU.add).then_inc(lora_z, 1)
                for a, full in ((0, lw), (1, kkn)):
                    dve.wait_ge(lora_h, a + 1)
                    nc.vector.tensor_tensor(ll[a][:, :], full, lh[a][:, :].bitcast(F32), ALU.subtract).then_inc(lora_l, 1)
                skip(4)
                dve.wait_ge(wk_in, 32)
                V = nc.vector

                def pair(c):
                    g0 = w.g

                    def tile_moved(i):
                        wait_tile((g0 + i) % 2, c * 3 + ((g0 + i) // 2 + 1))

                    def shift(i, dst):
                        link(V.tensor_tensor(sq[:, 0, :], z[i][:, 0:T], dst, ALU.subtract))
                        return V.scalar_tensor_tensor(dst, sq[:, 0, :], pcol_c("mu_rkv", i, c), dst, ALU.mult, ALU.add)
                    tile_moved(0)
                    half_e = 0.5 * np.exp(-0.5)
                    link(V.tensor_scalar(lw, lw, -half_e, -half_e, ALU.mult, ALU.add))
                    st.did(pair_dve, "sums", V.tensor_tensor_scan(cu, going[:, :], lw, 0.0, ALU.mult, ALU.add))
                    tile_moved(1)
                    if not isinstance(c, int) or c > 0:
                        centre(c + -1)
                    link(V.tensor_scalar(la, la, 0.5, 0.5, ALU.mult, ALU.add))
                    st.wait(pair_dve, c, "sums")
                    link(V.tensor_scalar(lw, la, -1.0, pcol_c("k_a", 0, c), ALU.add, ALU.mult))
                    if not isinstance(c, int) or c > 0:
                        output(c + -1)
                    tile_moved(3)
                    st.did(pair_dve, "mixed", shift(1, zk))
                    st.wait(pair_pe, c, "kk")
                    st.did(pair_dve, "kmax", V.tensor_scalar(rn, psum[:, 2, :], 64.0, 1e-24, ALU.mult, ALU.max))
                    tile_moved(4)
                    link(shift(0, zr))
                    st.wait(pair_act, c, "root")
                    link(V.reciprocal(rn, kkn))
                    link(V.scalar_tensor_tensor(kkn, zk, pcol_c("k_k", 0, c), rn, ALU.mult, ALU.mult))
                    link(V.scalar_tensor_tensor(zk, lw, 1.0, zk, ALU.add, ALU.mult))
                    link(V.tensor_tensor(la, kkn, la, ALU.mult))
                    st.did(pair_dve, "prod", V.scalar_tensor_tensor(sq[:, 1, :], zr, pcol_c("r_k", 0, c), zk, ALU.mult, ALU.mult))
                    operands(c * 2, 0)
                    tile_moved(5)
                    link(shift(2, zv))
                    st.wait(pair_pe, c, "bonus")
                    st.did(pair_dve, "ready", V.scalar_tensor_tensor(sq[:, 1, :], psum[:, 7, :], 64.0, zv, ALU.mult, ALU.mult))
                    half(c * 2, 0)
                    operands(c * 2 + 1, 1)
                    half(c * 2 + 1, 1)

                def centre(c):
                    st.wait(post_pe, c, "mean")
                    st.did(post_dve, "centred", V.tensor_tensor(zr, zr, psum[:, 2, :], ALU.subtract))

                def output(c):
                    st.wait(post_act, c, "oroot")
                    link(V.reciprocal(kkn, rn))
                    link(V.scalar_tensor_tensor(zr, zr, pcol_c("lnx_g", 0, c), kkn, ALU.mult, ALU.mult))
                    link(V.scalar_tensor_tensor(zr, zr, pcol_c("lnx_b", 0, c), sq[:, 1, :], ALU.add, ALU.add))
                    st.did(post_dve, "out", V.tensor_tensor(zr, zr, gt[:, :], ALU.mult))
                    st.wait(post_act, c, "high")
                    V.tensor_tensor(bl[1][:, c, :], zr, bh[1][:, c, :].bitcast(F32), ALU.subtract).then_inc(opnd_dve, 1)

                def operands(n, f):
                    cols = slice(f * 256, f * 256 + 256)
                    for sema in (half_pe, half_pool):
                        dve.wait_ge(sema, before(sema, n))

                    def chunks(a, r):
                        return a[r, cols].rearrange("p (a t) -> p a t", a=4)
                    decay_before, decay_upto = ep[:, 4 * f:4 * f + 4, 0:64], ep[:, 4 * f:4 * f + 4, 1:65]
                    rows = [slice(0, 64), slice(64, 128)]
                    for r in rows:
                        last = V.scalar_tensor_tensor(m_a[r, :, r], chunks(kkn, r), -1.0, decay_before[r], ALU.mult, ALU.mult)
                    st.did(half_dve, "a", last)
                    for r in rows:
                        last = V.tensor_tensor(m_b[r, :, r], chunks(la, r), chunks(em, r), ALU.mult)
                    st.did(half_dve, "b", last)
                    for r in rows:
                        last = V.tensor_tensor(m_k[r, :, r], chunks(zk, r), chunks(em, r), ALU.mult)
                    st.did(half_dve, "k", last)
                    for r in rows:
                        last = V.tensor_tensor(m_r[r, :, r], chunks(zr, r), decay_upto[r], ALU.mult)
                    st.did(half_dve, "r", last)

                def half(n, f):
                    def grouped(name, op, chained=False, also=None):
                        for g in range(2):
                            st.wait(half_pe, n, f"{name}.{g}")
                            op(slice(2 * g, 2 * g + 2), g)

                    def did(name, ins):
                        st.did(half_dve, name, ins)

                    def masked(dst, product, m):
                        grouped(product, lambda ch, g: did(f"{product}.{g}", V.tensor_tensor(
                            dst[:, ch, :], bank(f"{product}.{g}"), each(wm[:, m, :]), ALU.mult)))

                    def first_t(ch, g):
                        link(V.tensor_tensor(m_t[:, ch, :], bank(f"l.{g}"), each(wm[:, 2, :]), ALU.mult))
                        did(f"t1.{g}", V.tensor_tensor(m_t[:, ch, :], m_t[:, ch, :], each(ident[:, :]), ALU.add))

                    def first_x(ch, g):
                        link(V.tensor_tensor(m_x[:, ch, :], m_lt[:, ch, :], each(wm[:, 3, :]), ALU.mult))
                        did(f"x1.{g}", V.tensor_tensor(m_x[:, ch, :], m_x[:, ch, :], each(ident[:, :]), ALU.add))
                    grouped("l", first_t)
                    masked(m_lt, "lt", 0)
                    masked(m_rb, "rb", 1)
                    masked(m_ak, "ak", 0)
                    masked(m_rk, "rk", 1)
                    st.wait(half_dve, n, "rk.1")
                    grouped("bt", first_x)
                    for b in LEVELS:
                        for m, dst in (("t", m_t), ("x", m_x)):
                            if m + str(b) != "t32":
                                grouped(f"{m}{b}", lambda ch, g: did(f"{m}{b}.{g}", V.tensor_tensor(
                                    dst[:, ch, :], dst[:, ch, :], bank(f"{m}{b}.{g}"), ALU.add)))
                    grouped("tw", lambda ch, g: did(f"tw.{g}", V.tensor_copy(m_tw[:, ch, :], bank(f"tw.{g}"))))

                    def step_matrix(chs, g):
                        for i in range(2):
                            ch = 2 * g + i
                            last = V.scalar_tensor_tensor(m_mm[:, ch, :], ident[:, :], ep[:, 4 * f + ch, 64:65],
                                                          bank(f"mm.{g}")[:, i, :], ALU.mult, ALU.add)
                        did(f"mm.{g}", last)
                    grouped("mm", step_matrix)
                    grouped("p", lambda ch, g: did(f"p.{g}", V.tensor_tensor(m_p[:, ch, :], m_r[:, ch, :], bank(f"p.{g}"), ALU.add)))
                    if f == 0:
                        did("s0", V.memset(m_s[:, 0, :], 0.0))
                    else:
                        did("s0", V.tensor_copy(m_s[:, 0, :], m_s[:, 4, :]))
                    st.wait(half_act, n, "n.1")
                    st.wait(half_dve, n, "s0")
                    for ch in range(4):
                        st.wait(half_pe, n, f"c{ch}")
                        did(f"s{ch + 1}", V.tensor_tensor(m_s[:, ch + 1, :], bank(f"c{ch}")[:, 0, :], m_n[:, ch, :], ALU.add))
                    st.wait(half_dve, n, "s4")

                def pcol_c(name, i, c):
                    return par[:, bass.ds(c + (PAR[name][0] + NC * i), 1)]
                pair(0)
                at0 = chain.n
                chain.n -= PAIR_LINKS
                with dve.Fori(1, NC) as c:
                    chain.turn, chain.per = c, PAIR_LINKS
                    pair(c)
                assert chain.n == at0, (chain.n - at0 + PAIR_LINKS)
                chain.n += PAIR_LINKS * (NC - 1)
                chain.turn = chain.per = 0
                centre(NC - 1)
                output(NC - 1)
                w.p += 4 * NC
                w.g += 6 * NC
                w.od += NC
                link(V.memset(ub[:, 0:30], 0.0))
                link(V.memset(s1, 0.0))
                dve.wait_ge(cw_in, 16)
                p0, g0 = w.p, w.g

                def branches(c):
                    def gated(i, dst, slot):
                        b = (g0 + i) % 2
                        dve.wait_ge(panel_done, Idx(c, p0 + i + 1).v)
                        dve.wait_ge(bank_free[1 - b], Idx(c, g0 + i - 1).over2() + 1)
                        V.tensor_tensor(dst, psum[:, b, :], sq[:, slot, :], ALU.mult).then_inc(bank_free[b], 1)
                        dve.wait_ge(bank_free[b], Idx(c, g0 + i).over2() + 1)

                    def taps(some):
                        for tap in some:
                            link(V.scalar_tensor_tensor(y[:, c, :], ub[:, tap:tap + T], cw[:, c, tap:tap + 1], y[:, c, :],
                                                        ALU.mult, ALU.add))
                    gated(1, ub[:, 30:], 0)
                    link(V.tensor_scalar(y[:, c, :], ub[:, 0:T], cw[:, c, 0:1], pcol_c("conv_b", 0, c),
                                         ALU.mult, ALU.add))
                    taps(range(1, 16))
                    gated(3, mg[:, c, :], 1)
                    taps(range(16, 31))
                    link(V.tensor_tensor(s1, s1, y[:, c, :], ALU.add))
                at0 = chain.n
                with dve.Fori(0, NC) as c:
                    chain.turn, chain.per = c, CHUNK_LINKS
                    branches(c)
                assert chain.n - at0 == CHUNK_LINKS, chain.n - at0
                chain.n += CHUNK_LINKS * (NC - 1)
                chain.turn = chain.per = 0
                skip(5 * NC)
                norm(lambda c: ("cln_g", c), y)
                for c in range(NC):
                    dve.wait_ge(ysg, c + 1)
                    V.tensor_tensor(y[:, c, :], y[:, c, :], sq[:, c % 2, :], ALU.mult).then_inc(yz, 1)

                def merged(j, p, b, g):
                    slot = j.k % 2
                    dve.wait_ge(panel_done, (p + 1).v)
                    V.tensor_tensor(t2[:, slot, :], psum[:, b, :], sg[:, j.v, :], ALU.mult).then_inc(bank_free[b], 1)
                    dve.wait_ge(bank_free[b], g.over2() + 1)
                    V.tensor_tensor(mg[:, j.v, :], mg[:, j.v, :], t2[:, slot, :], ALU.add).then_inc(m_done, 1)
                    dve.wait_ge(mrg_h, (j + 1).v)
                    V.tensor_tensor(ml[:, j.v, :], mg[:, j.v, :], mh[:, j.v, :].bitcast(F32), ALU.subtract).then_inc(opnd_dve, 1)
                panels(NC, merged)
                w.od += NC
                residual(1.0, False)
                rms_norm("norm_ff")
                for part_name in MLP:
                    if part_name[0] == "U":
                        up(1 + int(part_name[1]) % 2)
                    else:
                        residual(1.0, False)
                rms_norm("norm_fin", final=True)

        @block.gpsimd
        def _(pool):
            w = Walk()

            def low(q, forced=False):
                if isinstance(q.turn, int) and (q.v >= n_pan or (q.v == B2 + 2 and not forced)):
                    return
                s = q.k % SLOTS
                pool.wait_ge(hi_ready, (q + 1).v)
                nc.gpsimd.tensor_tensor(wl[:, s, :], raw[:, s, :], wh[:, s, :].bitcast(F32), ALU.subtract).then_inc(lo_ready, 1)

            def panels(n):
                p0 = w.p
                turns(pool, n, lambda j: low(j + (p0 + 3)), w.p + n in (n_pan, B2))
                w.p += n

            def norm(bo, src=x, between=lambda c: None):
                for c in range(NC):
                    between(c)
                    pool.wait_ge(nhi_ready, NC * w.norm + c + 1)
                    y_c = t2[:, c % 2, :] if src is t2 else src[:, c, :]
                    nc.gpsimd.tensor_tensor(bl[bo][:, c, :], y_c, bh[bo][:, c, :].bitcast(F32),
                                            ALU.subtract).then_inc(opnd_pool, 1)
                w.norm += 1
                w.op += NC

            def attention(kind, units):
                h0, q0, v0 = w.h, w.qs, w.vs

                def stage_qk(u):
                    if not (isinstance(u, int) and u + h0 == 0):
                        pool.wait_ge(s_ready, u * 8 + 4 * h0)
                    if kind == "mla":
                        nc.gpsimd.tensor_copy(qs[0:96, :], qa[0:96, 2 * u:2 * u + 2, :].rearrange("p a b -> p (a b)"))
                        nc.gpsimd.tensor_copy(ks[0:96, :], ka[0:96, 2 * u:2 * u + 2, :].rearrange("p a b -> p (a b)")).then_inc(qk_staged, 1)
                        return
                    if kind == "swa":
                        nc.gpsimd.tensor_copy(qs[:, 0:T], qa[:, u, :]).then_inc(qk_staged, 1)
                        return
                    for a in range(2):
                        k = u + (8 * a + (h0 - 16) // 2)
                        col = slice(k, k + 1) if isinstance(k, int) else bass.ds(k, 1)
                        nc.gpsimd.tensor_copy(fsc[:, a:a + 1], fsel[:, col]).then_inc(fox_c, 1)
                    nc.gpsimd.tensor_copy(qs[:, 0:T], qa[:, u, :])
                    pool.wait_ge(fox_c, u * 2 + (2 + (h0 - 16)))
                    nc.gpsimd.tensor_copy(ks[:, 0:T], ka[:, u, :])
                    nc.gpsimd.tensor_scalar(fq[:, :], fc[:, :], fsc[:, 0:1], fsel[:, 16:17], ALU.mult, ALU.add)
                    last = nc.gpsimd.tensor_scalar(fk[:, :], fc[:, :], fsc[:, 1:2], fsel[:, 17:18], ALU.mult, ALU.add)
                    last.then_inc(qk_staged, 1)

                def stage_v(u):
                    if kind == "swa":
                        return
                    if not (isinstance(u, int) and u + h0 == 0):
                        pool.wait_ge(o_ready, u * 2 + h0)
                    c = u * P
                    cols = slice(c, c + P) if isinstance(c, int) else bass.ds(c, P)
                    nc.gpsimd.tensor_copy(vs[:, :, :], va[:, :, cols]).then_inc(v_staged, 1)

                def scale(u, e):
                    n = u * 2 + (h0 + e)
                    pool.wait_ge(rc_done, n + 1)
                    for i in range(NB):
                        col, width, _ = span(kind, i)
                        if i == 0:
                            ins = nc.gpsimd.tensor_tensor(pa[:, e, col:col + width], pa[:, e, col:col + width],
                                                          rc[:, e, i:i + 1].broadcast_to([P, width]), ALU.mult)
                        else:
                            ins = nc.gpsimd.tensor_scalar(pa[:, e, col:col + width], pa[:, e, col:col + width],
                                                          rc[:, e, i:i + 1], None, ALU.mult)
                        ins.then_inc(p_ready, 1)

                def body(u):
                    scale(u, 1)
                    stage_qk(u + 1)
                    scale(u + 1, 0)
                    stage_v(u + 1)
                pool.wait_ge(bank_free[0], (w.g + 1) // 2)
                pool.wait_ge(bank_free[1], w.g // 2)
                stage_qk(0)
                stage_v(0)
                scale(0, 0)
                if units > 2:
                    with pool.Fori(0, units - 1) as u:
                        body(u)
                else:
                    body(0)
                scale(units - 1, 1)
                w.qs += units
                w.vs += units * (kind != "swa")
                w.h += 2 * units
                w.g += 2 * units

            for q in range(3):
                low(Idx(0, q))
            w.p = 0
            w.qs = w.vs = 0
            panels(6)
            w.g = 6
            for grp in range(GROUPS):
                panels(4)
                w.g += 8
                attention("mla", 2)
            panels(6)
            w.g += 6
            attention("swa", 4)
            panels(NC)
            w.g += NC

            def feed_forward_and_gate(layer):
                norm(0)
                panels(8 * NC)
                norm(0)
                pool.dma_start(praw, A["pT"][:, 2 * layer:2 * layer + 2, :]).then_inc(pp_in, 16)
                panels(2)
                panels(NC)
                w.g += 8 * NC + 8 + NC
            feed_forward_and_gate(0)
            if upto != "l0":
                pool.dma_start(fsel[:, 0:18], A["fsel"]).then_inc(fsel_in, 16)
                pool.dma_start(fsel[:, 18:19], A["bf"]).then_inc(fsel_in, 16)
                panels(1)
                w.g += 1
                pool.wait_ge(fsel_in, 32)
                for grp in range(GROUPS):
                    panels(12)
                    w.g += 12
                    pool.wait_ge(fox_b, 1)
                    attention("fox", 4)
                panels(NC)
                w.g += NC
                feed_forward_and_gate(1)

            if upto not in ("l0", "l1"):
                norm(0, t2)
                low(Idx(0, B2 + 2), forced=True)
                panels(4)
                st = Steps(pool, half_pool)

                def half(n, f):
                    for sema in (half_pe, half_act):
                        pool.wait_ge(sema, before(sema, n))
                    last_decay = ep[:, 4 * f:4 * f + 4, 64:65].broadcast_to([P, 4, P])
                    st.wait(half_dve, n, "b")
                    st.did(half_pool, "bd", nc.gpsimd.tensor_tensor(m_bd[:, :, :], m_b[:, :, :], last_decay, ALU.mult))
                    st.wait(half_dve, n, "k")
                    st.did(half_pool, "kd", nc.gpsimd.tensor_tensor(m_kd[:, :, :], m_k[:, :, :], last_decay, ALU.mult))
                    for i, b in enumerate(LEVELS):
                        for g in range(2):
                            if i == 0:
                                st.wait(half_dve, n, f"lt.{g}")
                            else:
                                st.wait(half_pe, n, f"z{LEVELS[i - 1]}.{g}")
                            ch = slice(2 * g, 2 * g + 2)
                            st.did(half_pool, f"off{b}.{g}", nc.gpsimd.tensor_tensor(
                                m_off[:, ch, :], m_lt[:, ch, :], each(wm[:, 4 + i, :]), ALU.mult))

                def pair(c):
                    for i in range(4):
                        low(Idx(c, p0 + 3 + i))
                    for f in range(2):
                        half(c * 2 + f, f)
                pool.wait_ge(wk_in, 32)
                p0 = w.p
                with pool.Fori(0, NC) as c:
                    pair(c)
                w.p += 4 * NC
                panels(4 * NC)
                panels(5)

                def between(c):
                    if c in (3, 5, 7):
                        panels(1)
                norm(1, y, between)
                panels(NC)
                panels(NC)
                norm(0, t2)
                panels(8 * NC)

        @block.tensor
        def _(pe):
            w = Walk()

            def three(out, hi_a, lo_a, hi_b, lo_b, first, last):
                nc.tensor.matmul(out, hi_a, hi_b, start=first, stop=False)
                nc.tensor.matmul(out, hi_a, lo_b, start=False, stop=False)
                return nc.tensor.matmul(out, lo_a, hi_b, start=False, stop=last)

            def bank_wait(b, g):
                if not isinstance(g.turn, int) or g.v >= 2:
                    pe.wait_ge(bank_free[b], g.over2())

            def panels(n, bo, ready=None):
                p0, g0 = w.p, w.g

                def step(j):
                    p, b = j + p0, (g0 + j.k) % 2
                    s = p.k % SLOTS
                    pe.wait_ge(lo_ready, (p + 1).v)
                    bank_wait(b, j + g0)
                    for k in range(NC):
                        if ready:
                            pe.wait_ge(ready[0], ready[1] + k + 1)
                        c = slice(k * P, k * P + P)
                        last = three(psum[:, b, :], wh[:, s, c], wl[:, s, c], bh[bo][:, k, :], bl[bo][:, k, :],
                                     k == 0, k == NC - 1)
                    last.then_inc(panel_done, 1)
                turns(pe, n, step)
                w.p += n
                w.g += n

            def token_major(n, bo):
                p0, g0 = w.p, w.g

                def step(j):
                    p, b = j + p0, (g0 + j.k) % 2
                    s = p.k % SLOTS
                    pe.wait_ge(lo_ready, (p + 1).v)
                    bank_wait(b, j + g0)
                    for tb in range(NB):
                        r = slice(tb * P, tb * P + P)
                        for k in range(NC):
                            c = slice(k * P, k * P + P)
                            last = three(psum[:, b, r], bh[bo][:, k, r], bl[bo][:, k, r], wh[:, s, c], wl[:, s, c],
                                         k == 0, k == NC - 1)
                    last.then_inc(panel_done, 1)
                turns(pe, n, step)
                w.p += n
                w.g += n

            def short(tiles, hi, lo, n_k):
                s = w.p % SLOTS
                pe.wait_ge(lo_ready, w.p + 1)
                for t in range(tiles):
                    b = w.g % 2
                    bank_wait(b, Idx(0, w.g))
                    for k in range(n_k):
                        c = slice((t * n_k + k) * P, (t * n_k + k + 1) * P)
                        last = three(psum[:, b, :], wh[:, s, c], wl[:, s, c], hi[:, k, :], lo[:, k, :], k == 0, k == n_k - 1)
                    last.then_inc(mid_done if t < tiles - 1 else panel_done, 1)
                    w.g += 1
                w.mid += tiles - 1
                w.p += 1

            def norm_mean():
                pe.wait_ge(s1_ready, w.mean + 1)
                w.mean += 1
                nc.tensor.matmul(psum[:, 2, :], ones[:, :], s1c, start=True, stop=True).then_inc(mu_done, 1)

            def norm(mean):
                if mean:
                    norm_mean()
                for c in range(NC):
                    pe.wait_ge(sq_ready, w.nsq + c + 1)
                    nc.tensor.matmul(psum[:, 3, :], ones[:, :], sq[:, c % 2, :], start=(c == 0), stop=(c == NC - 1)).then_inc(sq_used, 1)
                w.nsq += NC
                w.norm += 1

            def attention(kind, units):
                h0, g0, q0, v0 = w.h, w.g, w.qs, w.vs

                def scores(u, e):
                    n = u * 2 + (h0 + e)
                    if e == 0:
                        pe.wait_ge(qk_staged, u + (q0 + 1))
                    for i in range(NB):
                        _, width, kb = span(kind, i)
                        out = psum[:, 4 + i, 0:width]
                        if not isinstance(n, int) or n >= 1:
                            pe.wait_ge(exp_done, n * 4 + (i - 3))
                        q_c = slice(i * P, i * P + P)
                        k_c = slice(kb * P, kb * P + width)
                        if kind == "mla":
                            q_, k_ = qs[0:96, e * T + i * P:e * T + i * P + P], ks[0:96, e * T:e * T + width]
                        elif kind == "swa":
                            q_, k_ = qs[64 * e:64 * e + 64, q_c], ka[64 * e:64 * e + 64, 0, k_c]
                        else:
                            q_, k_ = qs[64 * e:64 * e + 64, q_c], ks[64 * e:64 * e + 64, k_c]
                        nc.tensor.matmul(out, q_, k_, start=True, stop=False)
                        if kind == "swa":
                            k = u * 1 + 4 * e
                            lo_c = 2 * P - width
                            k = slice(k, k + 1) if isinstance(k, int) else bass.ds(k, 1)
                            last = nc.tensor.matmul(out, ident[:, :], bias[:, k, lo_c:2 * P].rearrange("p a b -> p (a b)"),
                                                    start=False, stop=True)
                        else:
                            if kind == "fox":
                                nc.tensor.matmul(out, fq[64 * e:64 * e + 48, q_c], fk[64 * e:64 * e + 48, 0:width], start=False, stop=False)
                            last = nc.tensor.matmul(out[:, width - P:width], ident[:, :], mask[:, :], start=False, stop=True)
                        last.then_inc(s_ready, 1)

                def turn(u, e, j):
                    n = u * 2 + (h0 + e)
                    if j == 0:
                        pe.wait_ge(p_ready, n * 4 + 4)
                    if not isinstance(n, int) or n * 4 + j >= 2:
                        pe.wait_ge(pt_copied, n * 4 + (j - 1))
                    blocks = pt_blocks(kind, j)
                    for a, i in enumerate(blocks):
                        col, _, kb = span(kind, i)
                        c = col + (j - kb) * P
                        last = nc.tensor.transpose(psum[:, 2 + j % 2, a * P:a * P + P], pa[:, e, c:c + P], ident[:, :])
                    last.then_inc(pt_ready, 1)

                def values(u, e):
                    n = u * 2 + (h0 + e)
                    b = (g0 + e) % 2
                    g = u + (g0 + e) // 2
                    r = slice(64 * e, 64 * e + 64)
                    if e == 0 and kind != "swa":
                        pe.wait_ge(v_staged, u + (v0 + 1))
                    pe.wait_ge(bank_free[b], g)
                    turn(u, e, 0)
                    turn(u, e, 1)
                    if kind != "swa":
                        for j in range(NB):
                            pe.wait_ge(pt_copied, n * 4 + (j + 1))
                            o = pts_at(kind, j)
                            last = nc.tensor.matmul(psum[r, b, j * P:T], vs[:, j, r], w4[:, o:o + T - j * P],
                                                    start=(j == 0), stop=(j == NB - 1))
                            if j + 2 < NB:
                                turn(u, e, j + 2)
                    else:
                        for i in range(NB):
                            pe.wait_ge(pt_copied, n * 4 + (i + 1))
                            js = [j for j in (i - 1, i) if j >= 0]
                            for j in js:
                                o = pts_at(kind, j) + (i - j) * P
                                last = nc.tensor.matmul(psum[r, b, i * P:i * P + P], vs[:, j, r], w4[:, o:o + P],
                                                        start=(j == js[0]), stop=(j == js[-1]))
                            if i + 2 < NB:
                                turn(u, e, i + 2)
                    last.then_inc(o_ready, 1)

                def body(u):
                    scores(u, 1)
                    values(u, 0)
                    scores(u + 1, 0)
                    values(u, 1)
                scores(0, 0)
                if units > 2:
                    with pe.Fori(0, units - 1) as u:
                        body(u)
                else:
                    body(0)
                scores(units - 1, 1)
                values(units - 1, 0)
                values(units - 1, 1)
                w.h += 2 * units
                w.g += 2 * units
                w.qs += units
                w.vs += units * (kind != "swa")
                pe.wait_ge(bank_free[0], (w.g + 1) // 2)
                pe.wait_ge(bank_free[1], w.g // 2)

            w.qs = w.vs = 0
            pe.wait_ge(const_set, 1)
            pe.wait_ge(par_in, 48)
            panels(6, 1, ready=(opnd_dve, 0))
            w.od += NC
            for c in range(5):
                pe.wait_ge(lat_sq, c + 1)
                nc.tensor.matmul(psum[:, 2 if c < 2 else 3, :], ones[:, :], sq[:, c % 2, :], start=(c in (0, 2)),
                                 stop=(c in (1, 4))).then_inc(lat_ss, 1)
            pe.wait_ge(lat_l, 5)
            for grp in range(GROUPS):
                short(2, lath[:, 0:2, :], latl[:, 0:2, :], 2)
                s = w.p % SLOTS
                pe.wait_ge(lo_ready, w.p + 1)
                for t in range(2):
                    b = w.g % 2
                    bank_wait(b, Idx(0, w.g))
                    for a in range(2):
                        r = slice((2 * t + a) * P, (2 * t + a + 1) * P)
                        for k in range(2):
                            c = slice(k * 2 * P, (k + 1) * 2 * P)
                            last = three(psum[:, b, a * 2 * P:(a + 1) * 2 * P], lath[:, k, r], latl[:, k, r], wh[:, s, c], wl[:, s, c],
                                         k == 0, k == 1)
                    last.then_inc(panel_done if t else mid_done, 1)
                    w.g += 1
                w.mid += 1
                w.p += 1
                short(2, lath[:, 2:5, :], latl[:, 2:5, :], 3)
                short(2, lath[:, 2:5, :], latl[:, 2:5, :], 3)
                attention("mla", 2)
            pe.wait_ge(bias_in, 64)
            nc.tensor.matmul(psum[0:8, 3, 0:SWA_F], relb[:, :], oneh[:, :], start=True, stop=True).then_inc(brow_mm, 1)
            panels(1, 1)
            token_major(1, 1)
            panels(4, 1)
            pe.wait_ge(bias_in, 80)
            attention("swa", 4)
            panels(NC, 0)

            def feed_forward_and_gate(layer):
                norm(True)
                for part_name in MLP:
                    q = int(part_name[1])
                    if part_name[0] == "U":
                        panels(NC, 0, ready=(opnd_pool, w.op) if q == 0 else None)
                        if q == 0:
                            w.op += NC
                        w.ud = w.od = w.od + NC
                        if q == 0:
                            w.d0 = w.od - NC
                    else:
                        pe.wait_ge(opnd_dve, w.d0 + NC * (q + 1))
                        panels(NC, 1 + q % 2)
                norm(True)
                pe.wait_ge(pl_ready, layer + 1)
                short(4, ph, pl, 2)
                short(4, ph, pl, 2)
                panels(NC, 0, ready=(opnd_pool, w.op))
                w.op += NC
                w.od += NC
            feed_forward_and_gate(0)
            if upto != "l0":
                panels(1, 1, ready=(opnd_dve, w.od - NC))
                for grp in range(GROUPS):
                    panels(8, 1)
                    token_major(4, 1)
                    attention("fox", 4)
                panels(NC, 0)
                feed_forward_and_gate(1)

            if upto not in ("l0", "l1"):
                st = Steps(pe, pair_pe, post_pe, half_pe)
                norm(False)
                panels(4, 0, ready=(opnd_pool, w.op))
                w.op += NC
                pe.wait_ge(wk_in, 32)
                pe.wait_ge(lora_l, 2)

                def pair(c):
                    p0, g0 = w.p, w.g

                    def tile_bank(i):
                        b = (g0 + i) % 2
                        pe.wait_ge(bank_free[b], c * 3 + (g0 + i) // 2)
                        return b

                    def dense_part(i, b, s, ks):
                        for k in ks:
                            cols = slice(k * P, k * P + P)
                            last = three(psum[:, b, :], wh[:, s, cols], wl[:, s, cols], bh[0][:, k, :], bl[0][:, k, :],
                                         k == 0, k == NC - 1)
                        return last
                    s = p0 % SLOTS
                    pe.wait_ge(lo_ready, Idx(c, p0 + 1).v)
                    for i, (r, cols, a, done) in enumerate(((slice(0, 64), 0, 0, mid_done), (slice(64, 128), 0, 0, mid_done),
                                                            (slice(0, 128), P, 1, panel_done))):
                        b = tile_bank(i)
                        w_c = slice(cols, cols + P)
                        three(psum[:, b, :], wh[r, s, w_c], wl[r, s, w_c], lh[a][r, :], ll[a][r, :], True, True).then_inc(done, 1)
                    later = not isinstance(c, int) or c > 0
                    if later:
                        mean(c + -1)
                    b, s = tile_bank(3), (p0 + 1) % SLOTS
                    pe.wait_ge(lo_ready, Idx(c, p0 + 2).v)
                    dense_part(3, b, s, range(4))
                    if later:
                        variance(c + -1)
                    dense_part(3, b, s, range(4, NC)).then_inc(panel_done, 1)
                    b, s = tile_bank(4), (p0 + 2) % SLOTS
                    pe.wait_ge(lo_ready, Idx(c, p0 + 3).v)
                    dense_part(4, b, s, range(NC)).then_inc(panel_done, 1)
                    st.wait(pair_act, c, "square")
                    st.did(pair_pe, "kk", nc.tensor.matmul(psum[:, 2, :], o64[:, :], sq[:, 0, :], start=True, stop=True))
                    b, s = tile_bank(5), (p0 + 3) % SLOTS
                    pe.wait_ge(lo_ready, Idx(c, p0 + 4).v)
                    dense_part(5, b, s, range(NC)).then_inc(panel_done, 1)
                    st.wait(pair_dve, c, "prod")
                    st.did(pair_pe, "bonus", nc.tensor.matmul(psum[:, 7, :], o64[:, :], sq[:, 1, :], start=True, stop=True))
                    for f in range(2):
                        half(c * 2 + f, (pair_dve, at(pair_dve, c, "ready")) if f == 0 else None)

                def mean(c):
                    st.wait(half_act, c * 2 + 1, "o")
                    st.wait(half_dve, c * 2 + 1, "s4")
                    st.did(post_pe, "mean", nc.tensor.matmul(psum[:, 2, :], o64[:, :], zr, start=True, stop=True))

                def variance(c):
                    st.wait(post_act, c, "osquare")
                    st.did(post_pe, "var", nc.tensor.matmul(psum[:, 3, :], o64[:, :], sq[:, 0, :], start=True, stop=True))

                def half(n, ready):
                    def waits(needs):
                        for sema in (half_act, half_dve, half_pool):
                            of = [EVENTS[sema].index(what) + 1 for s, what in needs if s is sema]
                            if of:
                                pe.wait_ge(sema, before(sema, n) + max(of))

                    def product(name, *terms, needs=(), turn=False):
                        for g in range(2):
                            i = PRODUCTS.index(f"{name}.{g}")
                            if i == 4:
                                pe.wait_ge(half_act, before(half_act, n))
                                if ready:
                                    pe.wait_ge(*ready)
                            waits([(s, what + f".{g}" if what + f".{g}" in EVENTS[s] else what) for s, what in needs]
                                  + ([MOVED[PRODUCTS[i - 6]]] if i >= 6 else []))
                            for j in range(2):
                                ch = 2 * g + j
                                for i, (a, b) in enumerate(terms):
                                    out = bank(f"{name}.{g}")[:, j, :]
                                    if turn:
                                        last = nc.tensor.transpose(out, a[:, ch, :], b)
                                    else:
                                        last = nc.tensor.matmul(out, a[:, ch, :], b[:, ch, :], start=(i == 0), stop=(i == len(terms) - 1))
                            st.did(half_pe, f"{name}.{g}", last)
                    by_act, by_dve, by_pool = (lambda what: (half_act, what)), (lambda what: (half_dve, what)), (lambda what: (half_pool, what))

                    product("l", (m_a, m_b), needs=[by_dve("b")])
                    product("lt", (m_b, m_a))
                    product("rb", (m_b, m_r), needs=[by_dve("r")])
                    product("ak", (m_k, m_a))
                    product("rk", (m_k, m_r))
                    product("at", (m_a, ident[:, :]), turn=True)
                    product("bt", (m_bd, ident[:, :]), needs=[by_pool("bd")], turn=True)
                    product("kt", (m_kd, ident[:, :]), needs=[by_pool("kd")], turn=True)
                    product("vt", (m_v, ident[:, :]), needs=[by_act("v")], turn=True)
                    last_t, last_x = "t1", "x1"
                    for b in LEVELS:
                        product(f"z{b}", (m_off, m_t), needs=[by_pool(f"off{b}"), by_dve(last_t)])
                        if b == LEVELS[0]:
                            product("w", (m_ak, m_vt), needs=[by_dve("ak"), by_act("vt")])
                        if b != LEVELS[-1]:
                            product(f"t{b}", (m_x, m_z), needs=[by_act(f"z{b}"), by_dve(last_x)])
                        product(f"x{b}", (m_z, m_x), needs=[by_act(f"z{b}"), by_dve(last_x)])
                        last_t, last_x = f"t{b}", f"x{b}"
                    product("ta", (m_x, m_at), needs=[by_dve(last_x), by_act("at")])
                    product("tw", (m_x, m_w), needs=[by_act("w")])
                    product("mm", (m_ta, m_bt), needs=[by_act("ta")])
                    product("p", (m_ta, m_rb), needs=[by_dve("rb")])
                    product("n", (m_bt, m_tw), (m_kt, m_vt), needs=[by_dve("tw"), by_act("kt")])
                    for ch in range(4):
                        waits([by_dve(f"s{ch}")] + ([MOVED["n.0"]] if ch == 3 else []))
                        st.did(half_pe, f"c{ch}", nc.tensor.matmul(bank(f"c{ch}")[:, 0, :], m_mm[:, ch, :], m_s[:, ch, :],
                                                                  start=True, stop=True))
                        for i, (a, b) in enumerate(((m_tw, m_rb), (m_vt, m_rk), (m_s, m_p))):
                            last = nc.tensor.matmul(o_bank[:, ch, :], a[:, ch, :], b[:, ch, :], start=(i == 0), stop=(i == 2))
                        st.did(half_pe, f"o{ch}", last)

                pair(0)
                with pe.Fori(1, NC) as c:
                    pair(c)
                mean(NC - 1)
                variance(NC - 1)
                w.p += 4 * NC
                w.g += 6 * NC
                w.mid += 2 * NC
                w.od += NC

                p0, g0 = w.p, w.g

                def branches(j):
                    p, b = j + p0, (g0 + j.k) % 2
                    s = p.k % SLOTS
                    o = 1 if j.k == 3 else 0
                    pe.wait_ge(lo_ready, (p + 1).v)
                    bank_wait(b, j + g0)
                    if o:
                        pe.wait_ge(opnd_dve, w.od)
                    for k in range(NC):
                        c = slice(k * P, k * P + P)
                        last = three(psum[:, b, :], wh[:, s, c], wl[:, s, c], bh[o][:, k, :], bl[o][:, k, :],
                                     k == 0, k == NC - 1)
                    last.then_inc(panel_done, 1)
                turns(pe, 4 * NC, branches)
                w.p += 4 * NC
                w.g += 4 * NC
                panels(2, 0)
                norm_mean()
                panels(2, 0)
                norm(False)
                panels(NC - 4, 0)
                panels(NC, 1, ready=(opnd_pool, w.op))
                w.op += NC
                panels(NC, 3, ready=(opnd_dve, w.od))
                w.od += NC
                norm(False)
                for part_name in MLP:
                    q = int(part_name[1])
                    if part_name[0] == "U":
                        panels(NC, 0, ready=(opnd_pool, w.op) if q == 0 else None)
                        if q == 0:
                            w.d0 = w.od
                    else:
                        pe.wait_ge(opnd_dve, w.d0 + NC * (q + 1))
                        panels(NC, 1 + q % 2)
                norm(False)


def dense(m):
    k, n = m.shape
    return m.reshape(k // P, P, n // P, P).transpose(2, 1, 0, 3).reshape(n // P, P, k // P * P)


def filled(a):
    while a.shape[1] < D:
        a = np.concatenate([a, a[:, :D - a.shape[1]]], axis=1)
    return a


def tiles(m):
    return dense(m).transpose(1, 0, 2).reshape(P, -1)


def weight_stream(I, upto=None):
    out = []
    w = I["ev_w_in"][0]
    rope = w[:, 640:672]
    swapped = np.concatenate([rope[:, 16:], rope[:, :16]], axis=1)
    out += [*dense(w[:, 384:640]), *dense(np.concatenate([rope, rope, rope, swapped], axis=1)), *dense(w[:, :384])]
    uq = I["ev_w_uq"][0].reshape(384, 8, 96)
    uq = np.concatenate([uq, uq[:, :, 80:96], uq[:, :, 64:80]], axis=2)
    ukv = I["ev_w_ukv"][0].reshape(256, 8, 128)
    for g in range(2):
        hs = slice(4 * g, 4 * g + 4)
        out.append(filled(tiles(ukv[:, hs, :64].reshape(256, 256))))
        out.append(filled(ukv[:, hs, 64:].reshape(2, P, 256).transpose(1, 0, 2).reshape(P, 512)))
        for h in (4 * g, 4 * g + 2):
            out.append(filled(tiles(uq[:, h:h + 2].reshape(384, 256))))
    out += [*dense(w[:, 1184:1440])]
    pair = np.array([(u + 4 * e) * 64 + d for u in range(4) for e in range(2) for d in range(64)])
    out += [*dense(w[:, 672:1184][:, pair])]
    out += [*dense(I["ev_w_out"][0][np.concatenate([np.arange(512), 512 + pair])])]

    def feed_forward(up, down):
        q = D
        for name in ("U0", "U1", "D0", "U2", "D1", "U3", "D2", "D3"):
            c = slice(int(name[1]) * q, int(name[1]) * q + q)
            out.extend(dense(up[:, c]) if name[0] == "U" else dense(down[c]))

    def ff_and_gate(l):
        feed_forward(I["w_up"][l], I["w_down"][l])
        pw = I["ple_w_proj"][l]
        out.extend([tiles(pw[:, :512]), tiles(pw[:, 512:])])
        out.extend(dense(I["ple_w_gate"][l]))
    ff_and_gate(0)
    if upto != "l0":
        w = I["od_w_in"][0]
        out += [*dense(np.tile(w[:, 3072:], (1, 8)))]
        for g in range(2):
            for a in range(3):
                out += [*dense(w[:, a * D + 512 * g:a * D + 512 * g + 512])]
        out += [*dense(I["od_w_out"][0])]
        ff_and_gate(1)
    first = len(out)
    if not upto:
        lora = [*dense(np.concatenate([I["decay_w1_2"][0], I["aaa_a1_2"][0]], axis=1)), *dense(I["gate_g1_2"][0])]
        out += lora + lora
        w = I["w_in_2"][0]
        r, k, v, glu_a, glu_b, gate0, gate1 = (dense(w[:, i * D:(i + 1) * D]) for i in range(7))
        second = np.concatenate([I["decay_w2_2"][0], I["aaa_a2_2"][0]], axis=0)
        for c in range(NC):
            cols = slice(c * P, c * P + P)
            out += [filled(np.concatenate([second[:, cols], I["gate_g2_2"][0][:, cols]], axis=1)), k[c], r[c], v[c]]

        def taking_turns(*kinds):
            return [m for one_of_each in zip(*kinds) for m in one_of_each]
        out += taking_turns(glu_b, glu_a, gate0, dense(I["w_rwkv_proj_2"][0]))
        out += [*gate1, *dense(I["w_conv_proj_2"][0])]
        out += [*dense(I["w_out_2"][0])]
        feed_forward(I["w_ff1_2"][0], I["w_ff2_2"][0])
    return np.stack(out), first


def layout(I, upto=None):
    stream, third_layer = weight_stream(I, upto)
    A = {"w": stream}

    def fm(a):
        return np.ascontiguousarray(a.T.reshape(-1, P, a.shape[0]).transpose(1, 0, 2))
    A["xT"] = fm(I["x"][0])
    A["pT"] = np.concatenate([fm(I["p"][l, 0]) for l in range(2)], axis=1)
    src = {"q_norm": "ev_q_norm", "kv_norm": "ev_kv_norm", "ln1_g": "ln1_g", "ln1_b": "ln1_b", "ln2_g": "ln2_g",
           "ln2_b": "ln2_b", "ple_b": "ple_b_gate", "norm_mix": "norm_mix_g_2", "b_gate": "b_gate_2",
           "mu_rkv": "mu_rkv_2", "mu_lora": "mu_lora_2", "w0": "decay_w0_2", "a0": "aaa_a0_2", "k_k": "k_k_2",
           "k_a": "k_a_2", "r_k": "r_k_2", "lnx_g": "ln_x_g_2", "lnx_b": "ln_x_b_2", "conv_b": "conv_b_2",
           "cln_g": "conv_ln_g_2", "cln_b": "conv_ln_b_2", "norm_ff": "norm_ff_g_2", "norm_fin": "norm_final_g_2"}
    A["par"] = np.concatenate([I[src[n]].reshape(-1, P).T for n in PAR], axis=1)
    A["ident"] = np.eye(P, dtype=np.float32)
    A["mask"] = np.where(np.arange(P)[None] > np.arange(P)[:, None], NEG, 0).astype(np.float32)
    inv = 1.0 / (10000.0 ** (np.arange(0, 32, 2, dtype=np.float32) / np.float32(32)))
    ang = (np.arange(T, dtype=np.float32)[:, None] * inv[None].astype(np.float32)).T
    c, s_ = np.cos(ang), np.sin(ang)
    A["rope"] = np.concatenate([np.ones((64, T)), c, c, -s_, s_]).astype(np.float32)
    dist = 255 - np.arange(SWA_F)
    ok = (dist >= 0) & (dist < P)
    d = np.maximum(dist, 1).astype(np.float32)
    large = 16 + (np.log(d / 16) / np.float32(np.log(8.0)) * 16).astype(np.int32)
    bucket = np.where(dist < 16, np.maximum(dist, 0), np.minimum(large, 31))
    A["oneh"] = ((np.arange(32)[:, None] == bucket[None]) & ok[None]).astype(np.float32)
    A["negm"] = np.repeat(np.where(ok, 0, NEG)[None], 8, axis=0).astype(np.float32)
    A["relb"] = I["rel_bias"]
    A["sink"] = I["ev_sinks"][0]
    row, u = np.arange(P)[:, None], np.arange(8)[None]
    e, r = row // 64, row % 64
    A["fsel"] = np.concatenate([r == 32 + 2 * u + e, -1.0 * (r == 2 * u + e), r < 16, (r >= 32) & (r < 48)],
                               axis=1).astype(np.float32)
    A["bf"] = np.tile(I["od_b_f"][0], 8).reshape(P, 1)
    i, j = np.arange(P)[:, None], np.arange(P)[None]
    head = i // 64 == j // 64
    wm = [head & (i < j), head & (i <= j), (i // 2 == j // 2) & (i > j), (i // 2 == j // 2) & (i < j)]
    wm += [(i // (2 * b) == j // (2 * b)) & (i // b < j // b) for b in (2, 4, 8, 16, 32)]
    A["wm"] = np.stack(wm, axis=1).astype(np.float32)
    A["o64"] = (head / 64.0).astype(np.float32)
    A["cw"] = I["conv_w_2"][0].T.reshape(NC, P, 31).transpose(1, 0, 2)
    return {n: np.ascontiguousarray(a) for n, a in A.items()}, third_layer


def kernel(**inputs):
    import concourse.bacc as bacc
    from concourse.bass_utils import run_bass_kernel_spmd

    arrays, third_layer = layout({n: np.asarray(a) for n, a in inputs.items()})
    nc = bacc.Bacc("TRN2", target_bir_lowering=False, num_devices=1)
    A = {n: nc.dram_tensor(n, a.shape, mybir.dt.from_np(a.dtype), kind="ExternalInput").ap() for n, a in arrays.items()}
    A["out"] = nc.dram_tensor("out", (P, NC, T), F32, kind="ExternalOutput").ap()
    build(nc, A, arrays["w"].shape[0], third_layer)
    run = run_bass_kernel_spmd(nc, [arrays], core_ids=[0])
    return run.results[0]["out"].transpose(2, 1, 0).reshape(1, T, D)
```

```python
from contextlib import ExitStack

import numpy as np
import concourse.bass as bass
from concourse import mybir

F32 = mybir.dt.float32
F32R = mybir.dt.float32r
ALU = mybir.AluOpType
ACT = mybir.ActivationFunctionType
AX = mybir.AxisListType.X

P = 128
T = 512
D = 1024
NC = D // P
NB = T // P
SLOTS = 4
ALPHA = 4 ** 0.25
LN_EPS, RMS1_EPS, RMS_EPS, GN_EPS = 1e-5, 1e-5, 1e-6, 64e-5
NEG = -1e30
MLA_SCALE = 96 ** -0.5
HEAD_SCALE = 64 ** -0.5


class Idx:

    def __init__(self, turn, k):
        self.turn, self.k = turn, k

    def __add__(self, n):
        return Idx(self.turn, self.k + n)

    @property
    def v(self):
        return self.turn * 4 + self.k

    def over4(self):
        return self.turn + self.k // 4

    def over2(self):
        return self.turn * 2 + self.k // 2


class Walk:

    def __init__(self):
        self.p = 0
        self.g = 0
        self.mid = 0
        self.od = 0
        self.op = 0
        self.h = 0
        self.norm = 0
        self.nsq = 0
        self.u = 0
        self.ple = 0
        self.nd = 0
        self.mean = 0


def turns(eng, n, body, peel_last=False):
    full = n // 4
    if peel_last and n % 4 == 0:
        full -= 1
    if full >= 2:
        with eng.Fori(0, full) as t:
            for k in range(4):
                body(Idx(t, k))
    else:
        full = 0
    for j in range(4 * full, n):
        body(Idx(0, j))


PAR = {}


def _par(name, n):
    PAR[name] = (sum(x[1] for x in PAR.values()), n)


for _n, _c in (("q_norm", 3), ("kv_norm", 2), ("ln1_g", 16), ("ln1_b", 16), ("ln2_g", 16), ("ln2_b", 16),
               ("ple_b", 16), ("norm_mix", 8), ("b_gate", 16), ("mu_rkv", 24), ("mu_lora", 24), ("w0", 8),
               ("a0", 8), ("k_k", 8), ("k_a", 8), ("r_k", 8), ("lnx_g", 8), ("lnx_b", 8), ("conv_b", 8),
               ("cln_g", 8), ("cln_b", 8), ("norm_ff", 8), ("norm_fin", 8)):
    _par(_n, _c)
NPAR = sum(x[1] for x in PAR.values())
SWA_F = 384
PAIR_LINKS = 23
CHUNK_LINKS = 33


class Chain:

    def __init__(self, eng, sem):
        self.eng, self.sem, self.n, self.turn, self.per = eng, sem, 0, 0, 0

    def link(self, ins):
        self.n += 1
        ins.then_inc(self.sem, 1)
        self.eng.wait_ge(self.sem, self.turn * self.per + self.n)

    def lagged(self, ins):
        self.n += 1
        ins.then_inc(self.sem, 1)
        self.eng.wait_ge(self.sem, self.turn * self.per + self.n - 1)

    def turns(self, n, body, links):
        seen = []

        def counted(j):
            self.turn = j.turn
            self.per = 4 * links if not isinstance(j.turn, int) else 0
            at = self.n
            body(j)
            seen.append(self.n - at)
            assert seen[-1] == links, (seen[-1], links)

        full = n // 4
        turns(self.eng, n, counted)
        if full >= 2:
            self.n += 4 * links * (full - 1)
        self.turn = self.per = 0


def build(nc, A, n_panels, b2_start):
    ctx = ExitStack()
    with ctx:
        def sb(name, shape, dt=F32, at=ctx):
            return at.enter_context(nc.sbuf_tensor("sb_" + name, shape, dt))

        def sem(name):
            return ctx.enter_context(nc.semaphore(name))

        raw = sb("raw", [P, SLOTS, D])
        wh = sb("wh", [P, SLOTS, D], F32R)
        wl = sb("wl", [P, SLOTS, D], F32R)
        x = sb("x", [P, NC, T])
        bh = [sb(f"bh{i}", [P, NC, T], F32R) for i in range(2)]
        bl = [sb(f"bl{i}", [P, NC, T], F32R) for i in range(2)]
        par = sb("par", [P, NPAR])
        ident = sb("ident", [P, P])
        ones = sb("ones", [P, P])
        mask = sb("mask", [P, P])
        t2 = sb("t2", [P, 2, T])
        sq = sb("sq", [P, 2, T])
        eps = sb("eps", [P, 4])
        w4 = sb("w4", [P, 4 * T])
        s1, s1c, sd, rs = (w4[:, i * T:(i + 1) * T] for i in range(4))
        psum = ctx.enter_context(nc.psum_tensor("banks", [P, 8, T], F32))

        def pcol(name, c=0):
            o = PAR[name][0]
            if isinstance(c, Idx):
                c = c.v
            return par[:, o + c:o + c + 1] if isinstance(c, int) else par[:, bass.ds(c + o, 1)]

        with ExitStack() as part:
            bh.append(sb("bh2", [P, NC, T], F32R, part))
            bl.append(sb("bl2", [P, NC, T], F32R, part))
            pj = sb("pj", [P, NC, T], F32, part)
            praw = pj[:, 6:8, :]
            ph = sb("ph", [P, 2, T], F32R, part)
            pl = sb("pl", [P, 2, T], F32R, part)
        with ExitStack() as part:
            qa = sb("qa", [P, 4, T], F32, part)
            ka = sb("ka", [P, 4, T], F32, part)
            va = sb("va", [P, NB, T], F32, part)
            qs = sb("qs", [P, 2 * T], F32, part)
            ks = sb("ks", [P, 2 * T], F32, part)
            vs = sb("vs", [P, NB, P], F32, part)
            pa = sb("pa", [P, 2, 1280], F32, part)
            lat = pa[:, :, :].rearrange("p a b -> p (a b)").rearrange("p (c t) -> p c t", t=T)
            nm = sb("nm", [P, 2, 4], F32, part)
            sm = sb("sm", [P, 2, 4], F32, part)
            rc = sb("rc", [P, 2, 4], F32, part)
            with ExitStack() as mla:
                lath, latl = bh[0][:, 3:8, :], bl[0][:, 3:8, :]
                rope = sb("rope", [P, T], F32, mla)
                rt = sb("rt", [P, 2, T], F32, mla)
            with ExitStack() as swa:
                bias = sb("bias", [P, 8, 2 * P], F32, swa)
                sink = sb("sink", [P, 8], F32, swa)
                nsink = sb("nsink", [P, 8], F32, swa)
                snk = sb("snk", [P, 3, 4], F32, swa)
                relb = sb("relb", [32, 8], F32, swa)
                oneh = sb("oneh", [32, SWA_F], F32, swa)
                negm = sb("negm", [8, SWA_F], F32, swa)
                brow = sb("brow", [8, SWA_F], F32, swa)
            with ExitStack() as fox:
                fsel = sb("fsel", [P, 19], F32, fox)
                fc = sb("fc", [P, T], F32, fox)
                ft = lat[:, 0:3, :]
                fone = t2[:, 0, :]
        with ExitStack() as part:
            z = [sb(f"z{n}", [P, T + 1], F32, part) for n in "rkv"]
            zr, zk, zv = (a[:, 1:T + 1] for a in z)
            gt = sb("gt", [P, T], F32, part)
            ep = sb("ep", [P, 8, 65], F32, part)
            m_a, m_b, m_k, m_r, m_v, m_bd, m_kd, m_at, m_bt, m_kt, m_vt, m_lt, m_rb, m_ak, m_rk, m_off = (
                sb("m_" + n, [P, 4, P], F32, part) for n in
                "a b k r v bd kd at bt kt vt lt rb ak rk off".split())
            m_t = sb("m_t", [P, 4, P], F32, part)
            m_w, m_ta, m_tw, m_p, m_x, m_z, m_mm, m_n = m_a, m_b, m_k, m_r, m_bd, m_kd, m_v, m_ak
            m_s = sb("m_s", [P, 5, P], F32, part)
            wm = sb("wm", [P, 9, P], F32, part)
            o64 = mask
            half_b = sb("half_b", [P, 16], F32, part)
            going = sb("going", [P, T], F32, part)
            lh = [sb(f"lh{n}", [P, T], F32R, part) for n in "ag"]
            ll = [sb(f"ll{n}", [P, T], F32R, part) for n in "ag"]
        cu, em, rn, kkn = s1, s1c, sd, rs
        la, lw = t2[:, 0, :], t2[:, 1, :]
        with ExitStack() as part:
            mg = sb("mg", [P, NC, T], F32, part)
            with ExitStack() as conv:
                y = sb("y", [P, NC, T], F32, conv)
                ub = sb("ub", [P, T + 30], F32, conv)
                cw = sb("cw", [P, NC, 31], F32, conv)
                sg = sb("sg", [P, NC, T], F32, conv)
            mh = sb("mh", [P, NC, T], F32R, part)
            ml = sb("ml", [P, NC, T], F32R, part)
        bh.append(mh)
        bl.append(ml)
        scratch = nc.dram_tensor("bias_rows", [8, P, SWA_F], F32, kind="Internal")

        panel_in = [sem(f"panel_in{i}") for i in range(SLOTS)]
        hi_ready, lo_ready = sem("hi_ready"), sem("lo_ready")
        panel_done, mid_done = sem("panel_done"), sem("mid_done")
        bank_free = [sem("bank0_free"), sem("bank1_free")]
        opnd_dve, opnd_pool = sem("opnd_dve"), sem("opnd_pool")
        dve_step, act_step, pool_step = sem("dve_step"), sem("act_step"), sem("pool_step")
        par_in = sem("par_in")
        x_in = [sem(f"x_in{i}") for i in range(4)]
        xh0 = sem("x_hi_ready")
        u_free = sem("u_free")
        s1_ready, mu_done, d_ready, sq_ready, sq_used = (sem(n) for n in (
            "s1_ready", "mu_done", "d_ready", "sq_ready", "sq_used"))
        sd_ready, t_ready, nhi_ready = sem("sd_ready"), sem("t_ready"), sem("nhi_ready")
        pp_in, ph_ready, pl_ready, xn_ready, xnh_ready = (sem(n) for n in (
            "pp_in", "ph_ready", "pl_ready", "xn_ready", "xnh_ready"))
        s_ready, nm_ready, exp_done, rc_done, p_ready, pt_ready, pt_copied, o_ready, ohi_done = (sem(n) for n in (
            "s_ready", "nm_ready", "exp_done", "rc_done", "p_ready", "pt_ready", "pt_copied", "o_ready", "ohi_done"))
        qk_staged, v_staged, lat_sq, lat_ss, lat_sd, lat_t, lat_h, lat_l = (sem(n) for n in (
            "qk_staged", "v_staged", "lat_sq", "lat_ss", "lat_sd", "lat_t", "lat_h", "lat_l"))
        snk_ready, snk_done, brow_ps, brow_out, bias_in, fox_a, fox_b, const_set = (sem(n) for n in (
            "snk_ready", "snk_done", "brow_ps", "brow_out", "bias_in", "fox_a", "fox_b", "const_set"))
        brow_mm, fsel_in, qs_zero = sem("brow_mm"), sem("fsel_in"), sem("qs_zero")
        scaled, wk_in, wk_set, lora_h, lora_l, m_done, mrg_h, cw_in, yz, ysg = (sem(n) for n in (
            "scaled", "wk_in", "wk_set", "lora_h", "lora_l", "m_done", "mrg_h", "cw_in", "yz", "ysg"))
        lora_z, lora_t = sem("lora_z"), sem("lora_t")
        pair_pe, pair_act, pair_dve = sem("pair_pe"), sem("pair_act"), sem("pair_dve")
        post_pe, post_act, post_dve = sem("post_pe"), sem("post_act"), sem("post_dve")
        half_pe, half_act, half_dve, half_pool = sem("half_pe"), sem("half_act"), sem("half_dve"), sem("half_pool")
        stored = sem("stored")

        block = ctx.enter_context(nc.Block())
        n_pan = n_panels
        MLP = ("U0", "U1", "D0", "U2", "D1", "U3", "D2", "D3")

        def span(kind, i):
            if kind == "swa":
                return (0, P, 0) if i == 0 else (P + 2 * P * (i - 1), 2 * P, i - 1)
            return P * (i * (i + 1) // 2), P * (i + 1), 0

        @block.sync
        def _(sp):
            for s in range(SLOTS):
                sp.dma_start(raw[:, s, :], A["w"][s]).then_inc(panel_in[s], 16)
                sp.dma_start(x[:, 2 * s:2 * s + 2, :], A["xT"][:, 2 * s:2 * s + 2, :]).then_inc(x_in[s], 16)
                if s == 0:
                    sp.dma_start(par[:, :], A["par"]).then_inc(par_in, 16)
                    sp.dma_start(ident[:, :], A["ident"]).then_inc(par_in, 16)
                    sp.dma_start(mask[:, :], A["mask"]).then_inc(par_in, 16)

            def load(q):
                s = q.k % SLOTS
                sp.wait_ge(lo_ready, (q + -3).v)
                sp.dma_start(raw[:, s, :], A["w"][q.v]).then_inc(panel_in[s], 16)

            turns(sp, n_pan - SLOTS, lambda j: load(j + SLOTS))
            for c in range(0, NC, 2):
                sp.wait_ge(t_ready, 7 * NC + c + 2)
                sp.dma_start(A["out"][:, c:c + 2, :], x[:, c:c + 2, :]).then_inc(stored, 16)
            sp.wait_ge(stored, 16 * (NC // 2))

        LEVELS = (2, 4, 8, 16, 32)
        EARLY = ["l", "lt", "rb", "ak", "rk", "at", "bt", "kt", "vt", "z2", "w"]
        INVERSE = [f"{m}{b}" for b in LEVELS for m in "ztx" if m + str(b) not in ("z2", "t32")]
        LATE = ["ta", "tw", "mm", "p", "n"]

        def groups(names):
            return [f"{n}.{g}" for n in names for g in range(2)]
        PRODUCTS = groups(EARLY + INVERSE + LATE)
        EVENTS = {
            pair_pe: ["kk", "bonus"],
            pair_act: ["decay", "square", "root"],
            pair_dve: ["sums", "mixed", "kmax", "prod", "ready"],
            post_pe: ["mean", "var"],
            post_act: ["osquare", "oroot", "high"],
            post_dve: ["centred", "out"],
            half_act: ["v"] + groups(["at", "bt", "kt", "vt", "z2", "w"] + [f"z{b}" for b in LEVELS[1:]] + ["ta", "n"]) + ["o"],
            half_dve: ["a", "b", "k", "r"] + groups(["t1", "lt", "rb", "ak", "rk", "x1"]
                                                    + [f"{m}{b}" for b in LEVELS for m in "tx" if m + str(b) != "t32"]
                                                    + ["tw", "mm", "p"]) + ["s0", "s1", "s2", "s3", "s4"],
            half_pool: ["bd", "kd"] + groups([f"off{b}" for b in LEVELS]),
            half_pe: PRODUCTS + [f"{m}{i}" for i in range(4) for m in "co"],
        }
        BANK = {n: 2 + i % 6 for i, n in enumerate(PRODUCTS)}
        O_BANK = 2 + len(PRODUCTS) % 6
        BANK.update({f"c{i}": 2 + (len(PRODUCTS) + 1 + i) % 6 for i in range(4)})

        def bank(product):
            return psum[:, BANK[product], 0:2 * P].rearrange("p (a n) -> p a n", a=2)
        o_bank = psum[:, O_BANK, :].rearrange("p (a n) -> p a n", a=4)

        MOVED = {}
        for n in PRODUCTS:
            name, g = n.split(".")
            MOVED[n] = (half_act, n) if n in EVENTS[half_act] else (half_dve, "t1." + g if name == "l" else n)

        def each(m):
            return m.unsqueeze(1).broadcast_to([P, 2, P])

        def hcol(c, o):
            return half_b[:, bass.ds(c + o, 1)]

        def at(sema, n, what):
            names = EVENTS[sema]
            return n * len(names) + (names.index(what) + credit(sema))

        def credit(sema):
            return 2 if sema in (half_pe, half_act, half_dve, half_pool) else 1

        def before(sema, n):
            return n * len(EVENTS[sema]) + 1

        class Steps:

            def __init__(self, eng, *sems):
                self.eng, self.seen = eng, {s: [] for s in sems}

            def did(self, sema, what, ins):
                assert EVENTS[sema][len(self.seen[sema]) % len(EVENTS[sema])] == what, (what, self.seen[sema][-3:])
                self.seen[sema].append(what)
                ins.then_inc(sema, 1)

            def wait(self, sema, n, what):
                self.eng.wait_ge(sema, at(sema, n, what))

        B2 = b2_start
        GROUPS = 2

        @block.scalar
        def _(act):
            w = Walk()

            def split(q, forced=False):
                if isinstance(q.turn, int) and (q.v >= n_pan or (q.v == B2 + 2 and not forced)):
                    return
                s = q.k % SLOTS
                act.wait_ge(panel_in[s], q.over4() * 16 + 16)
                if q.k >= SLOTS:
                    act.wait_ge(panel_done, (q + -3).v)
                nc.scalar.copy(wh[:, s, :], raw[:, s, :]).then_inc(hi_ready, 1)

            def panels(n, body):
                p0, g0 = w.p, w.g

                def step(j):
                    split(j + (p0 + 3))
                    body(j, j + p0, (g0 + j.k) % 2)
                turns(act, n, step, w.p + n in (n_pan, B2))
                w.p += n
                w.g += n

            def up():
                u0 = w.u

                def body(j, p, b):
                    act.wait_ge(panel_done, (p + 1).v)
                    act.wait_ge(u_free, (j + (u0 + 1)).v)
                    nc.scalar.activation(sq[:, j.k % 2, :], psum[:, b, :], ACT.Relu).then_inc(bank_free[b], 1)
                panels(NC, body)
                w.u += NC

            def only_split(n):
                panels(n, lambda j, p, b: None)

            def squares(src, mean, chunks):
                for c in chunks:
                    n = w.nsq
                    if mean:
                        act.wait_ge(d_ready, w.nd + 1)
                        w.nd += 1
                    if n >= 2:
                        act.wait_ge(sq_used, n - 1)
                    nc.scalar.activation(sq[:, c % 2, :], src[:, c, :], ACT.Square).then_inc(sq_ready, 1)
                    w.nsq += 1

            def root(mean):
                act.wait_ge(sq_used, w.nsq)
                nc.scalar.activation(sd, psum[:, 3, :], ACT.Sqrt, bias=eps_col[mean]).then_inc(sd_ready, 1)
                w.norm += 1

            def norm(src, mean, after=(), bcol=None, bo=0, final=False):
                for sema, n in after:
                    act.wait_ge(sema, n)
                squares(src, mean, range(NC))
                root(mean)
                if final:
                    return
                for c in range(NC):
                    act.wait_ge(t_ready, NC * (w.norm - 1) + c + 1)
                    if mean:
                        nc.scalar.activation(bh[bo][:, c, :], src[:, c, :], ACT.Identity, bias=pcol(*bcol(c)))
                        nc.scalar.activation(src[:, c, :], src[:, c, :], ACT.Identity, bias=pcol(*bcol(c))).then_inc(nhi_ready, 1)
                    else:
                        nc.scalar.copy(bh[bo][:, c, :], t2[:, c % 2, :]).then_inc(nhi_ready, 1)

            def silu(c):
                act.wait_ge(t_ready, NC * (w.norm - 1) + c + 1)
                nc.scalar.activation(sq[:, c % 2, :], y[:, c, :], ACT.Sigmoid, bias=pcol("cln_b", c))
                nc.scalar.activation(y[:, c, :], y[:, c, :], ACT.Identity, bias=pcol("cln_b", c)).then_inc(ysg, 1)
                act.wait_ge(yz, c + 1)
                nc.scalar.copy(bh[1][:, c, :], y[:, c, :]).then_inc(nhi_ready, 1)

            def ple(layer):
                act.wait_ge(pp_in, 16 * (layer + 1))
                nc.scalar.copy(ph[:, :, :], praw).then_inc(ph_ready, 1)

                p0, g0 = w.p, w.g
                for q in range(2):
                    split(Idx(0, p0 + q + 3))
                    for i in range(4):
                        if i < 3:
                            act.wait_ge(mid_done, w.mid + 3 * q + i + 1)
                        else:
                            act.wait_ge(panel_done, p0 + q + 1)
                        b = (g0 + i) % 2
                        nc.scalar.copy(pj[:, 4 * q + i, :], psum[:, b, :]).then_inc(bank_free[b], 1)
                w.mid += 6
                w.p += 2
                w.g += 8
                x0 = NC * w.ple

                def body(j, p, b):
                    act.wait_ge(panel_done, (p + 1).v)
                    nc.scalar.activation(sq[:, 0, :], psum[:, b, :], ACT.Sigmoid,
                                         bias=pcol("ple_b", j + NC * layer)).then_inc(bank_free[b], 1)
                    act.wait_ge(xn_ready, (j + (x0 + 1)).v)
                    nc.scalar.copy(bh[1][:, j.v, :], x[:, j.v, :]).then_inc(xnh_ready, 1)
                panels(NC, body)
                w.ple += 1

            def attention(kind, units, chunk0):
                h0, g0 = w.h, w.g

                def exps(u, e, between=lambda: None):
                    n = u * 2 + (h0 + e)
                    for i in range(NB):
                        col, width, _ = span(kind, i)
                        act.wait_ge(nm_ready, n * 4 + (i + 1))
                        if not isinstance(u, int) or n >= 2:
                            act.wait_ge(pt_ready, n * 4 - 4)
                        nc.scalar.activation(pa[:, e, col:col + width], psum[:, 4 + i, 0:width], ACT.Exp,
                                             bias=nm[:, e, i:i + 1], accum_out=sm[:, e, i:i + 1]).then_inc(exp_done, 1)
                        if i == 1:
                            between()
                    if kind == "swa":
                        k = u * 1 + 4 * e
                        sk = sink[:, bass.ds(k, 1)] if not isinstance(k, int) else sink[:, k:k + 1]
                        act.wait_ge(snk_done, u * 2 + e)
                        nc.scalar.activation(snk[:, 2, :], nm[:, e, :], ACT.Exp, bias=sk).then_inc(snk_ready, 1)

                def high(u, e):
                    b = (g0 + e) % 2
                    act.wait_ge(o_ready, u * 2 + (h0 + e + 1))
                    nc.scalar.copy(bh[0][64 * e:64 * e + 64, u + chunk0, :],
                                   psum[64 * e:64 * e + 64, b, :]).then_inc(ohi_done, 1)

                def stage(u, e):
                    if kind == "mla":
                        return
                    n = u * 2 + (h0 + e)
                    act.wait_ge(s_ready, n * 4 - 4)
                    own, other = slice(64 * e, 64 * e + 64), slice(64 - 64 * e, 128 - 64 * e)
                    slot = slice(e * T, e * T + T)
                    last = nc.scalar.copy(qs[own, slot], qa[own, u, :])
                    if kind == "fox":
                        nc.scalar.copy(ks[own, slot], ka[own, u, :])
                        for a, dst in ((0, qs), (1, ks)):
                            k = u + (8 * a + (h0 - 16) // 2)
                            col = slice(k, k + 1) if isinstance(k, int) else bass.ds(k, 1)
                            last = nc.scalar.activation(dst[other, slot], fc[other, :], ACT.Identity,
                                                        scale=fsel[other, col], bias=fsel[other, 16 + a:17 + a])
                    last.then_inc(qk_staged, 1)

                def body(u):
                    exps(u, 1, lambda: stage(u + 1, 0))
                    high(u, 0)
                    exps(u + 1, 0, lambda: stage(u + 1, 1))
                    high(u, 1)
                if kind != "mla":
                    act.wait_ge(bank_free[0], (w.g + 1) // 2)
                    act.wait_ge(bank_free[1], w.g // 2)
                    if kind == "swa":
                        act.wait_ge(qs_zero, 1)
                    else:
                        act.wait_ge(fox_b, 1)
                stage(0, 0)
                stage(0, 1)
                exps(0, 0)
                if units > 2:
                    with act.Fori(0, units - 1) as u:
                        body(u)
                else:
                    body(0)
                exps(units - 1, 1)
                high(units - 1, 0)
                high(units - 1, 1)
                w.h += 2 * units
                w.g += 2 * units

            def layer0_in():
                for q, c in ((0, 0), (1, 1), (2, None), (3, 2), (4, 3), (5, 4)):
                    split(Idx(0, w.p + 3))
                    if c is not None:
                        b = w.g % 2
                        act.wait_ge(panel_done, w.p + 1)
                        nc.scalar.copy(lat[:, c, :], psum[:, b, :]).then_inc(bank_free[b], 1)
                    w.p += 1
                    w.g += 1
                for c in range(5):
                    if c >= 2:
                        act.wait_ge(lat_ss, c - 1)
                    b = ((0, 1, 3, 4, 5)[c]) % 2
                    act.wait_ge(bank_free[b], (0, 1, 3, 4, 5)[c] // 2 + 1)
                    nc.scalar.activation(sq[:, c % 2, :], lat[:, c, :], ACT.Square).then_inc(lat_sq, 1)
                act.wait_ge(lat_ss, 5)
                nc.scalar.activation(sd, psum[:, 2, :], ACT.Sqrt, bias=eps_col["rms1"], scale=4.0).then_inc(lat_sd, 1)
                nc.scalar.activation(s1c, psum[:, 3, :], ACT.Sqrt, bias=eps_col["rms1"], scale=1024 / 384).then_inc(lat_sd, 1)
                for c in range(5):
                    act.wait_ge(lat_t, c + 1)
                    nc.scalar.copy(lath[:, c, :], lat[:, c, :]).then_inc(lat_h, 1)

            def mla_in(grp):
                split(Idx(0, w.p + 3))
                split(Idx(0, w.p + 4))
                w.mid += 1
                w.g += 2
                if grp:
                    act.wait_ge(v_staged, 4)
                for i in range(2):
                    b = w.g % 2
                    if i == 0:
                        act.wait_ge(mid_done, w.mid + 1)
                    else:
                        act.wait_ge(panel_done, w.p + 2)
                    nc.scalar.copy(va[:, 2 * i:2 * i + 2, 0:2 * P],
                                   psum[:, b, :].rearrange("p (a n) -> p a n", a=2)).then_inc(bank_free[b], 1)
                    w.g += 1
                split(Idx(0, w.p + 5))
                split(Idx(0, w.p + 6))
                w.mid += 3
                w.p += 4
                w.g += 4

            def token_major(dst, b, p):
                act.wait_ge(panel_done, p)
                nc.scalar.copy(dst, psum[:, b, :].rearrange("p (a n) -> p a n", a=NB)).then_inc(bank_free[b], 1)

            split(Idx(0, 0))
            for c in range(NC):
                act.wait_ge(x_in[c // 2], 16)
                nc.scalar.copy(bh[1][:, c, :], x[:, c, :]).then_inc(xh0, 1)
            split(Idx(0, 1))
            split(Idx(0, 2))
            act.dma_start(rope[:, :], A["rope"]).then_inc(par_in, 16)
            act.wait_ge(par_in, 64)
            act.wait_ge(const_set, 1)
            eps_col = {True: eps[:, 0:1], False: eps[:, 1:2], "rms1": eps[:, 0:1]}
            layer0_in()
            for grp in range(GROUPS):
                mla_in(grp)
                attention("mla", 2, 2 * grp)
            act.wait_ge(o_ready, 8)
            act.wait_ge(qk_staged, 8)
            act.wait_ge(bank_free[0], w.g // 2)
            act.wait_ge(bank_free[1], w.g // 2)
            act.dma_start(relb[:, :], A["relb"]).then_inc(bias_in, 16)
            act.dma_start(oneh[:, :], A["oneh"]).then_inc(bias_in, 16)
            act.dma_start(negm[:, :], A["negm"]).then_inc(bias_in, 16)
            act.dma_start(sink[:, :], A["sink"].partition_broadcast(P)).then_inc(bias_in, 16)
            act.wait_ge(brow_ps, 1)
            act.dma_start(scratch.ap(), brow[:, :].unsqueeze(1).broadcast_to([8, P, SWA_F])).then_inc(brow_out, 16)
            act.wait_ge(brow_out, 16)
            act.dma_start(bias[:, :, :], bass.AP(scratch, P - 1, [[SWA_F - 1, P], [P * SWA_F, 8], [1, 2 * P]])).then_inc(bias_in, 16)
            for i in range(6):
                split(Idx(0, w.p + 3))
                b = w.g % 2
                if i == 0:
                    act.wait_ge(panel_done, w.p + 1)
                    nc.scalar.copy(ka[:, 0, :], psum[:, b, :]).then_inc(bank_free[b], 1)
                elif i == 1:
                    token_major(vs[:, :, :], b, w.p + 1)
                else:
                    act.wait_ge(panel_done, w.p + 1)
                    nc.scalar.activation(qa[:, i - 2, :], psum[:, b, :], ACT.Copy, scale=HEAD_SCALE).then_inc(bank_free[b], 1)
                w.p += 1
                w.g += 1
            attention("swa", 4, 4)
            only_split(NC)

            def feed_forward_and_gate(layer):
                norm(x, True, (), lambda c: ("ln1_b", NC * layer + c))
                for part_name in MLP:
                    if part_name[0] == "U":
                        up()
                    else:
                        only_split(NC)
                norm(x, True, (), lambda c: ("ln2_b", NC * layer + c))
                ple(layer)
            feed_forward_and_gate(0)
            split(Idx(0, w.p + 3))
            b = w.g % 2
            act.wait_ge(fsel_in, 32)
            act.wait_ge(panel_done, w.p + 1)
            nc.scalar.activation(ft[:, 0, :], psum[:, b, :], ACT.Identity, bias=fsel[:, 18:19]).then_inc(bank_free[b], 1)
            act.wait_ge(bank_free[b], w.g // 2 + 1)
            w.p += 1
            w.g += 1
            nc.scalar.activation(ft[:, 1, :], ft[:, 0, :], ACT.Abs).then_inc(act_step, 1)
            act.wait_ge(act_step, 1)
            nc.scalar.activation(ft[:, 2, :], ft[:, 1, :], ACT.Exp, scale=-1.0).then_inc(act_step, 1)
            act.wait_ge(act_step, 2)
            nc.scalar.activation(ft[:, 1, :], ft[:, 2, :], ACT.Ln, bias=1.0).then_inc(fox_a, 1)
            for grp in range(GROUPS):
                p0, g0 = w.p, w.g

                def queries(j, p, b):
                    act.wait_ge(panel_done, (p + 1).v)
                    nc.scalar.activation(qa[:, j.v, :], psum[:, b, :], ACT.Copy, scale=HEAD_SCALE).then_inc(bank_free[b], 1)

                act.wait_ge(qk_staged, 16 + 8 * grp)
                panels(4, queries)
                only_split(4)
                act.wait_ge(v_staged, 8 + 8 * grp)
                for i in range(2):
                    split(Idx(0, w.p + 3))
                    split(Idx(0, w.p + 4))
                    act.wait_ge(panel_done, w.p + 2)
                    for t in range(2):
                        b = w.g % 2
                        nc.scalar.copy(va[:, 2 * t:2 * t + 2, 2 * P * i:2 * P * (i + 1)],
                                       psum[:, b, :].rearrange("p (a n) -> p a n", a=2)).then_inc(bank_free[b], 1)
                        w.g += 1
                    w.p += 2
                attention("fox", 4, 4 * grp)
            only_split(NC)
            feed_forward_and_gate(1)

            st = Steps(act, pair_act, post_act, half_act)
            act.wait_ge(xn_ready, 16)
            act.dma_start(wm[:, :, :], A["wm"]).then_inc(wk_in, 16)
            act.dma_start(o64[:, :], A["o64"]).then_inc(wk_in, 16)
            norm(x, False, ((xn_ready, 16),))
            act.wait_ge(scaled, 1)
            split(Idx(0, B2 + 2), forced=True)
            act.wait_ge(scaled, 2)
            for i, dst in enumerate((la, rn, zr, zv)):
                split(Idx(0, w.p + 3))
                b = w.g % 2
                act.wait_ge(panel_done, w.p + 1)
                if i >= 2:
                    act.wait_ge(wk_set, 1)
                nc.scalar.copy(dst, psum[:, b, :]).then_inc(bank_free[b], 1)
                w.p += 1
                w.g += 1
            act.wait_ge(lora_z, 1)
            nc.scalar.activation(lw[0:64, :], la[0:64, :], ACT.Tanh)
            nc.scalar.copy(lw[64:128, :], la[64:128, :]).then_inc(lora_t, 1)
            act.wait_ge(lora_t, 1)
            nc.scalar.copy(lh[0][:, :], lw).then_inc(lora_h, 1)
            act.wait_ge(lora_z, 2)
            nc.scalar.activation(rn, kkn, ACT.Tanh, scale=0.5).then_inc(lora_t, 1)
            act.wait_ge(lora_z, 3)
            nc.scalar.copy(lh[1][:, :], kkn).then_inc(lora_h, 1)

            od0 = NC * 11

            def pair(c):
                p0, g0, m0 = w.p, w.g, w.mid
                later = not isinstance(c, int) or c > 0
                split(Idx(c, p0 + 3))
                if later:
                    centred_square(c + -1)
                act.wait_ge(mid_done, c * 2 + (m0 + 1))
                nc.scalar.activation(lw, psum[:, g0 % 2, :], ACT.Tanh, bias=hcol(c, 0), scale=0.5).then_inc(bank_free[g0 % 2], 1)
                act.wait_ge(mid_done, c * 2 + (m0 + 2))
                b = (g0 + 1) % 2
                nc.scalar.activation(la, psum[:, b, :], ACT.Tanh, bias=hcol(c, 8), scale=0.5).then_inc(bank_free[b], 1)
                st.wait(pair_dve, c, "sums")
                nc.scalar.activation(ep[:, :, 1:65], cu.rearrange("p (a t) -> p a t", a=8), ACT.Exp)
                st.did(pair_act, "decay", nc.scalar.activation(em, cu, ACT.Exp, scale=-1.0))
                if later:
                    root_of_output(c + -1)

                def copy_tile(i, dst, p):
                    b = (g0 + i) % 2
                    act.wait_ge(panel_done, Idx(c, p0 + p).v)
                    nc.scalar.copy(dst, psum[:, b, :]).then_inc(bank_free[b], 1)
                split(Idx(c, p0 + 4))
                copy_tile(2, zk, 1)
                if later:
                    high(c + -1)
                split(Idx(c, p0 + 5))
                copy_tile(3, gt[:, :], 2)
                st.wait(pair_dve, c, "mixed")
                st.did(pair_act, "square", nc.scalar.activation(sq[:, 0, :], zk, ACT.Square, scale=pcol("k_k", c)))
                act.wait_ge(opnd_dve, c + od0)
                copy_tile(4, zr, 3)
                st.wait(pair_dve, c, "kmax")
                st.did(pair_act, "root", nc.scalar.activation(kkn, rn, ACT.Sqrt))
                split(Idx(c, p0 + 6))
                copy_tile(5, zv, 4)
                st.wait(pair_dve, c, "ready")
                for f in range(2):
                    half(c * 2 + f, f)

            def centred_square(c):
                st.wait(post_dve, c, "centred")
                st.did(post_act, "osquare", nc.scalar.activation(sq[:, 0, :], zr, ACT.Square))

            def root_of_output(c):
                st.wait(post_pe, c, "var")
                st.did(post_act, "oroot", nc.scalar.activation(rn, psum[:, 3, :], ACT.Sqrt, bias=eps[:, 2:3]))

            def high(c):
                st.wait(post_dve, c, "out")
                st.did(post_act, "high", nc.scalar.copy(bh[1][:, c, :], zr))

            def half(n, f):
                cols = slice(f * 256, f * 256 + 256)
                for sema in (half_pe, half_dve, half_pool):
                    act.wait_ge(sema, before(sema, n))
                for e in range(2):
                    r = slice(64 * e, 64 * e + 64)
                    last = nc.scalar.copy(m_v[r, :, r], zv[r, cols].rearrange("p (a t) -> p a t", a=4))
                st.did(half_act, "v", last)

                def move(dst, product):
                    for g in range(2):
                        st.wait(half_pe, n, f"{product}.{g}")
                        st.did(half_act, f"{product}.{g}", nc.scalar.copy(dst[:, 2 * g:2 * g + 2, :], bank(f"{product}.{g}")))
                move(m_at, "at")
                move(m_bt, "bt")
                move(m_kt, "kt")
                move(m_vt, "vt")
                move(m_z, "z2")
                move(m_w, "w")
                for b in LEVELS[1:]:
                    move(m_z, f"z{b}")
                move(m_ta, "ta")
                move(m_n, "n")
                st.wait(half_pe, n, "o3")
                for e in range(2):
                    r = slice(64 * e, 64 * e + 64)
                    last = nc.scalar.copy(zr[r, cols].rearrange("p (a t) -> p a t", a=4), o_bank[r, :, r])
                st.did(half_act, "o", last)

            pair(0)
            with act.Fori(1, NC) as c:
                pair(c)
            centred_square(NC - 1)
            root_of_output(NC - 1)
            high(NC - 1)
            w.p += 4 * NC
            w.g += 6 * NC
            w.mid += 2 * NC

            act.dma_start(cw[:, :, :], A["cw"]).then_inc(cw_in, 16)
            g0 = w.g

            def sigmoid(j, p, b):
                if j.k % 2 == 0:
                    act.wait_ge(panel_done, (p + 1).v)
                    act.wait_ge(bank_free[1 - b], (j + (g0 - 3)).over2() + 1)
                    nc.scalar.activation(sq[:, j.k // 2, :], psum[:, b, :], ACT.Sigmoid,
                                         bias=pcol("b_gate", j.over4()) if j.k else 0.0).then_inc(bank_free[b], 1)
            panels(4 * NC, sigmoid)
            for j in range(NC):
                split(Idx(0, w.p + 3))
                b = w.g % 2
                act.wait_ge(panel_done, w.p + 1)
                nc.scalar.activation(sg[:, j, :], psum[:, b, :], ACT.Sigmoid, bias=pcol("b_gate", NC + j)).then_inc(bank_free[b], 1)
                w.p += 1
                w.g += 1
                if j == 1:
                    squares(y, True, range(2))
                if j == 3:
                    squares(y, True, range(2, NC))
                    root(True)
                for c in {4: (0, 1, 2), 5: (3, 4, 5), 6: (6, 7)}.get(j, ()):
                    silu(c)

            def merged(j, p, b):
                act.wait_ge(m_done, (j + 1).v)
                nc.scalar.copy(mh[:, j.v, :], mg[:, j.v, :]).then_inc(mrg_h, 1)
            panels(NC, merged)
            only_split(NC)
            norm(x, False, ((bank_free[w.g % 2], w.g // 2), (bank_free[1 - w.g % 2], (w.g + 1) // 2)))
            for part_name in MLP:
                if part_name[0] == "U":
                    up()
                else:
                    only_split(NC)
            norm(x, False, ((bank_free[w.g % 2], w.g // 2), (bank_free[1 - w.g % 2], (w.g + 1) // 2)), final=True)

        @block.vector
        def _(dve):
            w = Walk()
            chain = Chain(dve, dve_step)
            link = chain.link

            def panels(n, body, links=0):
                p0, g0 = w.p, w.g
                chain.turns(n, lambda j: body(j, j + p0, (g0 + j.k) % 2, j + g0), links)
                w.p += n
                w.g += n

            def skip(n):
                w.p += n
                w.g += n

            def residual(scale, total):
                if total:
                    link(nc.vector.memset(s1, 0.0))

                def body(j, p, b, g):
                    dve.wait_ge(panel_done, (p + 1).v)
                    nc.vector.scalar_tensor_tensor(x[:, j.v, :], x[:, j.v, :], scale, psum[:, b, :],
                                                   ALU.mult, ALU.add).then_inc(bank_free[b], 1)
                    if total:
                        dve.wait_ge(bank_free[b], g.over2() + 1)
                        link(nc.vector.tensor_tensor(s1, s1, x[:, j.v, :], ALU.add))
                panels(NC, body, links=int(total))

            def up(hb):
                u0, d0 = w.u, w.od

                def body(j, p, b, g):
                    dve.wait_ge(bank_free[b], g.over2() + 1)
                    h = sq[:, j.k % 2, :]
                    nc.vector.tensor_tensor(bh[hb][:, j.v, :], h, h, ALU.mult)
                    nc.vector.tensor_tensor(t2[:, j.k % 2, :], h, h, ALU.mult).then_inc(u_free, 1)
                    dve.wait_ge(u_free, (j + (u0 + 3)).v)
                    nc.vector.tensor_tensor(bl[hb][:, j.v, :], t2[:, j.k % 2, :], bh[hb][:, j.v, :].bitcast(F32),
                                            ALU.subtract).then_inc(opnd_dve, 1)
                panels(NC, body)
                w.u += NC
                w.od += NC

            def norm(gcol, src=x):
                nc.vector.tensor_copy(s1c, s1).then_inc(s1_ready, 1)
                dve.wait_ge(mu_done, w.mean + 1)
                for c in range(NC):
                    nc.vector.tensor_tensor(src[:, c, :], src[:, c, :], psum[:, 2, :], ALU.subtract).then_inc(d_ready, 1)
                dve.wait_ge(sd_ready, w.norm + 1)
                link(nc.vector.reciprocal(rs, sd))
                for c in range(NC):
                    nc.vector.scalar_tensor_tensor(src[:, c, :], src[:, c, :], pcol(*gcol(c)), rs,
                                                   ALU.mult, ALU.mult).then_inc(t_ready, 1)
                w.norm += 1
                w.mean += 1
                w.op += NC

            def rms_norm(gain, final=False):
                dve.wait_ge(sd_ready, w.norm + 1)
                link(nc.vector.reciprocal(rs, sd))
                for c in range(NC):
                    dst = x[:, c, :] if final else t2[:, c % 2, :]
                    if c >= 2 and not final:
                        dve.wait_ge(opnd_pool, w.op + c - 1)
                    nc.vector.scalar_tensor_tensor(dst, x[:, c, :], pcol(gain, c), rs, ALU.mult, ALU.mult).then_inc(t_ready, 1)
                w.norm += 1
                w.op += NC

            def ple(layer):
                dve.wait_ge(ph_ready, layer + 1)
                nc.vector.tensor_tensor(pl[:, :, :], praw, ph[:, :, :].bitcast(F32), ALU.subtract).then_inc(pl_ready, 1)
                w.p += 2
                w.g += 8
                x0 = NC * w.ple

                def body(j, p, b, g):
                    dve.wait_ge(bank_free[b], g.over2() + 1)
                    link(nc.vector.tensor_tensor(t2[:, 0, :], sq[:, 0, :], pj[:, j.v, :], ALU.mult))
                    nc.vector.tensor_tensor(x[:, j.v, :], x[:, j.v, :], t2[:, 0, :], ALU.add).then_inc(xn_ready, 1)
                    dve.wait_ge(xnh_ready, (j + (x0 + 1)).v)
                    nc.vector.tensor_tensor(bl[1][:, j.v, :], x[:, j.v, :], bh[1][:, j.v, :].bitcast(F32),
                                            ALU.subtract).then_inc(opnd_dve, 1)
                panels(NC, body, links=1)
                w.ple += 1
                w.od += NC

            def attention(kind, units, chunk0):
                h0, g0 = w.h, w.g

                def maximum(u, e, i):
                    n = u * 2 + (h0 + e)
                    _, width, _ = span(kind, i)
                    dve.wait_ge(s_ready, n * 4 + (i + 1))
                    s_i = psum[:, 4 + i, 0:width]
                    if kind == "swa":
                        k = u * 1 + 4 * e
                        nk = nsink[:, k:k + 1] if isinstance(k, int) else nsink[:, bass.ds(k, 1)]
                        link(nc.vector.tensor_reduce(snk[:, 0, i:i + 1], s_i, AX, ALU.max, negate=True))
                        nc.vector.tensor_scalar(nm[:, e, i:i + 1], snk[:, 0, i:i + 1], nk, None,
                                                ALU.min).then_inc(nm_ready, 1)
                    else:
                        nc.vector.tensor_reduce(nm[:, e, i:i + 1], s_i, AX, ALU.max, negate=True).then_inc(nm_ready, 1)

                def inverse(u, e, i):
                    n = u * 2 + (h0 + e)
                    dve.wait_ge(exp_done, n * 4 + (i + 1))
                    nc.vector.reciprocal(rc[:, e, i:i + 1], sm[:, e, i:i + 1]).then_inc(rc_done, 1)

                def inverses(u, e):
                    dve.wait_ge(exp_done, (u * 2 + (h0 + e)) * 4 + 4)
                    dve.wait_ge(snk_ready, u * 2 + (e + 1))
                    nc.vector.tensor_tensor(sm[:, e, :], sm[:, e, :], snk[:, 2, :], ALU.add).then_inc(snk_done, 1)
                    dve.wait_ge(snk_done, u * 2 + (e + 1))
                    for i in range(NB):
                        nc.vector.reciprocal(rc[:, e, i:i + 1], sm[:, e, i:i + 1]).then_inc(rc_done, 1)

                def turned(u, e, i):
                    n = u * 2 + (h0 + e)
                    if i == 0 and (not isinstance(n, int) or n >= 1):
                        dve.wait_ge(o_ready, n)
                    col, width, _ = span(kind, i)
                    dve.wait_ge(pt_ready, n * 4 + (i + 1))
                    nc.vector.tensor_copy(w4[:, col:col + width], psum[:, 2 + i % 2, 0:width]).then_inc(pt_copied, 1)

                def step(after, now, done=None):
                    for i in range(NB):
                        if now:
                            turned(*now, i)
                        if after:
                            maximum(*after, i)
                            if i and kind != "swa":
                                inverse(*after, i - 1)
                        if i == 0:
                            if now and kind != "swa":
                                inverse(*now, NB - 1)
                            if done:
                                low(*done)
                    if after and kind == "swa":
                        inverses(*after)

                def low(u, e):
                    b = (g0 + e) % 2
                    dve.wait_ge(ohi_done, u * 2 + (h0 + e + 1))
                    r = slice(64 * e, 64 * e + 64)
                    nc.vector.tensor_tensor(bl[0][r, u + chunk0, :], psum[r, b, :], bh[0][r, u + chunk0, :].bitcast(F32),
                                            ALU.subtract).then_inc(bank_free[b], 1)

                def body(u):
                    step((u + 1, 0), (u, 1), (u, 0))
                    step((u + 1, 1), (u + 1, 0), (u, 1))
                step((0, 0), None)
                step((0, 1), (0, 0))
                if units > 2:
                    at = chain.n
                    with dve.Fori(0, units - 1) as u:
                        chain.turn, chain.per = u, 8 * (kind == "swa")
                        body(u)
                    assert chain.n - at == chain.per
                    chain.n += chain.per * (units - 2)
                    chain.turn = chain.per = 0
                else:
                    body(0)
                step(None, (units - 1, 1), (units - 1, 0))
                low(units - 1, 1)
                w.h += 2 * units
                w.g += 2 * units

            def rotate(dst, b, scale):
                nc.vector.scalar_tensor_tensor(rt[64:96, 0, :], psum[96:128, b, :], scale, rope[96:128, :], ALU.mult, ALU.mult)
                link(nc.vector.scalar_tensor_tensor(rt[64:96, 1, :], psum[64:96, b, :], scale, rope[64:96, :],
                                                    ALU.mult, ALU.mult))
                for d in dst:
                    last = nc.vector.tensor_tensor(d, rt[64:96, 0, :], rt[64:96, 1, :], ALU.add)
                return last

            def mla_in(grp):
                if grp:
                    dve.wait_ge(qk_staged, 4)
                else:
                    dve.wait_ge(bank_free[0], 2)
                for t in range(2):
                    b = w.g % 2
                    if t == 0:
                        dve.wait_ge(mid_done, w.mid + 1)
                    else:
                        dve.wait_ge(panel_done, w.p + 1)
                    nc.vector.tensor_copy(ka[0:64, 2 * t, :], psum[0:64, b, :])
                    nc.vector.tensor_copy(ka[0:64, 2 * t + 1, :], psum[64:128, b, :]).then_inc(bank_free[b], 1)
                    w.g += 1
                w.g += 2
                w.mid += 2
                for t in range(4):
                    b = w.g % 2
                    if t % 2 == 0:
                        w.mid += 1
                        dve.wait_ge(mid_done, w.mid)
                    else:
                        dve.wait_ge(panel_done, w.p + 3 + t // 2)
                    if t:
                        dve.wait_ge(bank_free[1 - b], (w.g - 1) // 2 + 1)
                    nc.vector.tensor_scalar(qa[0:64, t, :], psum[0:64, b, :], MLA_SCALE, None, ALU.mult)
                    rotate([qa[64:96, t, :]], b, MLA_SCALE).then_inc(bank_free[b], 1)
                    w.g += 1
                w.p += 4

            nc.vector.memset(ones[:, :], 1.0 / D)
            nc.vector.memset(eps[:, 0:1], LN_EPS)
            nc.vector.memset(eps[:, 2:3], GN_EPS)
            nc.vector.memset(eps[:, 1:2], RMS_EPS).then_inc(const_set, 1)
            nc.vector.memset(sq[:, 0, 0:1], 0.0).then_inc(u_free, 2)
            for c in range(NC):
                dve.wait_ge(xh0, c + 1)
                nc.vector.tensor_tensor(bl[1][:, c, :], x[:, c, :], bh[1][:, c, :].bitcast(F32), ALU.subtract).then_inc(opnd_dve, 1)
            w.od += NC
            dve.wait_ge(par_in, 64)
            dve.wait_ge(panel_done, 3)
            rotate([ka[64:96, h, :] for h in range(4)], 0, 1.0).then_inc(bank_free[0], 1)
            w.p += 6
            w.g += 6
            dve.wait_ge(lat_sd, 1)
            link(nc.vector.reciprocal(rs, sd))
            dve.wait_ge(lat_sd, 2)
            link(nc.vector.reciprocal(s1, s1c))
            for c in range(5):
                col = pcol("kv_norm", c) if c < 2 else pcol("q_norm", c - 2)
                nc.vector.scalar_tensor_tensor(lat[:, c, :], lat[:, c, :], col, rs if c < 2 else s1,
                                               ALU.mult, ALU.mult).then_inc(lat_t, 1)
            for c in range(5):
                dve.wait_ge(lat_h, c + 1)
                nc.vector.tensor_tensor(latl[:, c, :], lat[:, c, :], lath[:, c, :].bitcast(F32), ALU.subtract).then_inc(lat_l, 1)
            for grp in range(GROUPS):
                mla_in(grp)
                attention("mla", 2, 2 * grp)
            dve.wait_ge(brow_mm, 1)
            dve.wait_ge(bias_in, 64)
            nc.vector.tensor_scalar(nsink[:, :], sink[:, :], -1.0, None, ALU.mult)
            nc.vector.tensor_tensor(brow[:, :], psum[0:8, 3, 0:SWA_F], negm[:, :], ALU.add).then_inc(brow_ps, 1)
            skip(6)
            attention("swa", 4, 4)
            residual(ALPHA, True)

            def feed_forward_and_gate(layer):
                norm(lambda c: ("ln1_g", NC * layer + c))
                for part_name in MLP:
                    q = int(part_name[1])
                    if part_name[0] == "U":
                        up(1 + q % 2)
                    else:
                        residual(ALPHA if q == 0 else 1.0, q == 3)
                norm(lambda c: ("ln2_g", NC * layer + c))
                ple(layer)
            feed_forward_and_gate(0)
            skip(1)
            dve.wait_ge(fsel_in, 32)
            link(nc.vector.memset(fone, 1.0))
            dve.wait_ge(fox_a, 1)
            link(nc.vector.scalar_tensor_tensor(ft[:, 2, :], ft[:, 0, :], 0.0, ft[:, 1, :], ALU.min, ALU.subtract))
            nc.vector.tensor_tensor_scan(fc[:, :], fone, ft[:, 2, :], 0.0, ALU.mult, ALU.add).then_inc(fox_b, 1)
            for grp in range(GROUPS):
                skip(4)
                dve.wait_ge(qk_staged, 16 + 8 * grp)

                def keys(j, p, b, g):
                    dve.wait_ge(panel_done, (p + 1).v)
                    nc.vector.tensor_copy(ka[:, j.v, :], psum[:, b, :]).then_inc(bank_free[b], 1)
                panels(4, keys)
                skip(4)
                attention("fox", 4, 4 * grp)
            residual(ALPHA, True)
            feed_forward_and_gate(1)

            st = Steps(dve, pair_dve, post_dve, half_dve)
            wait_tile = lambda b, count: dve.wait_ge(bank_free[b], count)
            for q, gains in ((B2 + 2, (0, 1)), (B2 + 3, (2, 2))):
                s = q % SLOTS
                dve.wait_ge(panel_in[s], q // SLOTS * 16 + 16)
                for k in range(NC):
                    if gains[0] == gains[1]:
                        c = slice(k * P, k * P + P)
                        last = nc.vector.tensor_scalar(raw[:, s, c], raw[:, s, c], pcol("mu_lora", gains[0] * NC + k),
                                                       None, ALU.mult)
                        continue
                    for e in range(2):
                        c = slice(k * P + 64 * e, k * P + 64 * e + 64)
                        last = nc.vector.tensor_scalar(raw[:, s, c], raw[:, s, c], pcol("mu_lora", gains[e] * NC + k),
                                                       None, ALU.mult)
                last.then_inc(scaled, 1)
            nc.vector.memset(m_v[:, :, :], 0.0)
            for m, sema in ((m_a, half_pe), (m_b, half_act), (m_k, half_dve), (m_r, half_pool)):
                nc.vector.memset(m[:, :, :], 0.0).then_inc(sema, 1)
            for a in z:
                nc.vector.memset(a[:, 0:1], 0.0)
            nc.vector.memset(ep[:, :, 0:1], 1.0)
            link(nc.vector.memset(going[:, :], 1.0))
            nc.vector.memset(going[:, :].rearrange("p (a t) -> p a t", t=64)[:, :, 0:1], 0.0)
            nc.vector.tensor_scalar(half_b[:, 0:8], par[:, PAR["w0"][0]:PAR["w0"][0] + 8], 0.5, None, ALU.mult)
            nc.vector.tensor_scalar(half_b[:, 8:16], par[:, PAR["a0"][0]:PAR["a0"][0] + 8], 0.5, None,
                                    ALU.mult).then_inc(wk_set, 1)
            rms_norm("norm_mix")
            g = w.g
            wait_tile(g % 2, g // 2 + 2)
            link(nc.vector.tensor_tensor(la, la, z[0][:, 0:T], ALU.add))
            nc.vector.tensor_tensor(la, la, zr, ALU.subtract).then_inc(lora_z, 1)
            wait_tile(1 - g % 2, (g + 1) // 2 + 2)
            link(nc.vector.tensor_tensor(kkn, rn, z[2][:, 0:T], ALU.add))
            nc.vector.tensor_tensor(kkn, kkn, zv, ALU.subtract).then_inc(lora_z, 1)
            dve.wait_ge(lora_t, 2)
            nc.vector.tensor_scalar(kkn, rn, 0.5, 0.5, ALU.mult, ALU.add).then_inc(lora_z, 1)
            for a, full in ((0, lw), (1, kkn)):
                dve.wait_ge(lora_h, a + 1)
                nc.vector.tensor_tensor(ll[a][:, :], full, lh[a][:, :].bitcast(F32), ALU.subtract).then_inc(lora_l, 1)
            skip(4)
            dve.wait_ge(wk_in, 32)
            V = nc.vector

            def pair(c):
                g0 = w.g

                def tile_moved(i):
                    wait_tile((g0 + i) % 2, c * 3 + ((g0 + i) // 2 + 1))

                def shift(i, dst):
                    link(V.tensor_tensor(sq[:, 0, :], z[i][:, 0:T], dst, ALU.subtract))
                    return V.scalar_tensor_tensor(dst, sq[:, 0, :], pcol_c("mu_rkv", i, c), dst, ALU.mult, ALU.add)
                later = not isinstance(c, int) or c > 0
                if later:
                    centre(c + -1)
                tile_moved(0)
                half_e = 0.5 * np.exp(-0.5)
                link(V.tensor_scalar(lw, lw, -half_e, -half_e, ALU.mult, ALU.add))
                st.did(pair_dve, "sums", V.tensor_tensor_scan(cu, going[:, :], lw, 0.0, ALU.mult, ALU.add))
                tile_moved(1)
                link(V.tensor_scalar(la, la, 0.5, 0.5, ALU.mult, ALU.add))
                st.wait(pair_dve, c, "sums")
                link(V.tensor_scalar(lw, la, -1.0, pcol_c("k_a", 0, c), ALU.add, ALU.mult))
                if later:
                    output(c + -1)
                tile_moved(2)
                st.did(pair_dve, "mixed", shift(1, zk))
                st.wait(pair_pe, c, "kk")
                st.did(pair_dve, "kmax", V.tensor_scalar(rn, psum[:, 2, :], 64.0, 1e-24, ALU.mult, ALU.max))
                tile_moved(4)
                link(shift(0, zr))
                st.wait(pair_act, c, "root")
                link(V.reciprocal(rn, kkn))
                link(V.scalar_tensor_tensor(kkn, zk, pcol_c("k_k", 0, c), rn, ALU.mult, ALU.mult))
                link(V.scalar_tensor_tensor(zk, lw, 1.0, zk, ALU.add, ALU.mult))
                link(V.tensor_tensor(la, kkn, la, ALU.mult))
                st.did(pair_dve, "prod", V.scalar_tensor_tensor(sq[:, 1, :], zr, pcol_c("r_k", 0, c), zk, ALU.mult, ALU.mult))
                operands(c * 2, 0)
                tile_moved(5)
                link(shift(2, zv))
                st.wait(pair_pe, c, "bonus")
                st.did(pair_dve, "ready", V.scalar_tensor_tensor(sq[:, 1, :], psum[:, 7, :], 64.0, zv, ALU.mult, ALU.mult))
                half(c * 2, 0)
                operands(c * 2 + 1, 1)
                half(c * 2 + 1, 1)

            def centre(c):
                st.wait(post_pe, c, "mean")
                st.did(post_dve, "centred", V.tensor_tensor(zr, zr, psum[:, 2, :], ALU.subtract))

            def output(c):
                st.wait(post_act, c, "oroot")
                link(V.reciprocal(kkn, rn))
                link(V.scalar_tensor_tensor(zr, zr, pcol_c("lnx_g", 0, c), kkn, ALU.mult, ALU.mult))
                link(V.scalar_tensor_tensor(zr, zr, pcol_c("lnx_b", 0, c), sq[:, 1, :], ALU.add, ALU.add))
                st.did(post_dve, "out", V.tensor_tensor(zr, zr, gt[:, :], ALU.mult))
                st.wait(post_act, c, "high")
                V.tensor_tensor(bl[1][:, c, :], zr, bh[1][:, c, :].bitcast(F32), ALU.subtract).then_inc(opnd_dve, 1)

            def operands(n, f):
                cols = slice(f * 256, f * 256 + 256)
                for sema in (half_pe, half_pool):
                    dve.wait_ge(sema, before(sema, n))

                def chunks(a, r):
                    return a[r, cols].rearrange("p (a t) -> p a t", a=4)
                decay_before, decay_upto = ep[:, 4 * f:4 * f + 4, 0:64], ep[:, 4 * f:4 * f + 4, 1:65]
                rows = [slice(0, 64), slice(64, 128)]
                for r in rows:
                    last = V.scalar_tensor_tensor(m_a[r, :, r], chunks(kkn, r), -1.0, decay_before[r], ALU.mult, ALU.mult)
                st.did(half_dve, "a", last)
                for r in rows:
                    last = V.tensor_tensor(m_b[r, :, r], chunks(la, r), chunks(em, r), ALU.mult)
                st.did(half_dve, "b", last)
                for r in rows:
                    last = V.tensor_tensor(m_k[r, :, r], chunks(zk, r), chunks(em, r), ALU.mult)
                st.did(half_dve, "k", last)
                for r in rows:
                    last = V.tensor_tensor(m_r[r, :, r], chunks(zr, r), decay_upto[r], ALU.mult)
                st.did(half_dve, "r", last)

            def half(n, f):
                def grouped(name, op):
                    for g in range(2):
                        st.wait(half_pe, n, f"{name}.{g}")
                        op(slice(2 * g, 2 * g + 2), g)

                def did(name, ins):
                    st.did(half_dve, name, ins)

                def masked(dst, product, m):
                    grouped(product, lambda ch, g: did(f"{product}.{g}", V.tensor_tensor(
                        dst[:, ch, :], bank(f"{product}.{g}"), each(wm[:, m, :]), ALU.mult)))

                def first_t(ch, g):
                    link(V.tensor_tensor(m_t[:, ch, :], bank(f"l.{g}"), each(wm[:, 2, :]), ALU.mult))
                    did(f"t1.{g}", V.tensor_tensor(m_t[:, ch, :], m_t[:, ch, :], each(ident[:, :]), ALU.add))

                def first_x(ch, g):
                    link(V.tensor_tensor(m_x[:, ch, :], m_lt[:, ch, :], each(wm[:, 3, :]), ALU.mult))
                    did(f"x1.{g}", V.tensor_tensor(m_x[:, ch, :], m_x[:, ch, :], each(ident[:, :]), ALU.add))
                grouped("l", first_t)
                masked(m_lt, "lt", 0)
                masked(m_rb, "rb", 1)
                masked(m_ak, "ak", 0)
                masked(m_rk, "rk", 1)
                st.wait(half_dve, n, "rk.1")
                grouped("bt", first_x)
                for b in LEVELS:
                    for m, dst in (("t", m_t), ("x", m_x)):
                        if m + str(b) != "t32":
                            grouped(f"{m}{b}", lambda ch, g: did(f"{m}{b}.{g}", V.tensor_tensor(
                                dst[:, ch, :], dst[:, ch, :], bank(f"{m}{b}.{g}"), ALU.add)))
                grouped("tw", lambda ch, g: did(f"tw.{g}", V.tensor_copy(m_tw[:, ch, :], bank(f"tw.{g}"))))

                def step_matrix(chs, g):
                    for i in range(2):
                        ch = 2 * g + i
                        last = V.scalar_tensor_tensor(m_mm[:, ch, :], ident[:, :], ep[:, 4 * f + ch, 64:65],
                                                      bank(f"mm.{g}")[:, i, :], ALU.mult, ALU.add)
                    did(f"mm.{g}", last)
                grouped("mm", step_matrix)
                grouped("p", lambda ch, g: did(f"p.{g}", V.tensor_tensor(m_p[:, ch, :], m_r[:, ch, :], bank(f"p.{g}"), ALU.add)))
                if f == 0:
                    did("s0", V.memset(m_s[:, 0, :], 0.0))
                else:
                    did("s0", V.tensor_copy(m_s[:, 0, :], m_s[:, 4, :]))
                st.wait(half_act, n, "n.1")
                st.wait(half_dve, n, "s0")
                for ch in range(4):
                    st.wait(half_pe, n, f"c{ch}")
                    did(f"s{ch + 1}", V.tensor_tensor(m_s[:, ch + 1, :], bank(f"c{ch}")[:, 0, :], m_n[:, ch, :], ALU.add))
                st.wait(half_dve, n, "s4")

            def pcol_c(name, i, c):
                return par[:, bass.ds(c + (PAR[name][0] + NC * i), 1)]
            pair(0)
            at0 = chain.n
            chain.n -= PAIR_LINKS
            with dve.Fori(1, NC) as c:
                chain.turn, chain.per = c, PAIR_LINKS
                pair(c)
            assert chain.n == at0, (chain.n - at0 + PAIR_LINKS)
            chain.n += PAIR_LINKS * (NC - 1)
            chain.turn = chain.per = 0
            centre(NC - 1)
            output(NC - 1)
            w.p += 4 * NC
            w.g += 6 * NC
            w.od += NC
            link(V.memset(ub[:, 0:30], 0.0))
            link(V.memset(s1, 0.0))
            dve.wait_ge(cw_in, 16)
            p0, g0 = w.p, w.g

            def branches(c):
                def gated(i, dst, slot):
                    b = (g0 + i) % 2
                    dve.wait_ge(panel_done, Idx(c, p0 + i + 1).v)
                    dve.wait_ge(bank_free[1 - b], Idx(c, g0 + i - 1).over2() + 1)
                    V.tensor_tensor(dst, psum[:, b, :], sq[:, slot, :], ALU.mult).then_inc(bank_free[b], 1)
                    dve.wait_ge(bank_free[b], Idx(c, g0 + i).over2() + 1)

                def taps(some):
                    for tap in some:
                        dst = t2[:, 0, :] if tap % 2 else y[:, c, :]
                        if tap == 1:
                            ins = V.tensor_scalar(dst, ub[:, tap:tap + T], cw[:, c, tap:tap + 1], None, ALU.mult)
                        else:
                            ins = V.scalar_tensor_tensor(dst, ub[:, tap:tap + T], cw[:, c, tap:tap + 1], dst, ALU.mult, ALU.add)
                        if tap == 30:
                            link(ins)
                        else:
                            chain.lagged(ins)
                gated(1, ub[:, 30:], 0)
                chain.lagged(V.tensor_scalar(y[:, c, :], ub[:, 0:T], cw[:, c, 0:1], pcol_c("conv_b", 0, c),
                                             ALU.mult, ALU.add))
                taps(range(1, 16))
                gated(3, mg[:, c, :], 1)
                taps(range(16, 31))
                link(V.tensor_tensor(y[:, c, :], y[:, c, :], t2[:, 0, :], ALU.add))
                link(V.tensor_tensor(s1, s1, y[:, c, :], ALU.add))
            at0 = chain.n
            with dve.Fori(0, NC) as c:
                chain.turn, chain.per = c, CHUNK_LINKS
                branches(c)
            assert chain.n - at0 == CHUNK_LINKS, chain.n - at0
            chain.n += CHUNK_LINKS * (NC - 1)
            chain.turn = chain.per = 0
            skip(5 * NC)
            norm(lambda c: ("cln_g", c), y)
            for c in range(NC):
                dve.wait_ge(ysg, c + 1)
                V.tensor_tensor(y[:, c, :], y[:, c, :], sq[:, c % 2, :], ALU.mult).then_inc(yz, 1)

            def merged(j, p, b, g):
                slot = j.k % 2
                dve.wait_ge(panel_done, (p + 1).v)
                V.tensor_tensor(t2[:, slot, :], psum[:, b, :], sg[:, j.v, :], ALU.mult).then_inc(bank_free[b], 1)
                dve.wait_ge(bank_free[b], g.over2() + 1)
                V.tensor_tensor(mg[:, j.v, :], mg[:, j.v, :], t2[:, slot, :], ALU.add).then_inc(m_done, 1)
                dve.wait_ge(mrg_h, (j + 1).v)
                V.tensor_tensor(ml[:, j.v, :], mg[:, j.v, :], mh[:, j.v, :].bitcast(F32), ALU.subtract).then_inc(opnd_dve, 1)
            panels(NC, merged)
            w.od += NC
            residual(1.0, False)
            rms_norm("norm_ff")
            for part_name in MLP:
                if part_name[0] == "U":
                    up(1 + int(part_name[1]) % 2)
                else:
                    residual(1.0, False)
            rms_norm("norm_fin", final=True)

        @block.gpsimd
        def _(pool):
            w = Walk()

            def low(q, forced=False):
                if isinstance(q.turn, int) and (q.v >= n_pan or (q.v == B2 + 2 and not forced)):
                    return
                s = q.k % SLOTS
                pool.wait_ge(hi_ready, (q + 1).v)
                nc.gpsimd.tensor_tensor(wl[:, s, :], raw[:, s, :], wh[:, s, :].bitcast(F32), ALU.subtract).then_inc(lo_ready, 1)

            def panels(n):
                p0 = w.p
                turns(pool, n, lambda j: low(j + (p0 + 3)), w.p + n in (n_pan, B2))
                w.p += n

            def norm(bo, src=x, between=lambda c: None):
                for c in range(NC):
                    between(c)
                    pool.wait_ge(nhi_ready, NC * w.norm + c + 1)
                    y_c = t2[:, c % 2, :] if src is t2 else src[:, c, :]
                    nc.gpsimd.tensor_tensor(bl[bo][:, c, :], y_c, bh[bo][:, c, :].bitcast(F32),
                                            ALU.subtract).then_inc(opnd_pool, 1)
                w.norm += 1
                w.op += NC

            def attention(kind, units):
                h0, q0, v0 = w.h, w.qs, w.vs

                def stage_qk(u, e):
                    if kind != "mla":
                        return
                    n = u * 2 + (h0 + e)
                    if n >= 2:
                        pool.wait_ge(s_ready, n * 4 - 4)
                    slot = slice(e * T, e * T + T)
                    nc.gpsimd.tensor_copy(qs[0:96, slot], qa[0:96, 2 * u + e, :])
                    nc.gpsimd.tensor_copy(ks[0:96, slot], ka[0:96, 2 * u + e, :]).then_inc(qk_staged, 1)

                def stage_v(u, e):
                    if kind == "swa":
                        return
                    n = u * 2 + (h0 + e)
                    if not isinstance(n, int) or n >= 2:
                        pool.wait_ge(o_ready, n + -1)
                    c = u * P + 64 * e
                    cols = slice(c, c + 64) if isinstance(c, int) else bass.ds(c, 64)
                    nc.gpsimd.tensor_copy(vs[:, :, 64 * e:64 * e + 64], va[:, :, cols]).then_inc(v_staged, 1)

                def scale(u, e):
                    n = u * 2 + (h0 + e)
                    for i in range(NB):
                        col, width, _ = span(kind, i)
                        pool.wait_ge(rc_done, n * 4 + (i + 1))
                        nc.gpsimd.tensor_tensor(pa[:, e, col:col + width], pa[:, e, col:col + width],
                                                rc[:, e, i:i + 1].broadcast_to([P, width]), ALU.mult).then_inc(p_ready, 1)

                def body(u):
                    stage_qk(u + 1, 0)
                    scale(u, 1)
                    stage_v(u + 1, 0)
                    stage_qk(u + 1, 1)
                    scale(u + 1, 0)
                    stage_v(u + 1, 1)
                pool.wait_ge(bank_free[0], (w.g + 1) // 2)
                pool.wait_ge(bank_free[1], w.g // 2)
                stage_qk(0, 0)
                stage_qk(0, 1)
                stage_v(0, 0)
                stage_v(0, 1)
                scale(0, 0)
                if units > 2:
                    with pool.Fori(0, units - 1) as u:
                        body(u)
                else:
                    body(0)
                scale(units - 1, 1)
                w.qs += units
                w.vs += 2 * units * (kind != "swa")
                w.h += 2 * units
                w.g += 2 * units

            for q in range(3):
                low(Idx(0, q))
            w.p = 0
            w.qs = w.vs = 0
            nc.gpsimd.memset(qs[:, :], 0.0)
            nc.gpsimd.memset(ks[:, :], 0.0).then_inc(pool_step, 1)
            pool.wait_ge(pool_step, 1)
            panels(6)
            w.g = 6
            for grp in range(GROUPS):
                panels(4)
                w.g += 8
                attention("mla", 2)
            pool.wait_ge(s_ready, 4 * w.h)
            nc.gpsimd.memset(qs[:, :], 0.0).then_inc(qs_zero, 1)
            panels(6)
            w.g += 6
            attention("swa", 4)
            panels(NC)
            w.g += NC

            def feed_forward_and_gate(layer):
                norm(0)
                panels(8 * NC)
                norm(0)
                pool.dma_start(praw, A["pT"][:, 2 * layer:2 * layer + 2, :]).then_inc(pp_in, 16)
                panels(2)
                panels(NC)
                w.g += 8 * NC + 8 + NC
            feed_forward_and_gate(0)
            pool.dma_start(fsel[:, 0:18], A["fsel"]).then_inc(fsel_in, 16)
            pool.dma_start(fsel[:, 18:19], A["bf"]).then_inc(fsel_in, 16)
            panels(1)
            w.g += 1
            pool.wait_ge(fsel_in, 32)
            for grp in range(GROUPS):
                panels(12)
                w.g += 12
                attention("fox", 4)
            panels(NC)
            w.g += NC
            feed_forward_and_gate(1)

            norm(0, t2)
            low(Idx(0, B2 + 2), forced=True)
            panels(4)
            st = Steps(pool, half_pool)

            def half(n, f):
                for sema in (half_pe, half_act):
                    pool.wait_ge(sema, before(sema, n))
                last_decay = ep[:, 4 * f:4 * f + 4, 64:65].broadcast_to([P, 4, P])
                st.wait(half_dve, n, "b")
                st.did(half_pool, "bd", nc.gpsimd.tensor_tensor(m_bd[:, :, :], m_b[:, :, :], last_decay, ALU.mult))
                st.wait(half_dve, n, "k")
                st.did(half_pool, "kd", nc.gpsimd.tensor_tensor(m_kd[:, :, :], m_k[:, :, :], last_decay, ALU.mult))
                for i, b in enumerate(LEVELS):
                    for g in range(2):
                        if i == 0:
                            st.wait(half_dve, n, f"lt.{g}")
                        else:
                            st.wait(half_pe, n, f"z{LEVELS[i - 1]}.{g}")
                        ch = slice(2 * g, 2 * g + 2)
                        st.did(half_pool, f"off{b}.{g}", nc.gpsimd.tensor_tensor(
                            m_off[:, ch, :], m_lt[:, ch, :], each(wm[:, 4 + i, :]), ALU.mult))

            def pair(c):
                for i in range(4):
                    low(Idx(c, p0 + 3 + i))
                for f in range(2):
                    half(c * 2 + f, f)
            pool.wait_ge(wk_in, 32)
            p0 = w.p
            with pool.Fori(0, NC) as c:
                pair(c)
            w.p += 4 * NC
            panels(4 * NC)
            panels(5)

            def between(c):
                if c in (3, 5, 7):
                    panels(1)
            norm(1, y, between)
            panels(NC)
            panels(NC)
            norm(0, t2)
            panels(8 * NC)

        @block.tensor
        def _(pe):
            w = Walk()

            def three(out, hi_a, lo_a, hi_b, lo_b, first, last):
                nc.tensor.matmul(out, hi_a, hi_b, start=first, stop=False)
                nc.tensor.matmul(out, hi_a, lo_b, start=False, stop=False)
                return nc.tensor.matmul(out, lo_a, hi_b, start=False, stop=last)

            def bank_wait(b, g):
                if not isinstance(g.turn, int) or g.v >= 2:
                    pe.wait_ge(bank_free[b], g.over2())

            def panels(n, bo, ready=None):
                p0, g0 = w.p, w.g

                def step(j):
                    p, b = j + p0, (g0 + j.k) % 2
                    s = p.k % SLOTS
                    pe.wait_ge(lo_ready, (p + 1).v)
                    bank_wait(b, j + g0)
                    for k in range(NC):
                        if ready:
                            pe.wait_ge(ready[0], ready[1] + k + 1)
                        c = slice(k * P, k * P + P)
                        last = three(psum[:, b, :], wh[:, s, c], wl[:, s, c], bh[bo][:, k, :], bl[bo][:, k, :],
                                     k == 0, k == NC - 1)
                    last.then_inc(panel_done, 1)
                turns(pe, n, step)
                w.p += n
                w.g += n

            def token_major(bo):
                b = w.g % 2
                s = w.p % SLOTS
                pe.wait_ge(lo_ready, w.p + 1)
                bank_wait(b, Idx(0, w.g))
                for tb in range(NB):
                    r = slice(tb * P, tb * P + P)
                    for k in range(NC):
                        c = slice(k * P, k * P + P)
                        last = three(psum[:, b, r], bh[bo][:, k, r], bl[bo][:, k, r], wh[:, s, c], wl[:, s, c],
                                     k == 0, k == NC - 1)
                last.then_inc(panel_done, 1)
                w.p += 1
                w.g += 1

            def token_major_wide(bo):
                for half_k in range(2):
                    s = w.p % SLOTS
                    pe.wait_ge(lo_ready, w.p + 1)
                    for tb in range(NB):
                        g = w.g + tb // 2
                        b = g % 2
                        if half_k == 0 and tb % 2 == 0:
                            bank_wait(b, Idx(0, g))
                        r = slice(tb * P, tb * P + P)
                        cols = slice(tb % 2 * 2 * P, tb % 2 * 2 * P + 2 * P)
                        for i in range(4):
                            k = 4 * half_k + i
                            c = slice(i * 2 * P, i * 2 * P + 2 * P)
                            last = three(psum[:, b, cols], bh[bo][:, k, r], bl[bo][:, k, r], wh[:, s, c], wl[:, s, c],
                                         k == 0 and tb % 2 == 0, k == NC - 1 and tb % 2 == 1)
                    last.then_inc(panel_done, 1)
                    w.p += 1
                w.g += 2

            def short(tiles, hi, lo, n_k):
                s = w.p % SLOTS
                pe.wait_ge(lo_ready, w.p + 1)
                for t in range(tiles):
                    b = w.g % 2
                    bank_wait(b, Idx(0, w.g))
                    for k in range(n_k):
                        c = slice((t * n_k + k) * P, (t * n_k + k + 1) * P)
                        last = three(psum[:, b, :], wh[:, s, c], wl[:, s, c], hi[:, k, :], lo[:, k, :], k == 0, k == n_k - 1)
                    last.then_inc(mid_done if t < tiles - 1 else panel_done, 1)
                    w.g += 1
                w.mid += tiles - 1
                w.p += 1

            def norm_mean():
                pe.wait_ge(s1_ready, w.mean + 1)
                w.mean += 1
                nc.tensor.matmul(psum[:, 2, :], ones[:, :], s1c, start=True, stop=True).then_inc(mu_done, 1)

            def norm(mean):
                if mean:
                    norm_mean()
                for c in range(NC):
                    pe.wait_ge(sq_ready, w.nsq + c + 1)
                    nc.tensor.matmul(psum[:, 3, :], ones[:, :], sq[:, c % 2, :], start=(c == 0), stop=(c == NC - 1)).then_inc(sq_used, 1)
                w.nsq += NC
                w.norm += 1

            def attention(kind, units):
                h0, g0, q0, v0 = w.h, w.g, w.qs, w.vs

                def scores(u, e, i):
                    n = u * 2 + (h0 + e)
                    if i == 0:
                        pe.wait_ge(qk_staged, n + 1)
                    _, width, kb = span(kind, i)
                    out = psum[:, 4 + i, 0:width]
                    if not isinstance(n, int) or n >= 1:
                        pe.wait_ge(exp_done, n * 4 + (i - 3))
                    k_c = slice(kb * P, kb * P + width)
                    q_ = qs[:, e * T + i * P:e * T + i * P + P]
                    k_ = ka[:, 0, k_c] if kind == "swa" else ks[:, e * T:e * T + width]
                    nc.tensor.matmul(out, q_, k_, start=True, stop=False)
                    if kind == "swa":
                        k = u * 1 + 4 * e
                        lo_c = 2 * P - width
                        k = slice(k, k + 1) if isinstance(k, int) else bass.ds(k, 1)
                        last = nc.tensor.matmul(out, ident[:, :], bias[:, k, lo_c:2 * P].rearrange("p a b -> p (a b)"),
                                                start=False, stop=True)
                    else:
                        last = nc.tensor.matmul(out[:, width - P:width], ident[:, :], mask[:, :], start=False, stop=True)
                    last.then_inc(s_ready, 1)

                def turn(u, e, i):
                    n = u * 2 + (h0 + e)
                    pe.wait_ge(p_ready, n * 4 + (i + 1))
                    if not isinstance(n, int) or n * 4 + i >= 2:
                        pe.wait_ge(pt_copied, n * 4 + (i - 1))
                    col, width, _ = span(kind, i)
                    for c in range(0, width, P):
                        last = nc.tensor.transpose(psum[:, 2 + i % 2, c:c + P], pa[:, e, col + c:col + c + P], ident[:, :])
                    last.then_inc(pt_ready, 1)

                def values(u, e, i):
                    n = u * 2 + (h0 + e)
                    b = (g0 + e) % 2
                    r = slice(64 * e, 64 * e + 64)
                    if i == 0:
                        if kind != "swa":
                            pe.wait_ge(v_staged, u * 2 + (v0 + e + 1))
                        pe.wait_ge(bank_free[b], u + (g0 + e) // 2)
                    col, width, kb = span(kind, i)
                    pe.wait_ge(pt_copied, n * 4 + (i + 1))
                    for c in range(0, width, P):
                        last = nc.tensor.matmul(psum[r, b, i * P:i * P + P], vs[:, kb + c // P, r], w4[:, col + c:col + c + P],
                                                start=(c == 0), stop=(c == width - P))
                    if i == NB - 1:
                        last.then_inc(o_ready, 1)

                def step(after, now):
                    if now:
                        turn(*now, 0)
                    for i in range(NB):
                        if after:
                            scores(*after, i)
                        if now:
                            if i + 1 < NB:
                                turn(*now, i + 1)
                            values(*now, i)

                def body(u):
                    step((u, 1), (u, 0))
                    step((u + 1, 0), (u, 1))
                step((0, 0), None)
                if units > 2:
                    with pe.Fori(0, units - 1) as u:
                        body(u)
                else:
                    body(0)
                step((units - 1, 1), (units - 1, 0))
                step(None, (units - 1, 1))
                w.h += 2 * units
                w.g += 2 * units
                w.qs += units
                w.vs += 2 * units * (kind != "swa")
                pe.wait_ge(bank_free[0], (w.g + 1) // 2)
                pe.wait_ge(bank_free[1], w.g // 2)

            w.qs = w.vs = 0
            pe.wait_ge(const_set, 1)
            pe.wait_ge(par_in, 48)
            panels(6, 1, ready=(opnd_dve, 0))
            w.od += NC
            for c in range(5):
                pe.wait_ge(lat_sq, c + 1)
                nc.tensor.matmul(psum[:, 2 if c < 2 else 3, :], ones[:, :], sq[:, c % 2, :], start=(c in (0, 2)),
                                 stop=(c in (1, 4))).then_inc(lat_ss, 1)
            pe.wait_ge(lat_l, 5)
            for grp in range(GROUPS):
                short(2, lath[:, 0:2, :], latl[:, 0:2, :], 2)
                s = w.p % SLOTS
                pe.wait_ge(lo_ready, w.p + 1)
                for t in range(2):
                    b = w.g % 2
                    bank_wait(b, Idx(0, w.g))
                    for a in range(2):
                        r = slice((2 * t + a) * P, (2 * t + a + 1) * P)
                        for k in range(2):
                            c = slice(k * 2 * P, (k + 1) * 2 * P)
                            last = three(psum[:, b, a * 2 * P:(a + 1) * 2 * P], lath[:, k, r], latl[:, k, r], wh[:, s, c], wl[:, s, c],
                                         k == 0, k == 1)
                    last.then_inc(panel_done if t else mid_done, 1)
                    w.g += 1
                w.mid += 1
                w.p += 1
                short(2, lath[:, 2:5, :], latl[:, 2:5, :], 3)
                short(2, lath[:, 2:5, :], latl[:, 2:5, :], 3)
                attention("mla", 2)
            pe.wait_ge(bias_in, 64)
            nc.tensor.matmul(psum[0:8, 3, 0:SWA_F], relb[:, :], oneh[:, :], start=True, stop=True).then_inc(brow_mm, 1)
            panels(1, 1)
            token_major(1)
            panels(4, 1)
            pe.wait_ge(bias_in, 80)
            attention("swa", 4)
            panels(NC, 0)

            def feed_forward_and_gate(layer):
                norm(True)
                for part_name in MLP:
                    q = int(part_name[1])
                    if part_name[0] == "U":
                        panels(NC, 0, ready=(opnd_pool, w.op) if q == 0 else None)
                        if q == 0:
                            w.op += NC
                        w.ud = w.od = w.od + NC
                        if q == 0:
                            w.d0 = w.od - NC
                    else:
                        pe.wait_ge(opnd_dve, w.d0 + NC * (q + 1))
                        panels(NC, 1 + q % 2)
                norm(True)
                pe.wait_ge(pl_ready, layer + 1)
                short(4, ph, pl, 2)
                short(4, ph, pl, 2)
                panels(NC, 0, ready=(opnd_pool, w.op))
                w.op += NC
                w.od += NC
            feed_forward_and_gate(0)
            panels(1, 1, ready=(opnd_dve, w.od - NC))
            for grp in range(GROUPS):
                panels(8, 1)
                token_major_wide(1)
                token_major_wide(1)
                attention("fox", 4)
            panels(NC, 0)
            feed_forward_and_gate(1)

            st = Steps(pe, pair_pe, post_pe, half_pe)
            norm(False)
            panels(4, 0, ready=(opnd_pool, w.op))
            w.op += NC
            pe.wait_ge(wk_in, 32)
            pe.wait_ge(lora_l, 2)

            def pair(c):
                p0, g0 = w.p, w.g

                def tile_bank(i):
                    b = (g0 + i) % 2
                    pe.wait_ge(bank_free[b], c * 3 + (g0 + i) // 2)
                    return b

                def dense_part(b, s, ks):
                    for k in ks:
                        cols = slice(k * P, k * P + P)
                        last = three(psum[:, b, :], wh[:, s, cols], wl[:, s, cols], bh[0][:, k, :], bl[0][:, k, :],
                                     k == 0, k == NC - 1)
                    return last
                later = not isinstance(c, int) or c > 0
                if later:
                    mean(c + -1)
                s = (p0 + 1) % SLOTS
                pe.wait_ge(lo_ready, Idx(c, p0 + 2).v)

                def lora_part(i, r, cols, a):
                    b = tile_bank(i)
                    w_c = slice(cols, cols + P)
                    return three(psum[:, b, :], wh[r, s, w_c], wl[r, s, w_c], lh[a][r, :], ll[a][r, :], True, True)
                lora_part(0, slice(0, 64), 0, 0).then_inc(mid_done, 1)
                lora_part(1, slice(64, 128), 0, 0).then_inc(mid_done, 1)
                b = tile_bank(2)
                if later:
                    variance(c + -1)
                dense_part(b, p0 % SLOTS, range(NC)).then_inc(panel_done, 1)
                lora_part(3, slice(0, 128), P, 1).then_inc(panel_done, 1)
                b = tile_bank(4)
                pe.wait_ge(lo_ready, Idx(c, p0 + 3).v)
                dense_part(b, (p0 + 2) % SLOTS, range(4))
                st.wait(pair_act, c, "square")
                st.did(pair_pe, "kk", nc.tensor.matmul(psum[:, 2, :], o64[:, :], sq[:, 0, :], start=True, stop=True))
                dense_part(b, (p0 + 2) % SLOTS, range(4, NC)).then_inc(panel_done, 1)
                b = tile_bank(5)
                pe.wait_ge(lo_ready, Idx(c, p0 + 4).v)
                dense_part(b, (p0 + 3) % SLOTS, range(NC)).then_inc(panel_done, 1)
                st.wait(pair_dve, c, "prod")
                st.did(pair_pe, "bonus", nc.tensor.matmul(psum[:, 7, :], o64[:, :], sq[:, 1, :], start=True, stop=True))
                for f in range(2):
                    half(c * 2 + f, (pair_dve, at(pair_dve, c, "ready")) if f == 0 else None)

            def mean(c):
                st.wait(half_act, c * 2 + 1, "o")
                st.wait(half_dve, c * 2 + 1, "s4")
                st.did(post_pe, "mean", nc.tensor.matmul(psum[:, 2, :], o64[:, :], zr, start=True, stop=True))

            def variance(c):
                st.wait(post_act, c, "osquare")
                st.did(post_pe, "var", nc.tensor.matmul(psum[:, 3, :], o64[:, :], sq[:, 0, :], start=True, stop=True))

            def half(n, ready):
                def waits(needs):
                    for sema in (half_act, half_dve, half_pool):
                        of = [EVENTS[sema].index(what) + 1 for s, what in needs if s is sema]
                        if of:
                            pe.wait_ge(sema, before(sema, n) + max(of))

                def product(name, *terms, needs=(), turn=False):
                    for g in range(2):
                        i = PRODUCTS.index(f"{name}.{g}")
                        if i == 4:
                            pe.wait_ge(half_act, before(half_act, n))
                            if ready:
                                pe.wait_ge(*ready)
                        waits([(s, what + f".{g}" if what + f".{g}" in EVENTS[s] else what) for s, what in needs]
                              + ([MOVED[PRODUCTS[i - 6]]] if i >= 6 else []))
                        for j in range(2):
                            ch = 2 * g + j
                            for i, (a, b) in enumerate(terms):
                                out = bank(f"{name}.{g}")[:, j, :]
                                if turn:
                                    last = nc.tensor.transpose(out, a[:, ch, :], b)
                                else:
                                    last = nc.tensor.matmul(out, a[:, ch, :], b[:, ch, :], start=(i == 0), stop=(i == len(terms) - 1))
                        st.did(half_pe, f"{name}.{g}", last)
                by_act, by_dve, by_pool = (lambda what: (half_act, what)), (lambda what: (half_dve, what)), (lambda what: (half_pool, what))

                product("l", (m_a, m_b), needs=[by_dve("b")])
                product("lt", (m_b, m_a))
                product("rb", (m_b, m_r), needs=[by_dve("r")])
                product("ak", (m_k, m_a))
                product("rk", (m_k, m_r))
                product("at", (m_a, ident[:, :]), turn=True)
                product("bt", (m_bd, ident[:, :]), needs=[by_pool("bd")], turn=True)
                product("kt", (m_kd, ident[:, :]), needs=[by_pool("kd")], turn=True)
                product("vt", (m_v, ident[:, :]), needs=[by_act("v")], turn=True)
                last_t, last_x = "t1", "x1"
                for b in LEVELS:
                    product(f"z{b}", (m_off, m_t), needs=[by_pool(f"off{b}"), by_dve(last_t)])
                    if b == LEVELS[0]:
                        product("w", (m_ak, m_vt), needs=[by_dve("ak"), by_act("vt")])
                    if b != LEVELS[-1]:
                        product(f"t{b}", (m_x, m_z), needs=[by_act(f"z{b}"), by_dve(last_x)])
                    product(f"x{b}", (m_z, m_x), needs=[by_act(f"z{b}"), by_dve(last_x)])
                    last_t, last_x = f"t{b}", f"x{b}"
                product("ta", (m_x, m_at), needs=[by_dve(last_x), by_act("at")])
                product("tw", (m_x, m_w), needs=[by_act("w")])
                product("mm", (m_ta, m_bt), needs=[by_act("ta")])
                product("p", (m_ta, m_rb), needs=[by_dve("rb")])
                product("n", (m_bt, m_tw), (m_kt, m_vt), needs=[by_dve("tw"), by_act("kt")])
                for ch in range(4):
                    waits([by_dve(f"s{ch}")] + ([MOVED["n.0"]] if ch == 3 else []))
                    st.did(half_pe, f"c{ch}", nc.tensor.matmul(bank(f"c{ch}")[:, 0, :], m_mm[:, ch, :], m_s[:, ch, :],
                                                              start=True, stop=True))
                    for i, (a, b) in enumerate(((m_tw, m_rb), (m_vt, m_rk), (m_s, m_p))):
                        last = nc.tensor.matmul(o_bank[:, ch, :], a[:, ch, :], b[:, ch, :], start=(i == 0), stop=(i == 2))
                    st.did(half_pe, f"o{ch}", last)

            pair(0)
            with pe.Fori(1, NC) as c:
                pair(c)
            mean(NC - 1)
            variance(NC - 1)
            w.p += 4 * NC
            w.g += 6 * NC
            w.mid += 2 * NC
            w.od += NC

            p0, g0 = w.p, w.g

            def branches(j):
                p, b = j + p0, (g0 + j.k) % 2
                s = p.k % SLOTS
                o = 1 if j.k == 3 else 0
                pe.wait_ge(lo_ready, (p + 1).v)
                bank_wait(b, j + g0)
                if o:
                    pe.wait_ge(opnd_dve, w.od)
                for k in range(NC):
                    c = slice(k * P, k * P + P)
                    last = three(psum[:, b, :], wh[:, s, c], wl[:, s, c], bh[o][:, k, :], bl[o][:, k, :],
                                 k == 0, k == NC - 1)
                last.then_inc(panel_done, 1)
            turns(pe, 4 * NC, branches)
            w.p += 4 * NC
            w.g += 4 * NC
            panels(2, 0)
            norm_mean()
            panels(2, 0)
            norm(False)
            panels(NC - 4, 0)
            panels(NC, 1, ready=(opnd_pool, w.op))
            w.op += NC
            panels(NC, 3, ready=(opnd_dve, w.od))
            w.od += NC
            norm(False)
            for part_name in MLP:
                q = int(part_name[1])
                if part_name[0] == "U":
                    panels(NC, 0, ready=(opnd_pool, w.op) if q == 0 else None)
                    if q == 0:
                        w.d0 = w.od
                else:
                    pe.wait_ge(opnd_dve, w.d0 + NC * (q + 1))
                    panels(NC, 1 + q % 2)
            norm(False)


def dense(m):
    k, n = m.shape
    return m.reshape(k // P, P, n // P, P).transpose(2, 1, 0, 3).reshape(n // P, P, k // P * P)


def filled(a):
    while a.shape[1] < D:
        a = np.concatenate([a, a[:, :D - a.shape[1]]], axis=1)
    return a


def tiles(m):
    return dense(m).transpose(1, 0, 2).reshape(P, -1)


def weight_stream(I):
    out = []
    w = I["ev_w_in"][0]
    rope = w[:, 640:672]
    swapped = np.concatenate([rope[:, 16:], rope[:, :16]], axis=1)
    out += [*dense(w[:, 384:640]), *dense(np.concatenate([rope, rope, rope, swapped], axis=1)), *dense(w[:, :384])]
    uq = I["ev_w_uq"][0].reshape(384, 8, 96)
    uq = np.concatenate([uq, uq[:, :, 80:96], uq[:, :, 64:80]], axis=2)
    ukv = I["ev_w_ukv"][0].reshape(256, 8, 128)
    for g in range(2):
        hs = slice(4 * g, 4 * g + 4)
        out.append(filled(tiles(ukv[:, hs, :64].reshape(256, 256))))
        out.append(filled(ukv[:, hs, 64:].reshape(2, P, 256).transpose(1, 0, 2).reshape(P, 512)))
        for h in (4 * g, 4 * g + 2):
            out.append(filled(tiles(uq[:, h:h + 2].reshape(384, 256))))
    out += [*dense(w[:, 1184:1440])]
    pair = np.array([(u + 4 * e) * 64 + d for u in range(4) for e in range(2) for d in range(64)])
    out += [*dense(w[:, 672:1184][:, pair])]
    out += [*dense(I["ev_w_out"][0][np.concatenate([np.arange(512), 512 + pair])])]

    def feed_forward(up, down):
        q = D
        for name in ("U0", "U1", "D0", "U2", "D1", "U3", "D2", "D3"):
            c = slice(int(name[1]) * q, int(name[1]) * q + q)
            out.extend(dense(up[:, c]) if name[0] == "U" else dense(down[c]))

    def ff_and_gate(l):
        feed_forward(I["w_up"][l], I["w_down"][l])
        pw = I["ple_w_proj"][l]
        out.extend([tiles(pw[:, :512]), tiles(pw[:, 512:])])
        out.extend(dense(I["ple_w_gate"][l]))
    ff_and_gate(0)
    w = I["od_w_in"][0]
    out += [*dense(np.tile(w[:, 3072:], (1, 8)))]
    for g in range(2):
        for a in range(2):
            out += [*dense(w[:, a * D + 512 * g:a * D + 512 * g + 512])]
        for i in range(4):
            c = 2 * D + 512 * g + 256 * (i // 2)
            out.append(w[512 * (i % 2):512 * (i % 2) + 512, c:c + 256].reshape(4, P, 256).transpose(1, 0, 2).reshape(P, D))
    out += [*dense(I["od_w_out"][0])]
    ff_and_gate(1)
    first = len(out)
    lora = [*dense(np.concatenate([I["decay_w1_2"][0], I["aaa_a1_2"][0]], axis=1)), *dense(I["gate_g1_2"][0])]
    out += lora + lora
    w = I["w_in_2"][0]
    r, k, v, glu_a, glu_b, gate0, gate1 = (dense(w[:, i * D:(i + 1) * D]) for i in range(7))
    second = np.concatenate([I["decay_w2_2"][0], I["aaa_a2_2"][0]], axis=0)
    for c in range(NC):
        cols = slice(c * P, c * P + P)
        out += [k[c], filled(np.concatenate([second[:, cols], I["gate_g2_2"][0][:, cols]], axis=1)), r[c], v[c]]

    def taking_turns(*kinds):
        return [m for one_of_each in zip(*kinds) for m in one_of_each]
    out += taking_turns(glu_b, glu_a, gate0, dense(I["w_rwkv_proj_2"][0]))
    out += [*gate1, *dense(I["w_conv_proj_2"][0])]
    out += [*dense(I["w_out_2"][0])]
    feed_forward(I["w_ff1_2"][0], I["w_ff2_2"][0])
    return np.stack(out), first


def layout(I):
    stream, third_layer = weight_stream(I)
    A = {"w": stream}

    def fm(a):
        return np.ascontiguousarray(a.T.reshape(-1, P, a.shape[0]).transpose(1, 0, 2))
    A["xT"] = fm(I["x"][0])
    A["pT"] = np.concatenate([fm(I["p"][l, 0]) for l in range(2)], axis=1)
    src = {"q_norm": "ev_q_norm", "kv_norm": "ev_kv_norm", "ln1_g": "ln1_g", "ln1_b": "ln1_b", "ln2_g": "ln2_g",
           "ln2_b": "ln2_b", "ple_b": "ple_b_gate", "norm_mix": "norm_mix_g_2", "b_gate": "b_gate_2",
           "mu_rkv": "mu_rkv_2", "mu_lora": "mu_lora_2", "w0": "decay_w0_2", "a0": "aaa_a0_2", "k_k": "k_k_2",
           "k_a": "k_a_2", "r_k": "r_k_2", "lnx_g": "ln_x_g_2", "lnx_b": "ln_x_b_2", "conv_b": "conv_b_2",
           "cln_g": "conv_ln_g_2", "cln_b": "conv_ln_b_2", "norm_ff": "norm_ff_g_2", "norm_fin": "norm_final_g_2"}
    A["par"] = np.concatenate([I[src[n]].reshape(-1, P).T for n in PAR], axis=1)
    A["ident"] = np.eye(P, dtype=np.float32)
    A["mask"] = np.where(np.arange(P)[None] > np.arange(P)[:, None], NEG, 0).astype(np.float32)
    inv = 1.0 / (10000.0 ** (np.arange(0, 32, 2, dtype=np.float32) / np.float32(32)))
    ang = (np.arange(T, dtype=np.float32)[:, None] * inv[None].astype(np.float32)).T
    c, s_ = np.cos(ang), np.sin(ang)
    A["rope"] = np.concatenate([np.ones((64, T)), c, c, -s_, s_]).astype(np.float32)
    dist = 255 - np.arange(SWA_F)
    ok = (dist >= 0) & (dist < P)
    d = np.maximum(dist, 1).astype(np.float32)
    large = 16 + (np.log(d / 16) / np.float32(np.log(8.0)) * 16).astype(np.int32)
    bucket = np.where(dist < 16, np.maximum(dist, 0), np.minimum(large, 31))
    A["oneh"] = ((np.arange(32)[:, None] == bucket[None]) & ok[None]).astype(np.float32)
    A["negm"] = np.repeat(np.where(ok, 0, NEG)[None], 8, axis=0).astype(np.float32)
    A["relb"] = I["rel_bias"]
    A["sink"] = I["ev_sinks"][0]
    row, u = np.arange(P)[:, None], np.arange(8)[None]
    e, r = 1 - row // 64, row % 64
    A["fsel"] = np.concatenate([r == 32 + 2 * u + e, -1.0 * (r == 2 * u + e), r < 16, (r >= 32) & (r < 48)],
                               axis=1).astype(np.float32)
    A["bf"] = np.tile(I["od_b_f"][0], 8).reshape(P, 1)
    i, j = np.arange(P)[:, None], np.arange(P)[None]
    head = i // 64 == j // 64
    wm = [head & (i < j), head & (i <= j), (i // 2 == j // 2) & (i > j), (i // 2 == j // 2) & (i < j)]
    wm += [(i // (2 * b) == j // (2 * b)) & (i // b < j // b) for b in (2, 4, 8, 16, 32)]
    A["wm"] = np.stack(wm, axis=1).astype(np.float32)
    A["o64"] = (head / 64.0).astype(np.float32)
    A["cw"] = I["conv_w_2"][0].T.reshape(NC, P, 31).transpose(1, 0, 2)
    return {n: np.ascontiguousarray(a) for n, a in A.items()}, third_layer


def kernel(**inputs):
    import concourse.bacc as bacc
    from concourse.bass_utils import run_bass_kernel_spmd

    arrays, third_layer = layout({n: np.asarray(a) for n, a in inputs.items()})
    nc = bacc.Bacc("TRN2", target_bir_lowering=False, num_devices=1)
    A = {n: nc.dram_tensor(n, a.shape, mybir.dt.from_np(a.dtype), kind="ExternalInput").ap() for n, a in arrays.items()}
    A["out"] = nc.dram_tensor("out", (P, NC, T), F32, kind="ExternalOutput").ap()
    build(nc, A, arrays["w"].shape[0], third_layer)
    run = run_bass_kernel_spmd(nc, [arrays], core_ids=[0])
    return run.results[0]["out"].transpose(2, 1, 0).reshape(1, T, D)
```
